# Optimizing a Trainium2 kernel written in Bass

```python
import jax, jax.numpy as jnp
from jax import lax
import numpy as np

D_MODEL = 1024
BATCH = 1
SEQ = 2048
DEPTH = 1
DEC_BATCH = 8
DEC_SEQ = 4
PAST_LEN = 4096
PAGE_SIZE = 128

HEAD_DIM = 64
A_HEADS = 4
A_KV_HEADS = 2
A_WINDOW = 128
B_HEADS = 6
B_PATTERNS = ((128, 1), (512, 4), (2048, 16))
B_WINDOW_MAX = 2048
C_HEADS = 6
DECAY_LORA = 64
AAA_LORA = 64
GATE_LORA = 128
D_FF = 4 * D_MODEL
Q_BLOCK = 128
RMS_EPS = 1e-5
GN_EPS = 64e-5

A_Q = A_HEADS * HEAD_DIM
A_KV = A_KV_HEADS * HEAD_DIM
B_W = B_HEADS * HEAD_DIM
C_W = C_HEADS * HEAD_DIM
C_PROJ = 3 * C_W + DECAY_LORA + AAA_LORA + GATE_LORA
IN_COLS = A_Q + 2 * A_KV + 3 * B_W + C_PROJ
MIX_W = A_Q + B_W + C_W
IN_SPLITS = (A_Q, A_Q + A_KV, A_Q + 2 * A_KV, A_Q + 2 * A_KV + B_W,
             A_Q + 2 * A_KV + 2 * B_W, A_Q + 2 * A_KV + 3 * B_W)
C_SPLITS = (C_W, 2 * C_W, 3 * C_W, 3 * C_W + DECAY_LORA, 3 * C_W + DECAY_LORA + AAA_LORA)

kernel_name = 'hybrid_swa_sink_dilated_rwkv7_step'

def rmsnorm(x, g):
    xf = x.astype(jnp.float32)
    y = xf * lax.rsqrt(jnp.mean(xf * xf, axis=-1, keepdims=True) + RMS_EPS)
    return (y * g.astype(jnp.float32)).astype(x.dtype)

def banded_attn(q, k, v, n_past, window, sink=None):
    N, L, H, hd = q.shape
    G = k.shape[2]
    rep = H // G
    blk = L if L <= Q_BLOCK else Q_BLOCK
    nb = -(-L // blk)
    Lp = nb * blk
    front = window - n_past
    kv_pad = ((0, 0), (front, Lp - L), (0, 0), (0, 0))
    k = jnp.pad(k, kv_pad)
    v = jnp.pad(v, kv_pad)
    q = jnp.pad(q, ((0, 0), (0, Lp - L), (0, 0), (0, 0))).reshape(N, nb, blk, G, rep, hd)
    span = window + blk
    kidx = jnp.arange(nb)[:, None] * blk + jnp.arange(span)[None, :]
    kb = k[:, kidx]
    vb = v[:, kidx]
    s = jnp.einsum('nbqgrd,nbkgd->nbgrqk', q, kb).astype(jnp.float32) * (hd ** -0.5)
    dist = jnp.arange(blk)[:, None] + window - jnp.arange(span)[None, :]
    mask = ((dist >= 0) & (dist <= window))[None] & (kidx >= front)[:, None, :]
    s = jnp.where(mask[None, :, None, None], s, -jnp.inf)
    m = jnp.max(s, axis=-1)
    if sink is not None:
        sk = sink.astype(jnp.float32).reshape(1, 1, G, rep, 1)
        m = jnp.maximum(m, sk)
    p = jnp.exp(s - m[..., None])
    den = jnp.sum(p, axis=-1)
    if sink is not None:
        den = den + jnp.exp(sk - m)
    o = jnp.einsum('nbgrqk,nbkgd->nbqgrd', p.astype(v.dtype), vb).astype(jnp.float32)
    den_q = jnp.transpose(den, (0, 1, 4, 2, 3))
    o = (o / den_q[..., None]).reshape(N, Lp, H, hd)[:, :L]
    lse = (jnp.transpose(m, (0, 1, 4, 2, 3)) + jnp.log(den_q)).reshape(N, Lp, H)[:, :L]
    return o, lse

def merge_patterns(outs, lses):
    wts = jax.nn.softmax(jnp.stack(lses), axis=0)
    return jnp.sum(wts[..., None] * jnp.stack(outs), axis=0)

def dilated_prompt(q, k, v):
    N, S, H, hd = q.shape
    outs, lses = [], []
    for win, d in B_PATTERNS:
        Ls = S // d
        def to_classes(t):
            return t.reshape(N, Ls, d, H, hd).transpose(0, 2, 1, 3, 4).reshape(N * d, Ls, H, hd)
        o, lse = banded_attn(to_classes(q), to_classes(k), to_classes(v), 0, win // d)
        outs.append(o.reshape(N, d, Ls, H, hd).transpose(0, 2, 1, 3, 4).reshape(N, S, H, hd))
        lses.append(lse.reshape(N, d, Ls, H).transpose(0, 2, 1, 3).reshape(N, S, H))
    return merge_patterns(outs, lses)

def dilated_sample(q, k_all, v_all):
    N, L, H, hd = q.shape
    n_past = k_all.shape[1] - L
    outs, lses = [], []
    for win, d in B_PATTERNS:
        steps = jnp.arange(win // d + 1)
        idx = n_past + jnp.arange(L)[:, None] - steps[None, :] * d
        valid = idx >= 0
        idx = jnp.maximum(idx, 0)
        kg = k_all[:, idx]
        vg = v_all[:, idx]
        s = jnp.einsum('nlhd,nlkhd->nlhk', q, kg).astype(jnp.float32) * (hd ** -0.5)
        s = jnp.where(valid[None, :, None, :], s, -jnp.inf)
        m = jnp.max(s, axis=-1)
        p = jnp.exp(s - m[..., None])
        den = jnp.sum(p, axis=-1)
        o = jnp.einsum('nlhk,nlkhd->nlhd', p.astype(vg.dtype), vg).astype(jnp.float32) / den[..., None]
        outs.append(o)
        lses.append(m + jnp.log(den))
    return merge_patterns(outs, lses)

def wkv_scan(s0, r, w, k, v, kk, a):
    def step(S, inp):
        r_t, w_t, k_t, v_t, kk_t, a_t = inp
        sa = jnp.einsum('nhij,nhj->nhi', S, -kk_t)
        S = S * w_t[:, :, None, :] + sa[..., None] * (kk_t * a_t)[:, :, None, :] + v_t[..., None] * k_t[:, :, None, :]
        return S, jnp.einsum('nhij,nhj->nhi', S, r_t)
    xs = tuple(jnp.swapaxes(t, 0, 1) for t in (r, w, k, v, kk, a))
    s_fin, y = lax.scan(step, s0, xs)
    return jnp.swapaxes(y, 0, 1), s_fin

def rwkv_mixer(zc, z_before, s0, w):
    N, L, _ = zc.shape
    f32 = jnp.float32
    z_prev = jnp.concatenate([z_before[:, None, :].astype(zc.dtype), zc[:, :-1]], axis=1)
    zs = (zc + (z_prev - zc) * w['c_mu'].astype(zc.dtype)).astype(f32)
    r, k, v, zw, za, zg = jnp.split(zs, C_SPLITS, axis=-1)
    w_log = -jax.nn.softplus(-(w['c_w0'].astype(f32) + jnp.tanh(zw) @ w['c_w2'].astype(f32))) - 0.5
    decay = jnp.exp(-jnp.exp(w_log))
    a = jax.nn.sigmoid(w['c_a0'].astype(f32) + za @ w['c_a2'].astype(f32))
    g = jax.nn.sigmoid(zg) @ w['c_g2'].astype(f32)
    heads = lambda t: t.reshape(N, L, C_HEADS, HEAD_DIM)
    kk = heads(k * w['c_k_k'].astype(f32))
    kk = kk / jnp.maximum(jnp.sqrt(jnp.sum(kk * kk, axis=-1, keepdims=True)), 1e-12)
    k = k * (1.0 + (a - 1.0) * w['c_k_a'].astype(f32))
    rh, kh, vh, ah, dh = heads(r), heads(k), heads(v), heads(a), heads(decay)
    y, s_fin = wkv_scan(s0.astype(f32), rh, dh, kh, vh, kk, ah)
    mu = jnp.mean(y, axis=-1, keepdims=True)
    var = jnp.mean(jnp.square(y - mu), axis=-1, keepdims=True)
    ln_w = w['c_ln_w'].astype(f32).reshape(C_HEADS, HEAD_DIM)
    ln_b = w['c_ln_b'].astype(f32).reshape(C_HEADS, HEAD_DIM)
    y = (y - mu) * lax.rsqrt(var + GN_EPS) * ln_w + ln_b
    y = y + jnp.sum(rh * kh * w['c_r_k'].astype(f32), axis=-1, keepdims=True) * vh
    return y.reshape(N, L, C_W) * g, s_fin

def trunk_layer(x, w, past):
    N, L, _ = x.shape
    h = rmsnorm(x, w['norm1_g'])
    proj = jnp.einsum('nld,dc->nlc', h, w['w_in'])
    qa, ka, va, qb, kb, vb, zc = jnp.split(proj, IN_SPLITS, axis=-1)
    qa = qa.reshape(N, L, A_HEADS, HEAD_DIM)
    ka = ka.reshape(N, L, A_KV_HEADS, HEAD_DIM)
    va = va.reshape(N, L, A_KV_HEADS, HEAD_DIM)
    qb = qb.reshape(N, L, B_HEADS, HEAD_DIM)
    kb = kb.reshape(N, L, B_HEADS, HEAD_DIM)
    vb = vb.reshape(N, L, B_HEADS, HEAD_DIM)
    if past is None:
        oa, _ = banded_attn(qa, ka, va, 0, A_WINDOW, w['a_sink'])
        ob = dilated_prompt(qb, kb, vb)
        z_before = jnp.zeros((N, C_PROJ), zc.dtype)
        s0 = jnp.zeros((N, C_HEADS, HEAD_DIM, HEAD_DIM), jnp.float32)
    else:
        ca_k, ca_v, cb_k, cb_v, s0, z_before = past
        ka_all = jnp.concatenate([ca_k.astype(ka.dtype), ka], axis=1)
        va_all = jnp.concatenate([ca_v.astype(va.dtype), va], axis=1)
        oa, _ = banded_attn(qa, ka_all, va_all, ca_k.shape[1], A_WINDOW, w['a_sink'])
        kb_all = jnp.concatenate([cb_k.astype(kb.dtype), kb], axis=1)
        vb_all = jnp.concatenate([cb_v.astype(vb.dtype), vb], axis=1)
        ob = dilated_sample(qb, kb_all, vb_all)
    oc, s_fin = rwkv_mixer(zc, z_before, s0, w)
    mix = jnp.concatenate([oa.reshape(N, L, A_Q), ob.reshape(N, L, B_W), oc], axis=-1).astype(x.dtype)
    x = x + jnp.einsum('nlc,cd->nld', mix, w['w_out'])
    u = jnp.einsum('nld,df->nlf', rmsnorm(x, w['norm2_g']), w['mlp_up'])
    x = x + jnp.einsum('nlf,fd->nld', jnp.square(jax.nn.relu(u)), w['mlp_down'])
    if past is None:
        ra = min(A_WINDOW, L)
        rb = min(B_WINDOW_MAX, L)
        new = (ka[:, L - ra:], va[:, L - ra:], kb[:, L - rb:], vb[:, L - rb:], s_fin, zc[:, -1])
    else:
        new = (ka, va, kb, vb, s_fin, zc[:, -1])
    return x, new

def setup_inputs(seed: int = 0) -> dict:
    key = jax.random.key(seed)
    ks = jax.random.split(key, 32)
    f32 = jnp.float32
    nrm = lambda kk, shape, scale: jax.random.normal(kk, shape, f32) * scale
    pa = min(A_WINDOW, PAST_LEN)
    pb = min(B_WINDOW_MAX, PAST_LEN)
    return {
        'x_prompt': nrm(ks[0], (BATCH, SEQ, D_MODEL), 1.0),
        'x_sample': nrm(ks[1], (DEC_BATCH, DEC_SEQ, D_MODEL), 1.0),
        'cache_a_k': nrm(ks[2], (DEPTH, DEC_BATCH, pa, A_KV_HEADS, HEAD_DIM), 1.0),
        'cache_a_v': nrm(ks[3], (DEPTH, DEC_BATCH, pa, A_KV_HEADS, HEAD_DIM), 1.0),
        'cache_b_k': nrm(ks[4], (DEPTH, DEC_BATCH, pb, B_HEADS, HEAD_DIM), 1.0),
        'cache_b_v': nrm(ks[5], (DEPTH, DEC_BATCH, pb, B_HEADS, HEAD_DIM), 1.0),
        'state_c_wkv': nrm(ks[6], (DEPTH, DEC_BATCH, C_HEADS, HEAD_DIM, HEAD_DIM), 0.3),
        'state_c_shift': nrm(ks[7], (DEPTH, DEC_BATCH, C_PROJ), 1.0),
        'norm1_g': 1.0 + nrm(ks[8], (DEPTH, D_MODEL), 0.02),
        'norm2_g': 1.0 + nrm(ks[9], (DEPTH, D_MODEL), 0.02),
        'w_in': nrm(ks[10], (DEPTH, D_MODEL, IN_COLS), D_MODEL ** -0.5),
        'w_out': nrm(ks[11], (DEPTH, MIX_W, D_MODEL), MIX_W ** -0.5),
        'a_sink': nrm(ks[12], (DEPTH, A_HEADS), 0.5),
        'c_mu': jax.random.uniform(ks[13], (DEPTH, C_PROJ), f32),
        'c_w0': jax.random.uniform(ks[14], (DEPTH, C_W), f32, -4.0, 1.0),
        'c_w2': nrm(ks[15], (DEPTH, DECAY_LORA, C_W), 0.5 * DECAY_LORA ** -0.5),
        'c_a0': nrm(ks[16], (DEPTH, C_W), 0.5),
        'c_a2': nrm(ks[17], (DEPTH, AAA_LORA, C_W), 0.5 * AAA_LORA ** -0.5),
        'c_g2': nrm(ks[18], (DEPTH, GATE_LORA, C_W), GATE_LORA ** -0.5),
        'c_k_k': 0.85 + nrm(ks[19], (DEPTH, C_W), 0.05),
        'c_k_a': 1.0 + nrm(ks[20], (DEPTH, C_W), 0.05),
        'c_r_k': nrm(ks[21], (DEPTH, C_HEADS, HEAD_DIM), 0.1),
        'c_ln_w': 1.0 + nrm(ks[22], (DEPTH, C_W), 0.02),
        'c_ln_b': nrm(ks[23], (DEPTH, C_W), 0.02),
        'mlp_up': nrm(ks[24], (DEPTH, D_MODEL, D_FF), D_MODEL ** -0.5),
        'mlp_down': nrm(ks[25], (DEPTH, D_FF, D_MODEL), D_FF ** -0.5),
        'final_norm_g': 1.0 + nrm(ks[26], (D_MODEL,), 0.02),
    }

def reference(x_prompt, x_sample, cache_a_k, cache_a_v, cache_b_k, cache_b_v, state_c_wkv, state_c_shift,
              norm1_g, norm2_g, w_in, w_out, a_sink, c_mu, c_w0, c_w2, c_a0, c_a2, c_g2, c_k_k, c_k_a, c_r_k,
              c_ln_w, c_ln_b, mlp_up, mlp_down, final_norm_g):
    stacked = {'norm1_g': norm1_g, 'norm2_g': norm2_g, 'w_in': w_in, 'w_out': w_out, 'a_sink': a_sink,
               'c_mu': c_mu, 'c_w0': c_w0, 'c_w2': c_w2, 'c_a0': c_a0, 'c_a2': c_a2, 'c_g2': c_g2,
               'c_k_k': c_k_k, 'c_k_a': c_k_a, 'c_r_k': c_r_k, 'c_ln_w': c_ln_w, 'c_ln_b': c_ln_b,
               'mlp_up': mlp_up, 'mlp_down': mlp_down}
    yp, ys = x_prompt, x_sample
    p_new, s_new = [], []
    for l in range(DEPTH):
        w = {name: arr[l] for name, arr in stacked.items()}
        yp, st_p = trunk_layer(yp, w, None)
        ys, st_s = trunk_layer(ys, w, (cache_a_k[l], cache_a_v[l], cache_b_k[l], cache_b_v[l],
                                       state_c_wkv[l], state_c_shift[l]))
        p_new.append(st_p)
        s_new.append(st_s)
    p_a_k, p_a_v, p_b_k, p_b_v, p_c_wkv, p_c_shift = [jnp.stack(t) for t in zip(*p_new)]
    s_a_k, s_a_v, s_b_k, s_b_v, s_c_wkv, s_c_shift = [jnp.stack(t) for t in zip(*s_new)]
    y_prompt = rmsnorm(yp, final_norm_g)
    y_sample = rmsnorm(ys, final_norm_g)
    return (y_prompt, y_sample, p_a_k, p_a_v, p_b_k, p_b_v, p_c_wkv, p_c_shift,
            s_a_k, s_a_v, s_b_k, s_b_v, s_c_wkv, s_c_shift)


_drawn_inputs = setup_inputs


def setup_inputs(seed=0):
    import zlib

    import numpy as np

    out = dict(_drawn_inputs(seed))
    spreads = {}
    factors = {'norm2_g': 9.163,
     'a_sink': 158.173,
     'c_ln_w': 21.747,
     'c_ln_b': 21.556,
     'final_norm_g': 21.521,
     'cache_a_k': 2.698,
     'cache_b_k': 2.861,
     'c_r_k': 5.29}
    for name, (base, spread) in spreads.items():
        noise = np.random.default_rng([zlib.crc32(name.encode()), seed]).standard_normal(out[name].shape)
        drawn = base * np.exp(spread * noise) if base else spread * noise
        out[name] = __import__('jax').numpy.asarray(drawn.astype(out[name].dtype))
    for name, factor in factors.items():
        out[name] = (out[name] * factor).astype(out[name].dtype)
    return out
```

```python
from contextlib import ExitStack

import numpy as np
import concourse.bass as bass
from concourse import mybir

F32 = mybir.dt.float32
F32R = mybir.dt.float32r
ACT = mybir.ActivationFunctionType
ALU = mybir.AluOpType
AX = mybir.AxisListType

P = 128
D = 1024
KC = D // P
SEQ, NB, NQ = 2048, 8, 4
NS = NB * NQ
T = SEQ + NS
TG = 416
NG = T // TG
HD = 64
FMB = 20
ZC0 = 9
NV = 512
EPS = 1e-5


class Scope:

    def __init__(self, nc, ctx, outer):
        self.nc, self.ctx, self.outer = nc, ctx, outer

    def sb(self, name, shape, dt=F32):
        return self.ctx.enter_context(self.nc.sbuf_tensor(name, shape, dt))

    def ps(self, name, shape):
        return self.ctx.enter_context(self.nc.psum_tensor(name, shape, F32))

    def sem(self, name):
        return self.outer.enter_context(self.nc.semaphore(name))


def project(nc, outer, xT, g1, ones, w_fm, w_v, projT, vtok):
    with ExitStack() as ctx:
        s = Scope(nc, ctx, outer)
        x = s.sb("p1_x", [P, KC, T])
        sq = s.sb("p1_sq", [P, KC, TG])
        rs = s.sb("p1_rs", [P, TG])
        g = s.sb("p1_g", [P, KC])
        on = s.sb("p1_ones", [P, P])
        eps = s.sb("p1_eps", [P, 1])
        w = [s.sb(f"p1_w{i}", [P, KC, P]) for i in range(2)]
        wv = s.sb("p1_wv", [P, KC, NV])
        ob = [s.sb(f"p1_ob{i}", [P, T]) for i in range(2)]
        vo = [s.sb(f"p1_vo{i}", [P, NV]) for i in range(2)]
        bank = [s.ps(f"p1_bank{i}", [P, 512]) for i in range(NG)]
        sbank = s.ps("p1_sum", [P, 512])
        vbank = [s.ps(f"p1_vbank{i}", [P, NV]) for i in range(2)]
        x_in = [s.sem(f"p1_x_in{i}") for i in range(NG)]
        consts_in = s.sem("p1_consts_in")
        eps_set = s.sem("p1_eps_set")
        wv_in = s.sem("p1_wv_in")
        w_in = [s.sem(f"p1_w_in{i}") for i in range(2)]
        squared = s.sem("p1_squared")
        summed = s.sem("p1_summed")
        rooted = s.sem("p1_rooted")
        inverted = s.sem("p1_inverted")
        h_ready = s.sem("p1_h_ready")
        block_done = s.sem("p1_block_done")
        evac = s.sem("p1_evac")
        stored = [s.sem(f"p1_stored{i}") for i in range(2)]
        v_done = s.sem("p1_v_done")
        v_evac = s.sem("p1_v_evac")
        v_stored = [s.sem(f"p1_v_stored{i}") for i in range(2)]
        NT = SEQ // P + 1
        tiles = [(P * i, P) for i in range(SEQ // P)] + [(SEQ, NS)]
        block = ctx.enter_context(nc.Block())

        @block.sync
        def _(sp):
            for gi in range(NG):
                sp.dma_start(x[:, :, gi * TG:(gi + 1) * TG], xT[:, :, gi * TG:(gi + 1) * TG]).then_inc(x_in[gi], 16)
                if gi == 0:
                    sp.dma_start(on[:, :], ones).then_inc(consts_in, 16)
                    sp.dma_start(g[:, :], g1).then_inc(consts_in, 16)
            for j in range(2):
                sp.dma_start(w[j][:, :, :], w_fm[j]).then_inc(w_in[j], 16)
            sp.dma_start(wv[:, :, :], w_v).then_inc(wv_in, 16)
            for j in range(2):
                sp.sem_inc(stored[j], 16)
            with sp.Fori(0, FMB // 2 - 1) as i:
                for j in range(2):
                    sp.wait_ge(block_done, (2 * i + j + 1) * NG)
                    sp.dma_start(w[j][:, :, :], w_fm[2 * i + j + 2]).then_inc(w_in[j], 16)
                    sp.wait_ge(evac, (2 * i + j + 2) * NG)
                    sp.dma_start(projT[2 * i + j], ob[j][:, :]).then_inc(stored[j], 16)
            for j in range(2):
                sp.wait_ge(evac, (FMB + j) * NG)
                sp.dma_start(projT[FMB - 2 + j], ob[j][:, :]).then_inc(stored[j], 16)
            for t, (r0, n) in enumerate(tiles):
                sp.wait_ge(v_evac, t + 1)
                sp.dma_start(vtok[r0:r0 + n, :], vo[t % 2][0:n, :]).then_inc(v_stored[t % 2], 16)
            for j in range(2):
                sp.wait_ge(stored[j], 16 * (FMB // 2 + 1))
                sp.wait_ge(v_stored[j], 16 * ((NT + 1 - j) // 2))

        @block.tensor
        def _(pe):
            pe.wait_ge(consts_in, 32)
            for gi in range(NG):
                pe.wait_ge(squared, gi + 1)
                if gi:
                    pe.wait_ge(rooted, gi)
                for k in range(KC):
                    mm = pe.matmul(sbank[:, 0:TG], on[:, :], sq[:, k, :], start=(k == 0), stop=(k == KC - 1))
                mm.then_inc(summed, 1)
            pe.wait_ge(h_ready, NG)
            with pe.Fori(0, FMB // 2) as i:
                for j in range(2):
                    pe.wait_ge(w_in[j], (i + 1) * 16)
                    for gi in range(NG):
                        pe.wait_ge(evac, (2 * i + j) * NG + gi + 1)
                        for k in range(KC):
                            mm = pe.matmul(bank[gi][:, 0:TG], w[j][:, k, :], x[:, k, gi * TG:(gi + 1) * TG],
                                           start=(k == 0), stop=(k == KC - 1))
                        mm.then_inc(block_done, 1)
            pe.wait_ge(wv_in, 16)
            for t, (r0, n) in enumerate(tiles):
                if t >= 2:
                    pe.wait_ge(v_evac, t - 1)
                for k in range(KC):
                    mm = pe.matmul(vbank[t % 2][0:n, :], x[:, k, r0:r0 + n], wv[:, k, :],
                                   start=(k == 0), stop=(k == KC - 1))
                mm.then_inc(v_done, 1)

        @block.scalar
        def _(act):
            act.wait_ge(eps_set, 1)
            for gi in range(NG):
                act.wait_ge(x_in[gi], 16)
                if gi:
                    act.wait_ge(summed, gi)
                act.activation(sq[:, :, :], x[:, :, gi * TG:(gi + 1) * TG], ACT.Square).then_inc(squared, 1)
                act.wait_ge(summed, gi + 1)
                if gi:
                    act.wait_ge(h_ready, gi)
                act.activation(rs[:, :], sbank[:, 0:TG], ACT.Sqrt, bias=eps[:, 0:1], scale=1.0 / D).then_inc(rooted, 1)
            act.sem_inc(evac, NG)
            with act.Fori(0, FMB // 2) as i:
                for j in range(2):
                    act.wait_ge(stored[j], i * 16 + 16)
                    for gi in range(NG):
                        act.wait_ge(block_done, (2 * i + j) * NG + gi + 1)
                        act.activation(ob[j][:, gi * TG:(gi + 1) * TG], bank[gi][:, 0:TG], ACT.Copy).then_inc(evac, 1)

        @block.vector
        def _(dve):
            dve.memset(eps[:, :], EPS).then_inc(eps_set, 1)
            dve.wait_ge(consts_in, 32)
            for gi in range(NG):
                dve.wait_ge(rooted, gi + 1)
                dve.reciprocal(rs[:, :], rs[:, :]).then_inc(inverted, 1)
                dve.wait_ge(inverted, gi + 1)
                for k in range(KC):
                    xs = x[:, k, gi * TG:(gi + 1) * TG]
                    mul = dve.scalar_tensor_tensor(out=xs, in0=xs, scalar=g[:, k:k + 1], in1=rs[:, :],
                                                   op0=ALU.mult, op1=ALU.mult)
                mul.then_inc(h_ready, 1)
            for t, (r0, n) in enumerate(tiles):
                dve.wait_ge(v_done, t + 1)
                if t >= 2:
                    dve.wait_ge(v_stored[t % 2], 16 * (t // 2))
                dve.tensor_copy(vo[t % 2][0:n, :], vbank[t % 2][0:n, :]).then_inc(v_evac, 1)


TQ = SEQ // P
SCALE = HD ** -0.5
A_PAIRS, B_PAIRS = 2, 3
PAIRS = A_PAIRS + B_PAIRS
QB = [0, 1, 3, 4, 5]
KB = [2, 2, 6, 7, 8]
LAG = 2


def prompt_attention(nc, outer, projT, vtok, strip_a, strip_b, sinks, ident, mixT):
    jobs = [(u, t, h) for u in range(PAIRS) for t in range(TQ) for h in range(2)]
    first_block = lambda u, t: max(0, t - 1) if u < A_PAIRS else 0
    groups, done_groups = [], []
    for u, t, h in jobs:
        b0 = first_block(u, t)
        groups.append([(b, min(4, t + 1 - b)) for b in range(b0, t + 1, 4)])
        done_groups.append((done_groups[-1] if done_groups else 0) + len(groups[-1]))
    before = lambda n: done_groups[n] - len(groups[n])
    with ExitStack() as ctx:
        s = Scope(nc, ctx, outer)
        q = [s.sb(f"p2_q{i}", [P, 2, SEQ]) for i in range(2)]
        k = [s.sb(f"p2_k{i}", [P, SEQ]) for i in range(2)]
        v = [s.sb(f"p2_v{i}", [P, TQ, P]) for i in range(2)]
        mo = [s.sb(f"p2_mo{i}", [P, SEQ]) for i in range(2)]
        sa = s.sb("p2_strip_a", [P, 2 * P])
        sbm = s.sb("p2_strip_b", [P, SEQ])
        idt = s.sb("p2_ident", [P, P])
        sink = s.sb("p2_sink", [P, 4])
        sink8 = s.sb("p2_sink8", [P, 4])
        row = [s.sb(f"p2_row{i}", [P, SEQ]) for i in range(3)]
        pt = s.sb("p2_pt", [P, 4, 4, P])
        mx = s.sb("p2_mx", [P, 2, 4])
        mr = s.sb("p2_mr", [P, 2])
        nb = s.sb("p2_nb", [P, 4])
        den = s.sb("p2_den", [P, 4])
        sex = s.sb("p2_sex", [P, 4])
        rec = s.sb("p2_rec", [P, 4])
        on = s.sb("p2_on", [P, 2, P])
        sbank = [s.ps(f"p2_s{i}", [P, 512]) for i in range(3)]
        tbank = [s.ps(f"p2_t{i}", [P, 4, P]) for i in range(2)]
        obank = [s.ps(f"p2_o{i}", [P, P]) for i in range(2)]
        xbank = s.ps("p2_x", [P, P])
        consts_in = s.sem("p2_consts_in")
        q_zeroed = s.sem("p2_q_zeroed")
        pair_in = [s.sem(f"p2_pair_in{i}") for i in range(2)]
        scored = s.sem("p2_scored")
        masked = s.sem("p2_masked")
        reduced = s.sem("p2_reduced")
        biased = s.sem("p2_biased")
        sink_set = s.sem("p2_sink_set")
        expd = s.sem("p2_expd")
        turned = s.sem("p2_turned")
        t_copied = s.sem("p2_t_copied")
        used = s.sem("p2_used")
        summed_a = s.sem("p2_summed_a")
        inverted = s.sem("p2_inverted")
        normed = s.sem("p2_normed")
        o_turned = s.sem("p2_o_turned")
        o_copied = s.sem("p2_o_copied")
        m_stored = [s.sem(f"p2_m_stored{i}") for i in range(2)]
        slots = []
        for n in range(len(jobs) + LAG):
            sizes = [len(groups[m]) for m in (n, n - LAG) if 0 <= m < len(jobs)]
            slots += [(n, i) for i in range(max(sizes))]
        block = ctx.enter_context(nc.Block())
        hp = lambda h: slice(HD * h, HD * (h + 1))

        @block.sync
        def _(sp):
            def load(u):
                if u >= 2:
                    sp.wait_ge(used, done_groups[2 * TQ * (u - 1) - 1])
                sem = pair_in[u % 2]
                for h in range(2):
                    sp.dma_start(q[u % 2][hp(h), h, :], projT[QB[u], hp(h), 0:SEQ]).then_inc(sem, 16)
                if u < A_PAIRS:
                    for h in range(2):
                        sp.dma_start(k[u % 2][hp(h), :], projT[KB[u], hp(u), 0:SEQ]).then_inc(sem, 16)
                    for h in range(2):
                        sp.dma_start(v[u % 2][:, :, hp(h)],
                                     vtok[0:SEQ, hp(u)].rearrange("(t p) c -> p t c", p=P)).then_inc(sem, 16)
                else:
                    sp.dma_start(k[u % 2][:, :], projT[KB[u], :, 0:SEQ]).then_inc(sem, 16)
                    c = P * (u - A_PAIRS + 1)
                    sp.dma_start(v[u % 2][:, :, :],
                                 vtok[0:SEQ, c:c + P].rearrange("(t p) c -> p t c", p=P)).then_inc(sem, 16)

            sp.wait_ge(q_zeroed, 4)
            load(0)
            sp.dma_start(sa[:, :], strip_a).then_inc(consts_in, 16)
            sp.dma_start(sbm[:, :], strip_b).then_inc(consts_in, 16)
            sp.dma_start(idt[:, :], ident).then_inc(consts_in, 16)
            sp.dma_start(sink[:, :], sinks).then_inc(consts_in, 16)
            load(1)
            for u in range(PAIRS):
                if u + 2 < PAIRS:
                    load(u + 2)
                sp.wait_ge(o_copied, TQ * (u + 1))
                sp.dma_start(mixT[u, :, 0:SEQ], mo[u % 2][:, :]).then_inc(m_stored[u % 2], 16)
            sp.wait_ge(m_stored[0], 16 * 3)
            sp.wait_ge(m_stored[1], 16 * 2)

        n_dma = [6 if u < A_PAIRS else 4 for u in range(PAIRS)]
        pair_value = [16 * sum(n_dma[w] for w in range(u % 2, u + 1, 2)) for u in range(PAIRS)]
        @block.tensor
        def _(pe):
            pe.wait_ge(consts_in, 64)

            def score(n, i):
                u, t, h = jobs[n]
                b, nb_ = groups[n][i]
                c = before(n) + i
                if c >= 3:
                    pe.wait_ge(masked, c - 2)
                pe.matmul(sbank[c % 3][:, 0:nb_ * P], q[u % 2][:, h, t * P:(t + 1) * P],
                          k[u % 2][:, b * P:(b + nb_) * P], start=True, stop=True).then_inc(scored, 1)

            def turn(n, i):
                b, nb_ = groups[n][i]
                at = before(n) + i
                if i == 0:
                    pe.wait_ge(expd, n + 1)
                if at >= 2:
                    pe.wait_ge(t_copied, at - 1)
                c0 = (b - groups[n][0][0]) * P
                for j in range(nb_):
                    tr = pe.transpose(tbank[at % 2][:, j, :], row[n % 3][:, c0 + j * P:c0 + (j + 1) * P], idt[:, :])
                tr.then_inc(turned, 1)

            def times_v(n, i):
                u, t, h = jobs[n]
                b, nb_ = groups[n][i]
                c = before(n) + i
                if i == 0 and n >= 2:
                    pe.wait_ge(normed, n - 1)
                pe.wait_ge(t_copied, c + 1)
                for j in range(nb_):
                    mm = pe.matmul(obank[n % 2][:, :], pt[:, c % 4, j, :], v[u % 2][:, b + j, :],
                                   start=(i == 0 and j == 0), stop=(b + j == t))
                mm.then_inc(used, 1)

            def turn_out(m):
                pe.wait_ge(normed, 2 * m + 2)
                if m:
                    pe.wait_ge(o_copied, m)
                pe.transpose(xbank[:, :], on[:, m % 2, :], idt[:, :]).then_inc(o_turned, 1)

            pending = None
            for n, i in slots:
                if i == 0 and n < len(jobs) and jobs[n][1:] == (0, 0):
                    u = jobs[n][0]
                    pe.wait_ge(pair_in[u % 2], pair_value[u])
                if n < len(jobs) and i < len(groups[n]):
                    score(n, i)
                if 0 <= n - LAG < len(jobs) and i < len(groups[n - LAG]):
                    turn(n - LAG, i)
                    if pending:
                        times_v(*pending)
                    pending = (n - LAG, i)
                if i == 0 and n - LAG >= 2 and (n - LAG) % 2 == 0:
                    turn_out((n - LAG) // 2 - 1)
            times_v(*pending)
            turn_out(len(jobs) // 2 - 1)

        @block.scalar
        def _(act):
            act.wait_ge(consts_in, 64)
            for n, (u, t, h) in enumerate(jobs):
                act.wait_ge(biased, n + 1)
                if n >= 4:
                    act.wait_ge(normed, n - 3)
                w = (t + 1 - groups[n][0][0]) * P
                ex = act.activation(row[n % 3][:, 0:w], row[n % 3][:, 0:w], ACT.Exp, bias=nb[:, n % 4:n % 4 + 1],
                                    scale=SCALE, accum_out=den[:, n % 4:n % 4 + 1])
                ex.then_inc(expd, 1)
                if u < A_PAIRS:
                    act.activation(sex[:, n % 4:n % 4 + 1], sink[:, 2 * u + h:2 * u + h + 1], ACT.Exp,
                                   bias=nb[:, n % 4:n % 4 + 1]).then_inc(sink_set, 1)

        @block.gpsimd
        def _(pool):
            for i in range(2):
                for h in range(2):
                    pool.memset(q[i][hp(1 - h), h, :], 0.0).then_inc(q_zeroed, 1)

        @block.vector
        def _(dve):
            dve.wait_ge(consts_in, 64)
            dve.tensor_scalar(sink8[:, :], sink[:, :], 1.0 / SCALE, None, ALU.mult).then_inc(reduced, 1)

            def mask(n, i):
                u, t, h = jobs[n]
                b0 = groups[n][0][0]
                strip = sa if u < A_PAIRS else sbm
                off = (1 if u < A_PAIRS else TQ - 1) - t
                if i == 0 and n >= 3:
                    dve.wait_ge(turned, done_groups[n - 3])
                b, nb_ = groups[n][i]
                c = before(n) + i
                dve.wait_ge(scored, c + 1)
                dve.tensor_tensor_reduce(row[n % 3][:, (b - b0) * P:(b - b0 + nb_) * P], sbank[c % 3][:, 0:nb_ * P],
                                         strip[:, (b + off) * P:(b + off + nb_) * P], 1.0, -3.0e38, ALU.add, ALU.max,
                                         mx[:, n % 2, i:i + 1]).then_inc(masked, 1)

            def bias(n):
                u, t, h = jobs[n]
                dve.wait_ge(masked, done_groups[n])
                dve.tensor_reduce(mr[:, n % 2:n % 2 + 1], mx[:, n % 2, 0:len(groups[n])], AX.X, ALU.max).then_inc(reduced, 1)
                dve.wait_ge(reduced, n + 2)
                if n >= 4:
                    dve.wait_ge(expd, n - 3)
                    if jobs[n - 4][0] < A_PAIRS:
                        dve.wait_ge(sink_set, n - 3)
                if u < A_PAIRS:
                    dve.tensor_scalar(nb[:, n % 4:n % 4 + 1], mr[:, n % 2:n % 2 + 1], sink8[:, 2 * u + h:2 * u + h + 1],
                                      -SCALE, ALU.max, ALU.mult).then_inc(biased, 1)
                else:
                    dve.tensor_scalar(nb[:, n % 4:n % 4 + 1], mr[:, n % 2:n % 2 + 1], -SCALE, None,
                                      ALU.mult).then_inc(biased, 1)

            def copy_group(n, i):
                b, nb_ = groups[n][i]
                c = before(n) + i
                dve.wait_ge(turned, c + 1)
                if c >= 4:
                    dve.wait_ge(used, c - 3)
                dve.tensor_copy(pt[:, c % 4, 0:nb_, :], tbank[c % 2][:, 0:nb_, :]).then_inc(t_copied, 1)

            def normalise(n):
                u, t, h = jobs[n]
                a = n % 4
                if u < A_PAIRS:
                    dve.wait_ge(sink_set, n + 1)
                    dve.wait_ge(expd, n + 1)
                    dve.tensor_tensor(den[:, a:a + 1], den[:, a:a + 1], sex[:, a:a + 1], ALU.add).then_inc(summed_a, 1)
                    dve.wait_ge(summed_a, n + 1)
                dve.reciprocal(rec[:, a:a + 1], den[:, a:a + 1]).then_inc(inverted, 1)
                dve.wait_ge(inverted, n + 1)
                dve.wait_ge(used, done_groups[n])
                m = n // 2
                if m >= 2:
                    dve.wait_ge(o_turned, m - 1)
                dve.tensor_scalar(on[:, m % 2, hp(h)], obank[n % 2][:, hp(h)], rec[:, a:a + 1], None, ALU.mult).then_inc(normed, 1)

            def copy_out(m):
                u, t, _ = jobs[2 * m]
                dve.wait_ge(o_turned, m + 1)
                if t == 0 and u >= 2:
                    dve.wait_ge(m_stored[u % 2], 16 * (u // 2))
                dve.tensor_copy(mo[u % 2][:, t * P:(t + 1) * P], xbank[:, :]).then_inc(o_copied, 1)

            for n, i in slots:
                if n < len(jobs) and i < len(groups[n]):
                    mask(n, i)
                    if i == len(groups[n]) - 1:
                        bias(n)
                if 0 <= n - LAG < len(jobs) and i < len(groups[n - LAG]):
                    copy_group(n - LAG, i)
                if i == 0 and 0 <= n - LAG - 1:
                    normalise(n - LAG - 1)
                if i == 0 and n - LAG >= 2 and (n - LAG) % 2 == 0:
                    copy_out((n - LAG) // 2 - 1)
            normalise(len(jobs) - 1)
            copy_out(len(jobs) // 2 - 1)


def strips():
    def strip(blocks, offset):
        dist = np.arange(P)[:, None] + (blocks - 1) * P - np.arange(blocks * P)[None, :]
        return offset(dist)
    return strip(2, offset_a).astype(np.float32), strip(TQ, offset_b).astype(np.float32)


def offset_a(dist):
    return np.where((dist >= 0) & (dist <= 128), 0.0, -1e30)


def offset_b(dist):
    count = sum(((dist >= 0) & (dist <= win) & (dist % d == 0)).astype(np.float64)
                for win, d in ((128, 1), (512, 4), (2048, 16)))
    return np.where(count > 0, np.log(np.maximum(count, 1)) / SCALE, -1e30)




NKC = 896
NKB = NKC + NQ
NTB = NKC // P
A_WIN = 128
NKA = A_WIN + NQ + 1


def sample_attention(nc, outer, projT, vtok, kbT, vb, kaT, va, mask_b, mask_a, sink_a, ident, mixT):
    RB, RA = 6 * NQ, 4 * NQ
    with ExitStack() as ctx:
        s = Scope(nc, ctx, outer)
        qb = s.sb("p3_qb", [P, B_PAIRS, NS])
        kn = s.sb("p3_kn", [P, B_PAIRS, NS])
        qa = s.sb("p3_qa", [P, 2, NS])
        kna = s.sb("p3_kna", [P, NS])
        vn = s.sb("p3_vn", [NQ, NB, NV])
        qz = s.sb("p3_qz", [P, NB, B_PAIRS, RB])
        qza = s.sb("p3_qza", [P, NB, RA])
        kc = [s.sb(f"p3_kc{i}", [P, B_PAIRS, NKC]) for i in range(2)]
        vc = [s.sb(f"p3_vc{i}", [P, NTB, 384]) for i in range(2)]
        kca = s.sb("p3_kca", [P, NB, A_WIN])
        vca = s.sb("p3_vca", [P, NB, P])
        mb = s.sb("p3_mb", [RB, NKB])
        ma = s.sb("p3_ma", [RA, NB, NKA - 1])
        ska = s.sb("p3_ska", [RA, NB, 1])
        idt = s.sb("p3_ident", [P, P])
        rw = [s.sb(f"p3_row{i}", [RB, NKB]) for i in range(2)]
        pr = [s.sb(f"p3_prob{i}", [RB, NKB]) for i in range(2)]
        mx = s.sb("p3_mx", [RB, NB, 4])
        st = s.sb("p3_st", [RB, NB, 4])
        pt = [s.sb(f"p3_pt{i}", [P, NTB + 1, RB]) for i in range(2)]
        ra = s.sb("p3_ra", [RA, NB, NKA])
        sta = s.sb("p3_sta", [RA, 3, NB])
        pta = s.sb("p3_pta", [P, NB, RA])
        ptn = s.sb("p3_ptn", [NQ, NB, RA])
        mo = s.sb("p3_mo", [P, PAIRS, NS])
        sbank = [s.ps(f"p3_s{i}", [P, 512]) for i in range(4)]
        tbank = s.ps("p3_t", [P, NTB + 1, RB])
        obank = s.ps("p3_o", [P, B_PAIRS, 8])
        tabank = s.ps("p3_ta", [P, 2, NB, RA])
        oabank = s.ps("p3_oa", [P, NB, RA])
        c_in = s.sem("p3_c_in")
        cache_in = [s.sem(f"p3_cache_in{i}") for i in range(2)]
        zeroed = s.sem("p3_zeroed")
        q_set = s.sem("p3_q_set")
        scored = s.sem("p3_scored")
        masked = s.sem("p3_masked")
        reduced = s.sem("p3_reduced")
        biased = s.sem("p3_biased")
        expd = s.sem("p3_expd")
        inverted = s.sem("p3_inverted")
        normed = s.sem("p3_normed")
        turned = s.sem("p3_turned")
        t_copied = s.sem("p3_t_copied")
        summed = s.sem("p3_summed")
        o_copied = s.sem("p3_o_copied")
        a_scored = s.sem("p3_a_scored")
        a_step = s.sem("p3_a_step")
        a_expd = s.sem("p3_a_expd")
        a_turned = s.sem("p3_a_turned")
        a_copied = s.sem("p3_a_copied")
        a_summed = s.sem("p3_a_summed")
        stored = s.sem("p3_stored")
        block = ctx.enter_context(nc.Block())
        half = lambda h: slice(HD * h, HD * h + HD)
        consts = ([(qa[half(u), h, :], projT[u, half(h), SEQ:T]) for u in range(2) for h in range(2)]
                  + [(qb[:, :, :], projT[3:6, :, SEQ:T].rearrange("u p t -> p u t")),
                     (kn[:, :, :], projT[6:9, :, SEQ:T].rearrange("u p t -> p u t")), (kna[:, :], projT[2, :, SEQ:T]),
                     (vn[:, :, :], vtok[SEQ:T, :].rearrange("(b q) c -> q b c", q=NQ)), (kca[:, :, :], kaT),
                     (vca[:, :, :], va), (mb[:, :], mask_b), (ma[:, :, :], mask_a), (ska[:, :, :], sink_a),
                     (idt[:, :], ident)])

        @block.sync
        def _(sp):
            for dst, src in consts:
                sp.dma_start(dst, src).then_inc(c_in, 16)
            for b in range(NB):
                if b >= 2:
                    sp.wait_ge(summed, b - 1)
                sp.dma_start(kc[b % 2][:, :, :], kbT[b]).then_inc(cache_in[b % 2], 16)
                sp.dma_start(vc[b % 2][:, :, :], vb[b]).then_inc(cache_in[b % 2], 16)
            sp.wait_ge(o_copied, NB)
            sp.wait_ge(a_copied, 3)
            sp.dma_start(mixT[0:PAIRS, :, SEQ:T].rearrange("u p t -> p u t"), mo[:, :, :]).then_inc(stored, 16)
            sp.wait_ge(stored, 16)

        @block.tensor
        def _(pe):
            pe.wait_ge(c_in, 16 * len(consts))
            pe.wait_ge(q_set, 1)

            def scores(b):
                pe.wait_ge(cache_in[b % 2], 32 * (b // 2 + 1))
                if b >= 2:
                    pe.wait_ge(masked, 2 * (b - 1))
                lo, hi = sbank[2 * (b % 2)], sbank[2 * (b % 2) + 1]
                for p in range(B_PAIRS):
                    pe.matmul(lo[0:RB, :], qz[:, b, p, :], kc[b % 2][:, p, 0:512], start=(p == 0), stop=(p == 2))
                for p in range(B_PAIRS):
                    pe.matmul(hi[0:RB, 0:NKC - 512], qz[:, b, p, :], kc[b % 2][:, p, 512:NKC], start=(p == 0), stop=(p == 2))
                for p in range(B_PAIRS):
                    mm = pe.matmul(hi[0:RB, NKC - 512:NKB - 512], qz[:, b, p, :], kn[:, p, NQ * b:NQ * (b + 1)],
                                   start=(p == 0), stop=(p == 2))
                mm.then_inc(scored, 1)

            def values(b):
                pe.wait_ge(normed, b + 1)
                if b:
                    pe.wait_ge(t_copied, b)
                for t in range(NTB):
                    pe.transpose(tbank[:, t, :], pr[b % 2][:, t * P:(t + 1) * P], idt[0:RB, 0:RB])
                pe.transpose(tbank[0:NQ, NTB, :], pr[b % 2][:, NKC:NKB], idt[0:RB, 0:RB]).then_inc(turned, 1)
                pe.wait_ge(t_copied, b + 1)
                if b:
                    pe.wait_ge(o_copied, b)
                for p in range(B_PAIRS):
                    for t in range(NTB):
                        pe.matmul(obank[:, p, :], vc[b % 2][:, t, p * P:(p + 1) * P], pt[b % 2][:, t, 8 * p:8 * p + 8],
                                  start=(t == 0), stop=False)
                    mm = pe.matmul(obank[:, p, :], vn[:, b, (p + 1) * P:(p + 2) * P], pt[b % 2][0:NQ, NTB, 8 * p:8 * p + 8],
                                   start=False, stop=True)
                mm.then_inc(summed, 1)

            scores(0)
            for b in range(NB):
                if b + 1 < NB:
                    scores(b + 1)
                values(b)
            pe.wait_ge(masked, 2 * NB)
            for b in range(NB):
                o = sbank[b // 2][0:RA, (b % 2) * 256:(b % 2) * 256 + NKA - 1]
                pe.matmul(o[:, 0:A_WIN], qza[:, b, :], kca[:, b, :], start=True, stop=True)
                mm = pe.matmul(o[:, A_WIN:NKA - 1], qza[:, b, :], kna[:, NQ * b:NQ * (b + 1)], start=True, stop=True)
            mm.then_inc(a_scored, 1)
            pe.wait_ge(a_step, 6)
            for b in range(NB):
                pe.transpose(tabank[:, 0, b, :], ra[:, b, 0:A_WIN], idt[0:RA, 0:RA])
                tr = pe.transpose(tabank[0:NQ, 1, b, :], ra[:, b, A_WIN:NKA - 1], idt[0:RA, 0:RA])
            tr.then_inc(a_turned, 1)
            pe.wait_ge(a_copied, 2)
            for b in range(NB):
                pe.matmul(oabank[:, b, :], vca[:, b, :], pta[:, b, :], start=True, stop=False)
                mm = pe.matmul(oabank[:, b, :], vn[:, b, 0:P], ptn[:, b, :], start=False, stop=True)
            mm.then_inc(a_summed, 1)

        @block.scalar
        def _(act):
            for b in range(NB):
                act.wait_ge(biased, b + 1)
                if b >= 2:
                    act.wait_ge(turned, b - 1)
                act.activation(pr[b % 2][:, :], rw[b % 2][:, :], ACT.Exp, bias=st[:, b, 1:2], scale=SCALE,
                               accum_out=st[:, b, 2:3]).then_inc(expd, 1)
                act.wait_ge(turned, b + 1)
                if b >= 2:
                    act.wait_ge(summed, b - 1)
                act.activation(pt[b % 2][:, 0:NTB, :], tbank[:, 0:NTB, :], ACT.Copy)
                act.activation(pt[b % 2][0:NQ, NTB, :], tbank[0:NQ, NTB, :], ACT.Copy).then_inc(t_copied, 1)
            act.wait_ge(a_step, 3)
            act.activation(ra[:, :, :], ra[:, :, :], ACT.Exp, scale=SCALE).then_inc(a_expd, 1)

        @block.vector
        def _(dve):
            dve.memset(qz[:, :, :, :].rearrange("p a b c -> p (a b c)"), 0.0).then_inc(zeroed, 1)
            dve.memset(qza[:, :, :].rearrange("p a b -> p (a b)"), 0.0).then_inc(zeroed, 1)
            dve.wait_ge(zeroed, 2)
            dve.wait_ge(c_in, 16 * len(consts))
            rows = lambda ap: ap.rearrange("p (b q) -> p b q", q=NQ)
            for h in range(2):
                for p in range(B_PAIRS):
                    c = 8 * p + NQ * h
                    dve.tensor_copy(qz[half(h), :, p, c:c + NQ], rows(qb[half(h), p, :]))
                for u in range(2):
                    c = 8 * u + NQ * h
                    i = dve.tensor_copy(qza[half(u), :, c:c + NQ], rows(qa[half(u), h, :]))
            i.then_inc(q_set, 1)

            def normalise(b):
                dve.wait_ge(expd, b + 1)
                dve.reciprocal(st[:, b, 3:4], st[:, b, 2:3]).then_inc(inverted, 1)
                dve.wait_ge(inverted, b + 1)
                dve.tensor_scalar(pr[b % 2][:, :], pr[b % 2][:, :], st[:, b, 3:4], None, ALU.mult).then_inc(normed, 1)

            def copy_out(b):
                dve.wait_ge(summed, b + 1)
                for h in range(2):
                    i = dve.tensor_copy(mo[half(h), A_PAIRS:PAIRS, NQ * b:NQ * (b + 1)],
                                        obank[half(h), :, NQ * h:NQ * (h + 1)])
                i.then_inc(o_copied, 1)

            def mask(b):
                dve.wait_ge(scored, b + 1)
                if b >= 2:
                    dve.wait_ge(expd, b - 1)
                for j, (c0, c1) in enumerate(((0, 512), (512, NKB))):
                    dve.tensor_tensor_reduce(rw[b % 2][:, c0:c1], sbank[2 * (b % 2) + j][0:RB, 0:c1 - c0], mb[:, c0:c1],
                                             1.0, -3.0e38, ALU.add, ALU.max, mx[:, b, j:j + 1]).then_inc(masked, 1)
                dve.wait_ge(masked, 2 * b + 2)
                dve.tensor_reduce(st[:, b, 0:1], mx[:, b, 0:2], AX.X, ALU.max).then_inc(reduced, 1)
                dve.wait_ge(reduced, b + 1)
                dve.tensor_scalar(st[:, b, 1:2], st[:, b, 0:1], -SCALE, None, ALU.mult).then_inc(biased, 1)

            mask(0)
            for b in range(NB):
                if b + 1 < NB:
                    mask(b + 1)
                normalise(b)
                copy_out(b)
            dve.wait_ge(a_scored, 1)
            for j in range(NB // 2):
                i = dve.tensor_tensor(ra[:, 2 * j:2 * j + 2, 0:NKA - 1],
                                      sbank[j][0:RA, :].rearrange("p (b k) -> p b k", b=2)[:, :, 0:NKA - 1],
                                      ma[:, 2 * j:2 * j + 2, :], ALU.add)
            dve.tensor_scalar(ra[:, :, NKA - 1:NKA], ska[:, :, :], 1.0 / SCALE, None, ALU.mult).then_inc(a_step, 1)
            dve.wait_ge(a_step, 1)
            dve.tensor_reduce(sta[:, 0, :], ra[:, :, :], AX.X, ALU.max).then_inc(a_step, 1)
            dve.wait_ge(a_step, 2)
            per_row = lambda k: sta[:, k, :].unsqueeze(2).broadcast_to([RA, NB, NKA])
            dve.tensor_tensor(ra[:, :, :], ra[:, :, :], per_row(0), ALU.subtract).then_inc(a_step, 1)
            dve.wait_ge(a_expd, 1)
            dve.tensor_reduce(sta[:, 1, :], ra[:, :, :], AX.X, ALU.add).then_inc(a_step, 1)
            dve.wait_ge(a_step, 4)
            dve.reciprocal(sta[:, 2, :], sta[:, 1, :]).then_inc(a_step, 1)
            dve.wait_ge(a_step, 5)
            dve.tensor_tensor(ra[:, :, :], ra[:, :, :], per_row(2), ALU.mult).then_inc(a_step, 1)
            dve.wait_ge(a_turned, 1)
            dve.tensor_copy(pta[:, :, :], tabank[:, 0, :, :]).then_inc(a_copied, 1)
            dve.tensor_copy(ptn[:, :, :], tabank[0:NQ, 1, :, :]).then_inc(a_copied, 1)
            dve.wait_ge(a_summed, 1)
            for u in range(2):
                for h in range(2):
                    c = 8 * u + NQ * h
                    i = dve.tensor_copy(rows(mo[half(h), u, :]), oabank[half(u), :, c:c + NQ])
            i.then_inc(a_copied, 1)


def sample_order():
    i = np.arange(2048)
    far = (i < 1536) & (i % 16 < NQ)
    return np.concatenate([i[far], i[i >= 1536], i[(i < 1536) & ~far]])


def sample_masks():
    qn = np.arange(NQ)[:, None]
    index = np.concatenate([sample_order()[:NKC], 2048 + np.arange(NQ)])
    mb = offset_b(2048 + qn - index[None, :])
    ma = offset_a(A_WIN + qn - np.arange(A_WIN + NQ)[None, :])
    return (np.tile(mb, (6, 1)).astype(np.float32),
            np.ascontiguousarray(np.broadcast_to(np.tile(ma, (4, 1))[:, None, :], (4 * NQ, NB, NKA - 1))).astype(np.float32))


NP3 = 3
NZ = 11
GN_EPS = 64e-5
DECAY = float(np.exp(-0.5))


class Steps:

    def __init__(self, sem):
        self.sem, self.number, self.count, self.per_segment = sem, {}, 0, 0

    def done(self, instruction, name):
        self.count += 1
        assert self.number[name] == (self.count - 1) % self.per_segment + 1, name
        instruction.then_inc(self.sem, 1)

    def wait(self, eng, name, seg=0):
        eng.wait_ge(self.sem, seg * self.per_segment + self.number[name])

    def close(self):
        self.per_segment, self.count = self.count, 0


class Rehearsal:

    def __getattr__(self, name):
        return lambda *a, **k: self


class RehearsedSteps:

    def __init__(self, steps):
        self.steps = steps

    def done(self, instruction, name):
        self.steps.count += 1
        self.steps.number[name] = self.steps.count

    def wait(self, eng, name, seg=0):
        pass


def rwkv(nc, outer, tag, sample, src, shift0, state0, cst, wts, mixT, col0, state_out):
    nb, nq = (NB, NQ) if sample else (1, 256)
    W = nb * nq
    C = NS if sample else 64
    nseg = 1 if sample else SEQ // W
    nch = W // C
    nc_ = 1 if sample else 2
    ngr = nch // nc_
    U = nc_ * NP3
    levels = [2] if sample else [2, 4, 8, 16, 32]
    parts = [slice(0, C), slice(HD, HD + C)] if sample else [slice(0, P)]
    half = lambda h: slice(HD * h, HD * h + HD)
    rows = lambda h: slice(HD * h, HD * h + C)
    with ExitStack() as ctx:
        s = Scope(nc, ctx, outer)
        n_ = lambda x: f"{tag}_{x}"
        z = s.sb(n_("z"), [P, NZ, nb, nq + 1])
        d = s.sb(n_("d"), [P, NZ, W])
        zs = s.sb(n_("zs"), [P, NZ, W])
        th = s.sb(n_("th"), [P, W])
        sg = s.sb(n_("sg"), [P, W])
        big = lambda x: s.sb(n_(x), [P, NP3, W])
        lw, av, gg, kk, tA, tB, cs, cp = map(big, ("lw", "av", "gg", "kk", "tA", "tB", "cs", "cp"))
        De, Dp, Di, be, ka, bv, y, yc = map(big, ("De", "Dp", "Di", "be", "ka", "bv", "y", "yc"))
        ar = s.sb(n_("ar"), [P, NP3, nch, 2, C])
        sh0 = s.sb(n_("sh0"), [P, NZ, nb, 1]) if sample else None
        znew = s.sb(n_("znew"), [P, NZ, W]) if sample else None
        am = s.sb(n_("am"), [P, NP3, NB, C]) if sample else None
        vm = s.sb(n_("vm"), [P, NP3, NB, HD]) if sample else None
        um = s.sb(n_("um"), [P, NP3, NB, HD]) if sample else None
        par = s.sb(n_("par"), [P, 32])
        omka = s.sb(n_("omka"), [P, NP3])
        w2 = s.sb(n_("w2"), [P, 384])
        g2 = s.sb(n_("g2"), [P, 384])
        hones = s.sb(n_("hones"), [P, P])
        hmean = s.sb(n_("hmean"), [P, P])
        rko = s.sb(n_("rko"), [P, NP3, P])
        id64 = s.sb(n_("id64"), [P, HD])
        mAB = s.sb(n_("mAB"), [P, NP3, 2, C])
        mT1 = s.sb(n_("mT1"), [P, U, C])
        mM1 = s.sb(n_("mM1"), [P, U, C])
        idU = s.sb(n_("idU"), [P, U, C])
        mL = s.sb(n_("mL"), [P, len(levels), U, C])
        scm = s.sb(n_("scm"), [P, W])
        cc = s.sb(n_("cc"), [P, 1])
        rm = s.sb(n_("rm"), [P, NB]) if sample else None
        GA = s.sb(n_("GA"), [P, 2, nc_, NP3, 2, C])
        GB = s.sb(n_("GB"), [P, 2, nc_, NP3, 2, C])
        Tm = s.sb(n_("Tm"), [P, U, C])
        Tt = s.sb(n_("Tt"), [P, 2, U, C])
        Ys = s.sb(n_("Ys"), [P, U, C])
        ML = s.sb(n_("ML"), [P, len(levels), U, C])
        tok = s.sb(n_("tok"), [P, 2, 3, U, HD])
        rh = s.sb(n_("rh"), [P, NP3, HD])
        uu = s.sb(n_("uu"), [P, NP3, HD])
        NS0 = 1 if sample else 2
        S0 = s.sb(n_("S0"), [P, NS0, NP3, nb, HD])
        S1 = s.sb(n_("S1"), [P, NP3, nb, HD])
        pb = [s.ps(n_(f"pb{i}"), [P, 512]) for i in range(3)]
        q = [s.ps(n_(f"q{i}"), [P, 512]) for i in range(5)]
        c_in = s.sem(n_("c_in"))
        z_in = s.sem(n_("z_in"))
        shift_in = s.sem(n_("shift_in"))
        stored = s.sem(n_("stored"))
        V = Steps(s.sem(n_("vector_step")))
        S = Steps(s.sem(n_("scalar_step")))
        E = Steps(s.sem(n_("tensor_step")))
        G = Steps(s.sem(n_("pool_step")))
        zeroed = s.sem(n_("zeroed"))
        MU, W0, A0, KK, KA, LNW, LNB, RK = 0, 11, 14, 17, 20, 23, 26, 29
        pv = lambda base, p, sl=slice(0, P): par[sl, base + p:base + p + 1]
        consts = [(par[:, :], cst["par"]), (w2[:, :], wts["w2"]), (g2[:, :], wts["g2"]), (hones[:, :], cst["hones"]),
                  (hmean[:, :], cst["hmean"]), (id64[:, :], cst["id64"]), (mAB[:, :, :, :], cst[tag + "AB"]),
                  (mT1[:, :, :], cst[tag + "T1"]), (mM1[:, :, :], cst[tag + "M1"]), (idU[:, :, :], cst[tag + "I"]),
                  (mL[:, :, :, :], cst[tag + "L"]), (scm[:, :], cst[tag + "scan"])]
        if sample:
            consts += [(rm[:, :], cst["rowmask"]), (S0[:, 0], state0)]
        bank = lambda i, n, w: q[i][:, 0:n * w].rearrange("p (u w) -> p u w", u=n)
        unit = lambda ap, g: ap[:, :, g * nc_ * C:(g + 1) * nc_ * C]
        hops = [] if sample else [(c, k) for c in range(nc_) for k in ("rhs", "u", "y")]

        def tensor_segment(e, E, V, S, G, seg):
            W_ = lambda st, name, back=0: st.wait(e, name, seg - back) if seg >= back else None
            W_(S, "tanh"); W_(S, "sd", 1)
            for p in range(NP3):
                mm = e.matmul(pb[p][:, 0:W], w2[0:64, p * P:(p + 1) * P], th[0:64, :], start=True, stop=True)
            E.done(mm, "w_pre")
            W_(S, "lw")
            for p in range(NP3):
                mm = e.matmul(pb[p][:, 0:W], w2[64:128, p * P:(p + 1) * P], zs[64:128, 9, :], start=True, stop=True)
            E.done(mm, "a_pre")
            W_(S, "av"); W_(S, "sgate")
            for p in range(NP3):
                mm = e.matmul(pb[p][:, 0:W], g2[:, p * P:(p + 1) * P], sg[:, :], start=True, stop=True)
            E.done(mm, "g_pre")
            W_(S, "gg"); W_(V, "kk2")
            for p in range(NP3):
                mm = e.matmul(pb[p][:, 0:W], hones[:, :], tA[:, p, :], start=True, stop=True)
            E.done(mm, "kksum")
            W_(V, "ssmax"); W_(V, "rkp")
            for p in range(NP3):
                mm = e.matmul(pb[p][:, 0:W], rko[:, p, :], tA[:, p, :], start=True, stop=True)
            E.done(mm, "bonus")
            W_(V, "rho"); W_(V, "alpha"); W_(V, "beta"); W_(V, "kappa")
            gram = lambda out, lhs, rhs, c: [
                e.matmul(out(p, h), lhs[half(h), p, c * C:(c + 1) * C], rhs(p, h), start=True, stop=True)
                for p in range(NP3) for h in range(2)][-1]

            def hop(g, c, k):
                gc = g * nc_ + c
                pg = g % 2
                if k == "rhs":
                    if g or c:
                        W_(V, ("state", gc - 1)); W_(S, ("y", gc - 1))
                    elif seg:
                        W_(V, ("state", nch - 1), 1); W_(S, ("y", nch - 1), 1)
                    else:
                        e.wait_ge(zeroed, 2)
                    for p in range(NP3):
                        for h in range(2):
                            o = q[3][rows(h), p * HD:(p + 1) * HD]
                            e.matmul(o, ar[half(h), p, gc, 0, :], S0[half(h), gc % 2, p, 0, :], start=True, stop=False)
                            mm = e.matmul(o, GB[rows(h), pg, c, p, 0, :], tok[rows(h), pg, 2, c * NP3 + p, :],
                                          start=False, stop=True)
                    E.done(mm, ("rhs", gc))
                elif k == "u":
                    W_(S, ("rhs", gc)); W_(V, ("tt", g, len(levels) - 1))
                    if g or c:
                        W_(V, ("state", gc - 1))
                    for p in range(NP3):
                        for h in range(2):
                            mm = e.matmul(q[4][rows(h), p * HD:(p + 1) * HD], Tt[rows(h), pg, c * NP3 + p, :],
                                          rh[rows(h), p, :], start=True, stop=True)
                    E.done(mm, ("u", gc))
                else:
                    W_(S, ("u", gc))
                    for p in range(NP3):
                        for h in range(2):
                            o = q[4][half(h), p * HD:(p + 1) * HD]
                            e.matmul(o, tok[rows(h), pg, 0, c * NP3 + p, :], uu[rows(h), p, :], start=True, stop=False)
                            mm = e.matmul(o, tok[rows(h), pg, 1, c * NP3 + p, :], tok[rows(h), pg, 2, c * NP3 + p, :],
                                          start=False, stop=True)
                    E.done(mm, ("s", gc))
                    for p in range(NP3):
                        for h in range(2):
                            o = q[3][half(h), p * C:(p + 1) * C]
                            e.matmul(o, S0[half(h), gc % 2, p, 0, :], ar[half(h), p, gc, 1, :], start=True, stop=False)
                            e.matmul(o, uu[rows(h), p, :], GA[rows(h), pg, c, p, 1, :], start=False, stop=False)
                            mm = e.matmul(o, tok[rows(h), pg, 2, c * NP3 + p, :], GB[rows(h), pg, c, p, 1, :],
                                          start=False, stop=True)
                    E.done(mm, ("y", gc))

            for g in range(ngr + (0 if sample else 1)):
                left = [] if g == 0 else [(g - 1, c, k) for c, k in hops]
                if g < ngr:
                    for c in range(nc_):
                        gc = g * nc_ + c
                        if c:
                            W_(V, ("gab", gc - 1))
                        elif g:
                            W_(V, ("tt", g - 1, len(levels) - 1)); W_(V, ("t", g - 1, len(levels) - 2))
                            W_(S, ("ys", g - 1, len(levels) - 1))
                        elif seg:
                            W_(V, ("tt", ngr - 1, len(levels) - 1), 1); W_(S, ("ys", ngr - 1, len(levels) - 1), 1)
                        gram(lambda p, h: q[0][rows(h), p * 2 * C:(p + 1) * 2 * C], be,
                             lambda p, h: ar[half(h), p, gc].rearrange("p a c -> p (a c)"), gc)
                        mm = gram(lambda p, h: q[1][rows(h), p * 2 * C:(p + 1) * 2 * C], ka,
                                  lambda p, h: ar[half(h), p, gc].rearrange("p a c -> p (a c)"), gc)
                        E.done(mm, ("gab", gc))
                        if c == 0:
                            for c1 in range(nc_):
                                for p in range(NP3):
                                    for h in range(2):
                                        u = c1 * NP3 + p
                                        mm = e.matmul(q[2][rows(h), u * C:(u + 1) * C], ar[half(h), p, g * nc_ + c1, 0, :],
                                                      be[half(h), p, (g * nc_ + c1) * C:(g * nc_ + c1 + 1) * C],
                                                      start=True, stop=True)
                            E.done(mm, ("m", g))
                    for i, x in enumerate((be, ka, zs)):
                        b = (2, 0, 1)[i]
                        if i == 0:
                            W_(V, ("T2", g))
                        else:
                            W_(V, ("gab", g * nc_ + nc_ - 1))
                        for c1 in range(nc_):
                            for p in range(NP3):
                                for h in range(2):
                                    u = c1 * NP3 + p
                                    f = x[half(h), p + (6 if i == 2 else 0), (g * nc_ + c1) * C:(g * nc_ + c1 + 1) * C]
                                    mm = e.matmul(q[b][rows(h), u * HD:(u + 1) * HD], f, id64[half(h), :],
                                                  start=True, stop=True)
                        E.done(mm, ("tok", g, i))
                    for l in range(len(levels)):
                        if l:
                            W_(V, ("tt", g, l - 1))
                        else:
                            W_(S, ("tok", g, 1)); W_(G, ("tt2", g))
                        W_(G, ("ml", g, l))
                        for u in range(U):
                            for h in range(2):
                                mm = e.matmul(q[0][rows(h), u * C:(u + 1) * C], ML[rows(h), l, u, :], Tm[rows(h), u, :],
                                              start=True, stop=True)
                        E.done(mm, ("yl", g, l))
                        if left:
                            hop(*left.pop(0))
                        W_(S, ("ys", g, l))
                        if l == 0:
                            W_(S, ("tok", g, 2)); W_(S, ("tok", g, 0))
                        if l < len(levels) - 1:
                            for u in range(U):
                                for h in range(2):
                                    mm = e.matmul(q[1][rows(h), u * C:(u + 1) * C], Tt[rows(h), g % 2, u, :],
                                                  Ys[rows(h), u, :], start=True, stop=True)
                            E.done(mm, ("dt", g, l))
                        for u in range(U):
                            for h in range(2):
                                mm = e.matmul(q[2][rows(h), u * C:(u + 1) * C], Ys[rows(h), u, :],
                                              Tt[rows(h), g % 2, u, :], start=True, stop=True)
                        E.done(mm, ("dtt", g, l))
                        if left:
                            hop(*left.pop(0))
                while left:
                    hop(*left.pop(0))
            if sample:
                W_(V, "am"); W_(V, "vm"); W_(V, ("tt", 0, len(levels) - 1))
                for p in range(NP3):
                    for h in range(2):
                        o = q[3][rows(h), p * HD:(p + 1) * HD]
                        for b in range(NB):
                            e.matmul(o, am[half(h), p, b, :], S0[half(h), 0, p, b, :], start=(b == 0), stop=False)
                        mm = e.matmul(o, GB[rows(h), 0, 0, p, 0, :], tok[rows(h), 0, 2, p, :], start=False, stop=True)
                E.done(mm, ("rhs", 0))
                W_(S, ("rhs", 0))
                for p in range(NP3):
                    for h in range(2):
                        mm = e.matmul(q[4][rows(h), p * HD:(p + 1) * HD], Tt[rows(h), 0, p, :], rh[rows(h), p, :],
                                      start=True, stop=True)
                E.done(mm, ("u", 0))
                W_(S, ("u", 0)); W_(V, "um")
                for p in range(NP3):
                    for h in range(2):
                        o = q[3][half(h), p * C:(p + 1) * C]
                        e.matmul(o, uu[rows(h), p, :], GA[rows(h), 0, 0, p, 1, :], start=True, stop=False)
                        e.matmul(o, tok[rows(h), 0, 2, p, :], GB[rows(h), 0, 0, p, 1, :], start=False, stop=False)
                        for b in range(NB):
                            mm = e.matmul(q[3][half(h), p * C + NQ * b:p * C + NQ * (b + 1)], S0[half(h), 0, p, b, :],
                                          ar[half(h), p, 0, 1, NQ * b:NQ * (b + 1)], start=False, stop=(b == NB - 1))
                E.done(mm, ("y", 0))
                for p in range(NP3):
                    for h in range(2):
                        o = q[p][half(h), 0:NB * HD]
                        e.matmul(o, tok[rows(h), 0, 0, p, :], um[rows(h), p].rearrange("p b v -> p (b v)"),
                                 start=True, stop=False)
                        mm = e.matmul(o, tok[rows(h), 0, 1, p, :], vm[rows(h), p].rearrange("p b v -> p (b v)"),
                                      start=False, stop=True)
                E.done(mm, ("s", 0))
            W_(S, ("y", nch - 1)); W_(V, "bv")
            for p in range(NP3):
                mm = e.matmul(pb[p][:, 0:W], hmean[:, :], y[:, p, :], start=True, stop=True)
            E.done(mm, "mean")
            W_(S, "ysq"); W_(V, "yc")
            for p in range(NP3):
                mm = e.matmul(pb[p][:, 0:W], hmean[:, :], tB[:, p, :], start=True, stop=True)
            E.done(mm, "var")

        def scalar_segment(e, E, V, S, G, seg):
            W_ = lambda st, name, back=0: st.wait(e, name, seg - back) if seg >= back else None
            W_(V, "mixed"); W_(E, "g_pre", 1)
            S.done(e.activation(th[0:64, :], zs[0:64, 9, :], ACT.Tanh), "tanh")
            S.done(e.activation(sg[:, :], zs[:, 10, :], ACT.Sigmoid), "sgate")
            for name, src_, dst, base in (("lw", "w_pre", lw, W0), ("av", "a_pre", av, A0)):
                W_(E, src_)
                for p in range(NP3):
                    a = e.activation(dst[:, p, :], pb[p][:, 0:W], ACT.Sigmoid, bias=pv(base, p))
                S.done(a, name)
            W_(E, "g_pre"); W_(V, "out", 1)
            for p in range(NP3):
                a = e.activation(gg[:, p, :], pb[p][:, 0:W], ACT.Copy)
            S.done(a, "gg")
            W_(V, "cprev"); W_(V, ("state", nch - 1), 1)
            S.done(e.activation(De[:, :, :], cs[:, :, :], ACT.Exp, scale=-DECAY), "De")
            S.done(e.activation(Dp[:, :, :], cp[:, :, :], ACT.Exp, scale=-DECAY), "Dp")
            S.done(e.activation(Di[:, :, :], cs[:, :, :], ACT.Exp, scale=DECAY), "Di")
            W_(V, "ssmax")
            S.done(e.activation(tB[:, :, :], tB[:, :, :], ACT.Sqrt), "sroot")

            def hop(g, c, k):
                gc = g * nc_ + c
                W_(E, (k, gc))
                if k == "rhs":
                    W_(E, ("u", gc - 1) if gc else ("u", nch - 1), 0 if gc else 1)
                    S.done(e.activation(rh[:, :, :], bank(3, NP3, HD), ACT.Copy), ("rhs", gc))
                elif k == "u":
                    W_(E, ("y", gc - 1) if gc else ("y", nch - 1), 0 if gc else 1)
                    S.done(e.activation(uu[:, :, :], bank(4, NP3, HD), ACT.Copy), ("u", gc))
                else:
                    if gc == 0:
                        W_(V, "yc", 1)
                    S.done(e.activation(y[:, :, gc * C:(gc + 1) * C], bank(3, NP3, C), ACT.Copy), ("y", gc))

            for g in range(ngr + (0 if sample else 1)):
                left = [] if g == 0 else [(g - 1, c, k) for c, k in hops]
                if g < ngr:
                    for i, b in enumerate((2, 0, 1)):
                        W_(E, ("tok", g, i))
                        for sl in parts:
                            a = e.activation(tok[sl, g % 2, i], q[b][sl, 0:U * HD].rearrange("p (u w) -> p u w", u=U), ACT.Copy)
                        S.done(a, ("tok", g, i))
                    for l in range(len(levels)):
                        W_(E, ("yl", g, l))
                        if l:
                            W_(E, ("dtt", g, l - 1))
                        for sl in parts:
                            a = e.activation(Ys[sl], q[0][sl, 0:U * C].rearrange("p (u w) -> p u w", u=U), ACT.Copy)
                        S.done(a, ("ys", g, l))
                        if left:
                            hop(*left.pop(0))
                        if left:
                            hop(*left.pop(0))
                while left:
                    hop(*left.pop(0))
            if sample:
                W_(E, ("rhs", 0))
                for sl in parts:
                    a = e.activation(rh[sl], q[3][sl, 0:NP3 * HD].rearrange("p (u w) -> p u w", u=NP3), ACT.Copy)
                S.done(a, ("rhs", 0))
                W_(E, ("u", 0))
                for sl in parts:
                    a = e.activation(uu[sl], q[4][sl, 0:NP3 * HD].rearrange("p (u w) -> p u w", u=NP3), ACT.Copy)
                S.done(a, ("u", 0))
                W_(E, ("y", 0))
                S.done(e.activation(y[:, :, 0:C], bank(3, NP3, C), ACT.Copy), ("y", 0))
            W_(V, "yc")
            S.done(e.activation(tB[:, :, :], yc[:, :, :], ACT.Square), "ysq")
            W_(E, "var")
            for p in range(NP3):
                a = e.activation(tB[:, p, :], pb[p][:, 0:W], ACT.Sqrt, bias=cc[:, 0:1])
            S.done(a, "sd")

        def vector_segment(e, E, V, S, G, seg):
            W_ = lambda st, name, back=0: st.wait(e, name, seg - back) if seg >= back else None
            own = lambda name: W_(V, name)
            f4 = lambda ap: ap.rearrange("p (b q) -> p b q", b=nb)
            e.wait_ge(z_in, 16 * (seg + 1))
            if sample:
                e.wait_ge(shift_in, 16)
                e.tensor_copy(z[:, :, :, 0:1], sh0[:, :, :, :])
                V.done(e.tensor_copy(z[:, :, :, 1:nq + 1], znew[:, :, :].rearrange("p z (b q) -> p z b q", b=nb)), "z")
                own("z")
            V.done(e.tensor_tensor(d[:, :, :].rearrange("p z (b q) -> p z b q", b=nb) if sample else d[:, :, :],
                                   z[:, :, :, 0:nq] if sample else z[:, :, 0, 0:nq],
                                   z[:, :, :, 1:nq + 1] if sample else z[:, :, 0, 1:nq + 1], ALU.subtract), "shift")
            own("shift")
            W_(E, "a_pre", 1); W_(S, "sgate", 1); W_(E, ("tok", ngr - 1, 2), 1)
            for b in range(NZ):
                i = e.scalar_tensor_tensor(out=f4(zs[:, b, :]), in0=f4(d[:, b, :]), scalar=par[:, MU + b:MU + b + 1],
                                           in1=z[:, b, :, 1:nq + 1], op0=ALU.mult, op1=ALU.add)
            V.done(i, "mixed")
            own("mixed")
            V.done(e.tensor_copy(z[:, :, 0, 0:1], z[:, :, 0, nq:nq + 1]), "carry")
            for p in range(NP3):
                i = e.tensor_scalar(kk[:, p, :], zs[:, 3 + p, :], pv(KK, p), None, ALU.mult)
            V.done(i, "kk")
            own("kk")
            W_(E, "bonus", 1)
            V.done(e.tensor_tensor(tA[:, :, :], kk[:, :, :], kk[:, :, :], ALU.mult), "kk2")
            W_(S, "lw"); W_(S, "Di", 1)
            for p in range(NP3):
                i = e.tensor_tensor_scan(cs[:, p, :], scm[:, :], lw[:, p, :], 0.0, ALU.mult, ALU.add)
            V.done(i, "scan")
            own("scan")
            V.done(e.tensor_tensor(cp[:, :, :], cs[:, :, :], lw[:, :, :], ALU.subtract), "cprev")
            W_(E, "kksum"); W_(E, "var", 1); W_(V, "rsd", 1)
            for p in range(NP3):
                i = e.tensor_scalar(tB[:, p, :], pb[p][:, 0:W], 1e-24, None, ALU.max)
            V.done(i, "ssmax")
            W_(S, "sroot")
            V.done(e.reciprocal(tB[:, :, :], tB[:, :, :]), "sinv")
            own("sinv")
            V.done(e.tensor_tensor(kk[:, :, :], kk[:, :, :], tB[:, :, :], ALU.mult), "kkn")
            W_(S, "av")
            for p in range(NP3):
                i = e.tensor_scalar(tA[:, p, :], av[:, p, :], pv(KA, p), omka[:, p:p + 1], ALU.mult, ALU.add)
            V.done(i, "kscale")
            own("kscale")
            V.done(e.tensor_tensor(yc[:, :, :], zs[:, 3:6, :], tA[:, :, :], ALU.mult), "kp")
            W_(S, "Di")
            own("kp")
            last = ("y", nch - 1)
            W_(E, last, 1)
            for p in range(NP3):
                i = e.tensor_tensor(ar[:, p, :, 0, :], Dp[:, p, :].rearrange("p (c t) -> p c t", t=C),
                                    kk[:, p, :].rearrange("p (c t) -> p c t", t=C), ALU.mult)
            V.done(i, "alpha")
            for p in range(NP3):
                i = e.tensor_tensor(ar[:, p, :, 1, :], De[:, p, :].rearrange("p (c t) -> p c t", t=C),
                                    zs[:, p, :].rearrange("p (c t) -> p c t", t=C), ALU.mult)
            V.done(i, "rho")
            V.done(e.scalar_tensor_tensor(out=be[:, :, :], in0=kk[:, :, :], scalar=-1.0, in1=av[:, :, :],
                                          op0=ALU.mult, op1=ALU.mult), "beta0")
            own("beta0")
            V.done(e.tensor_tensor(be[:, :, :], be[:, :, :], Di[:, :, :], ALU.mult), "beta")
            V.done(e.tensor_tensor(ka[:, :, :], yc[:, :, :], Di[:, :, :], ALU.mult), "kappa")
            own("kappa")
            V.done(e.tensor_tensor(tA[:, :, :], yc[:, :, :], zs[:, 0:3, :], ALU.mult), "rkp")
            W_(E, "bonus")
            if seg:
                e.wait_ge(stored, 16 * seg)
            for p in range(NP3):
                i = e.tensor_tensor(bv[:, p, :], zs[:, 6 + p, :], pb[p][:, 0:W], ALU.mult)
            V.done(i, "bv")

            def state(gc):
                W_(E, ("s", gc))
                if gc == 0:
                    W_(V, ("state", nch - 1), 1)
                V.done(e.tensor_tensor(S1[:, :, 0, :], S0[:, gc % 2, :, 0, :], bank(4, NP3, HD), ALU.add), ("sum", gc))
                own(("sum", gc))
                W_(E, ("y", gc - 1) if gc else ("y", nch - 1), 0 if gc else 1)
                for p in range(NP3):
                    i = e.tensor_scalar(S0[:, (gc + 1) % 2, p, 0, :], S1[:, p, 0, :],
                                        De[:, p, gc * C + C - 1:gc * C + C], None, ALU.mult)
                V.done(i, ("state", gc))

            for g in range(ngr + (0 if sample else 1)):
                left = [] if g == 0 else [(g - 1) * nc_ + c for c in range(nc_)]
                if g < ngr:
                    for c in range(nc_):
                        gc = g * nc_ + c
                        W_(E, ("gab", gc))
                        if c == 0 and g >= 2:
                            W_(E, ("y", (g - 1) * nc_ - 1))
                        elif c == 0 and g < 2:
                            W_(E, ("y", nch - 1), 1)
                        if c == 0 and g:
                            W_(G, ("ml", g - 1, len(levels) - 1))
                        elif c == 0:
                            W_(G, ("ml", ngr - 1, len(levels) - 1), 1)
                        for sl in parts:
                            for i_, GX in enumerate((GA, GB)):
                                i = e.tensor_tensor(GX[sl, g % 2, c].rearrange("p a b c -> p (a b c)"),
                                                    q[i_][sl, 0:NP3 * 2 * C],
                                                    mAB[sl].rearrange("p a b c -> p (a b c)"), ALU.mult)
                        V.done(i, ("gab", gc))
                        if c == 0:
                            W_(E, ("m", g))
                            if g:
                                W_(E, ("yl", g - 1, len(levels) - 1))
                            else:
                                W_(E, ("yl", ngr - 1, len(levels) - 1), 1)
                            for sl in parts:
                                i = e.tensor_tensor(Tm[sl], q[2][sl, 0:U * C].rearrange("p (u w) -> p u w", u=U),
                                                    mT1[sl], ALU.mult)
                            V.done(i, ("T1", g))
                            own(("T1", g))
                            for sl in parts:
                                i = e.tensor_tensor(Tm[sl], Tm[sl], idU[sl], ALU.add)
                            V.done(i, ("T2", g))
                    for l in range(len(levels)):
                        if l < len(levels) - 1:
                            W_(E, ("dt", g, l))
                            own(("T2", g) if l == 0 else ("t", g, l - 1))
                            for sl in parts:
                                i = e.tensor_tensor(Tm[sl], Tm[sl], q[1][sl, 0:U * C].rearrange("p (u w) -> p u w", u=U),
                                                    ALU.add)
                            V.done(i, ("t", g, l))
                        W_(E, ("dtt", g, l))
                        if l == 0:
                            W_(G, ("tt2", g))
                        else:
                            own(("tt", g, l - 1))
                        for sl in parts:
                            i = e.tensor_tensor(Tt[sl, g % 2], Tt[sl, g % 2],
                                                q[2][sl, 0:U * C].rearrange("p (u w) -> p u w", u=U), ALU.add)
                        V.done(i, ("tt", g, l))
                        if l in (1, 3) and left:
                            state(left.pop(0))
                while left:
                    state(left.pop(0))
            if sample:
                e.wait_ge(zeroed, 2)
                for b in range(NB):
                    i = e.tensor_copy(am[:, :, b, NQ * b:NQ * (b + 1)], ar[:, :, 0, 0, NQ * b:NQ * (b + 1)])
                V.done(i, "am")
                W_(S, ("tok", 0, 2))
                for name, dst, src_ in (("vm", vm, None), ("um", um, uu)):
                    if name == "um":
                        W_(S, ("u", 0))
                    for sl in parts:
                        for p in range(NP3):
                            rv = tok[sl, 0, 2, p, :] if src_ is None else uu[sl, p, :]
                            n = sl.stop - sl.start
                            i = e.tensor_tensor(dst[sl, p], rv.unsqueeze(1).broadcast_to([n, NB, HD]),
                                                rm[sl].unsqueeze(2).broadcast_to([n, NB, HD]), ALU.mult)
                    V.done(i, name)
                W_(E, ("s", 0))
                for p in range(NP3):
                    i = e.tensor_tensor(S1[:, p], S0[:, 0, p], q[p][:, :].rearrange("p (b v) -> p b v", b=NB), ALU.add)
                V.done(i, "sum")
                own("sum")
                for p in range(NP3):
                    last_d = De[:, p, :].rearrange("p (b q) -> p b q", b=NB)[:, :, NQ - 1:NQ]
                    i = e.tensor_tensor(S1[:, p], S1[:, p], last_d.broadcast_to([P, NB, HD]), ALU.mult)
                V.done(i, ("state", 0))
            W_(E, "mean"); own("rkp")
            for p in range(NP3):
                i = e.tensor_tensor(yc[:, p, :], y[:, p, :], pb[p][:, 0:W], ALU.subtract)
            V.done(i, "yc")
            W_(S, "sd")
            V.done(e.reciprocal(tB[:, :, :], tB[:, :, :]), "rsd")
            own("rsd")
            V.done(e.tensor_tensor(yc[:, :, :], yc[:, :, :], tB[:, :, :], ALU.mult), "yn")
            own("yn")
            for p in range(NP3):
                i = e.tensor_scalar(yc[:, p, :], yc[:, p, :], pv(LNW, p), pv(LNB, p), ALU.mult, ALU.add)
            V.done(i, "ln")
            own("ln")
            V.done(e.tensor_tensor(yc[:, :, :], yc[:, :, :], bv[:, :, :], ALU.add), "plus")
            own("plus")
            V.done(e.tensor_tensor(bv[:, :, :], yc[:, :, :], gg[:, :, :], ALU.mult), "out")

        def pool_segment(e, E, V, S, G, seg):
            W_ = lambda st, name, back=0: st.wait(e, name, seg - back) if seg >= back else None
            for g in range(ngr):
                W_(V, ("gab", g * nc_ + nc_ - 1))
                if g >= 2:
                    W_(E, ("u", (g - 1) * nc_ - 1))
                else:
                    W_(E, ("u", nch - 1), 1)
                mt = lambda sl, c: GA[sl, g % 2, c, :, 0, :]
                for sl in parts:
                    for c in range(nc_):
                        i = e.tensor_tensor(Tt[sl, g % 2, c * NP3:(c + 1) * NP3], mt(sl, c),
                                            mM1[sl, c * NP3:(c + 1) * NP3], ALU.mult)
                G.done(i, ("tt1", g))
                W_(G, ("tt1", g))
                for sl in parts:
                    i = e.tensor_tensor(Tt[sl, g % 2], Tt[sl, g % 2], idU[sl], ALU.add)
                G.done(i, ("tt2", g))
                for l in range(len(levels)):
                    if g:
                        W_(E, ("yl", g - 1, l))
                    else:
                        W_(E, ("yl", ngr - 1, l), 1)
                    for sl in parts:
                        for c in range(nc_):
                            i = e.tensor_tensor(ML[sl, l, c * NP3:(c + 1) * NP3], mt(sl, c),
                                                mL[sl, l, c * NP3:(c + 1) * NP3], ALU.mult)
                    G.done(i, ("ml", g, l))

        for segment, steps in ((tensor_segment, E), (scalar_segment, S), (vector_segment, V), (pool_segment, G)):
            r = {id(x): RehearsedSteps(x) for x in (E, V, S, G)}
            segment(Rehearsal(), *[r[id(x)] for x in (E, V, S, G)], 1)
            steps.close()
        block = ctx.enter_context(nc.Block())

        @block.sync
        def _(sp):
            for dst, src_ in consts:
                sp.dma_start(dst, src_).then_inc(c_in, 16)
            if sample:
                sp.dma_start(sh0[:, :, :, :], shift0).then_inc(shift_in, 16)
            for seg in range(nseg):
                if seg:
                    V.wait(sp, "carry", seg - 1)
                    sp.dma_start(z[:, :, 0, 1:nq + 1], src[:, :, W * seg:W * (seg + 1)].rearrange("z p t -> p z t")).then_inc(z_in, 16)
                elif sample:
                    sp.dma_start(znew[:, :, :], src[:, :, SEQ:T].rearrange("z p t -> p z t")).then_inc(z_in, 16)
                else:
                    sp.dma_start(z[:, :, 0, 1:nq + 1], src[:, :, 0:W].rearrange("z p t -> p z t")).then_inc(z_in, 16)
                if seg:
                    V.wait(sp, "out", seg - 1)
                    sp.dma_start(mixT[:, :, col0 + W * (seg - 1):col0 + W * seg].rearrange("k p t -> p k t"), bv[:, :, :]).then_inc(stored, 16)
            V.wait(sp, "out", nseg - 1)
            sp.dma_start(mixT[:, :, col0 + W * (nseg - 1):col0 + W * nseg].rearrange("k p t -> p k t"), bv[:, :, :]).then_inc(stored, 16)
            V.wait(sp, ("state", nch - 1), nseg - 1)
            sp.dma_start(state_out, S1[:, :, :, :] if sample else S0[:, nch % 2]).then_inc(stored, 16)
            sp.wait_ge(stored, 16 * (nseg + 1))

        @block.tensor
        def _(pe):
            pe.wait_ge(c_in, 16 * len(consts))
            pe.wait_ge(zeroed, 1)
            for seg in range(nseg):
                tensor_segment(pe, E, V, S, G, seg)

        @block.scalar
        def _(act):
            act.wait_ge(c_in, 16 * len(consts))
            act.wait_ge(zeroed, 1)
            for seg in range(nseg):
                scalar_segment(act, E, V, S, G, seg)

        @block.vector
        def _(dve):
            dve.wait_ge(c_in, 16 * len(consts))
            dve.memset(cc[:, 0:1], GN_EPS)
            if not sample:
                dve.memset(z[:, :, 0, 0:1], 0.0)
            dve.tensor_scalar(omka[:, :], par[:, KA:KA + 3], -1.0, 1.0, ALU.mult, ALU.add)
            for p in range(NP3):
                i = dve.tensor_scalar(rko[:, p, :], hones[:, :], pv(RK, p), None, ALU.mult)
            i.then_inc(zeroed, 1)
            dve.wait_ge(zeroed, 1)
            if sample:
                dve.memset(am[:, :, :, :].rearrange("p a b c -> p (a b c)"), 0.0).then_inc(zeroed, 1)
            else:
                dve.memset(S0[:, 0].rearrange("p a b v -> p (a b v)"), 0.0).then_inc(zeroed, 1)
            for seg in range(nseg):
                vector_segment(dve, E, V, S, G, seg)

        @block.gpsimd
        def _(pool):
            pool.wait_ge(c_in, 16 * len(consts))
            for seg in range(nseg):
                pool_segment(pool, E, V, S, G, seg)


def rwkv_constants():
    out = {}
    for tag, C, group, U, levels, W in (("cp", 64, 64, 6, [2, 4, 8, 16, 32], 256), ("cs", NS, NQ, 3, [2], NS)):
        i = np.arange(P)[:, None] % HD
        j = np.arange(C)[None, :]
        live = (i < C) & (i // group == j // group)
        below = lambda a, b, n: (a // (2 * n) == b // (2 * n)) & (a // n % 2 == 0) & (b // n % 2 == 1)
        tile = lambda m, *dims: np.ascontiguousarray(np.broadcast_to(
            m.astype(np.float32).reshape((P,) + (1,) * len(dims) + m.shape[1:]), (P,) + dims + m.shape[1:]))
        out[tag + "AB"] = tile(np.stack([live & (i < j), live & (i <= j)], 1), NP3)
        out[tag + "M1"] = tile(live & below(i, j, 1), U)
        out[tag + "T1"] = tile(live & below(j, i, 1), U)
        out[tag + "I"] = tile(i == j, U)
        out[tag + "L"] = np.stack([tile(live & below(i, j, n), U) for n in levels], 1)
        out[tag + "scan"] = tile(np.arange(W)[None] % group != 0 + 0 * np.arange(P)[:, None])
    same = (np.arange(P)[:, None] // HD == np.arange(P)[None, :] // HD).astype(np.float32)
    out["hones"], out["hmean"] = same, same / HD
    out["id64"] = (np.arange(P)[:, None] % HD == np.arange(HD)[None, :]).astype(np.float32)
    out["rowmask"] = (np.arange(P)[:, None] % HD // NQ == np.arange(NB)[None, :]).astype(np.float32)
    return out


def out_project(nc, outer, mixT, xtok, w_o, g2, ident, x2, h2T):
    NT = SEQ // P + 1
    tiles = [(P * i, P) for i in range(SEQ // P)] + [(SEQ, NS)]
    with ExitStack() as ctx:
        s = Scope(nc, ctx, outer)
        wo = s.sb("p5_wo", [P, KC, D])
        g = s.sb("p5_g", [P, KC])
        idt = s.sb("p5_ident", [P, P])
        eps = s.sb("p5_eps", [P, 1])
        m = [s.sb(f"p5_mix{i}", [P, KC, P]) for i in range(2)]
        xt = [s.sb(f"p5_x{i}", [P, D]) for i in range(2)]
        junk = s.sb("p5_junk", [P, D])
        xn = [s.sb(f"p5_xn{i}", [P, D]) for i in range(2)]
        st = s.sb("p5_stat", [P, 4, 2])
        ht = [s.sb(f"p5_h{i}", [P, KC, P]) for i in range(2)]
        acc = [[s.ps(f"p5_acc{i}{h}", [P, 512]) for h in range(2)] for i in range(2)]
        tp = [s.ps(f"p5_tp{h}", [P, 4, P]) for h in range(2)]
        consts_in = s.sem("p5_consts_in")
        eps_set = s.sem("p5_eps_set")
        tile_in = [s.sem(f"p5_tile_in{i}") for i in range(2)]
        producted = s.sem("p5_producted")
        added = s.sem("p5_added")
        squared = s.sem("p5_squared")
        rooted = s.sem("p5_rooted")
        inverted = s.sem("p5_inverted")
        scaled = s.sem("p5_scaled")
        turned = s.sem("p5_turned")
        h_out = s.sem("p5_h_out")
        x_stored = [s.sem(f"p5_x_stored{i}") for i in range(2)]
        h_stored = [s.sem(f"p5_h_stored{i}") for i in range(2)]
        block = ctx.enter_context(nc.Block())

        @block.sync
        def _(sp):
            sp.dma_start(wo[:, :, :], w_o).then_inc(consts_in, 16)
            sp.dma_start(g[:, :], g2).then_inc(consts_in, 16)
            sp.dma_start(idt[:, :], ident).then_inc(consts_in, 16)

            def load(t):
                r0, n = tiles[t]
                if t >= 2:
                    sp.wait_ge(producted, t - 1)
                    sp.wait_ge(scaled, t - 1)
                    sp.wait_ge(x_stored[t % 2], 16 * (t // 2))
                sp.dma_start(m[t % 2][:, :, 0:n], mixT[:, :, r0:r0 + n].rearrange("k p n -> p k n")).then_inc(tile_in[t % 2], 16)
                sp.dma_start(xt[t % 2][0:n, :], xtok[r0:r0 + n, :]).then_inc(tile_in[t % 2], 16)

            load(0)
            load(1)
            for t, (r0, n) in enumerate(tiles):
                sp.wait_ge(added, t + 1)
                sp.dma_start(x2[r0:r0 + n, :], xt[t % 2][0:n, :]).then_inc(x_stored[t % 2], 16)
                if t + 2 < NT:
                    load(t + 2)
                sp.wait_ge(h_out, t + 1)
                sp.dma_start(h2T[:, :, r0:r0 + n].rearrange("k p n -> p k n"), ht[t % 2][:, :, 0:n]).then_inc(h_stored[t % 2], 16)
            for j in range(2):
                sp.wait_ge(x_stored[j], 16 * ((NT + 1 - j) // 2))
                sp.wait_ge(h_stored[j], 16 * ((NT + 1 - j) // 2))

        @block.tensor
        def _(pe):
            pe.wait_ge(consts_in, 48)

            def turn(t):
                n = tiles[t][1]
                pe.wait_ge(scaled, t + 1)
                if t:
                    pe.wait_ge(h_out, t)
                for k in range(KC):
                    tr = pe.transpose(tp[k // 4][:, k % 4, 0:n], xn[t % 2][0:n, k * P:(k + 1) * P], idt[0:n, 0:n])
                tr.then_inc(turned, 1)

            for t, (r0, n) in enumerate(tiles):
                pe.wait_ge(tile_in[t % 2], 32 * (t // 2 + 1))
                if t >= 2:
                    pe.wait_ge(added, t - 1)
                for h in range(2):
                    for k in range(KC):
                        mm = pe.matmul(acc[t % 2][h][0:n, :], m[t % 2][:, k, 0:n], wo[:, k, h * 512:(h + 1) * 512],
                                       start=(k == 0), stop=(k == KC - 1))
                mm.then_inc(producted, 1)
                if t:
                    turn(t - 1)
            turn(NT - 1)

        @block.scalar
        def _(act):
            act.wait_ge(eps_set, 1)
            for t, (r0, n) in enumerate(tiles):
                act.wait_ge(added, t + 1)
                act.activation(junk[0:n, :], xt[t % 2][0:n, :], ACT.Square,
                               accum_out=st[0:n, 0, t % 2:t % 2 + 1]).then_inc(squared, 1)
                act.wait_ge(squared, t + 1)
                act.activation(st[0:n, 1, t % 2:t % 2 + 1], st[0:n, 0, t % 2:t % 2 + 1], ACT.Sqrt,
                               bias=eps[0:n, 0:1], scale=1.0 / D).then_inc(rooted, 1)
                act.wait_ge(inverted, t + 1)
                if t >= 2:
                    act.wait_ge(turned, t - 1)
                act.activation(xn[t % 2][0:n, :], xt[t % 2][0:n, :], ACT.Copy,
                               scale=st[0:n, 2, t % 2:t % 2 + 1]).then_inc(scaled, 1)

        @block.vector
        def _(dve):
            dve.memset(eps[:, :], EPS).then_inc(eps_set, 1)
            dve.wait_ge(consts_in, 48)

            def copy_out(t):
                n = tiles[t][1]
                dve.wait_ge(turned, t + 1)
                if t >= 2:
                    dve.wait_ge(h_stored[t % 2], 16 * (t // 2))
                for k in range(KC):
                    c = dve.tensor_scalar(ht[t % 2][:, k, 0:n], tp[k // 4][:, k % 4, 0:n], g[:, k:k + 1], None, ALU.mult)
                c.then_inc(h_out, 1)

            for t, (r0, n) in enumerate(tiles):
                dve.wait_ge(producted, t + 1)
                dve.wait_ge(tile_in[t % 2], 32 * (t // 2 + 1))
                for h in range(2):
                    xs = xt[t % 2][0:n, h * 512:(h + 1) * 512]
                    a = dve.tensor_tensor(xs, xs, acc[t % 2][h][0:n, :], ALU.add)
                a.then_inc(added, 1)
                dve.wait_ge(rooted, t + 1)
                dve.reciprocal(st[0:n, 2, t % 2:t % 2 + 1], st[0:n, 1, t % 2:t % 2 + 1]).then_inc(inverted, 1)
                if t:
                    copy_out(t - 1)
            copy_out(NT - 1)


FFB = 32
SUP = 2
NSUP = FFB // SUP


def super_loop(eng, body):
    body(0)
    body(1)
    with eng.Fori(1, NSUP // 2 - 1) as i:
        body(i * 2, 0)
        body(i * 2 + 1, 1)
    body(NSUP - 2)
    body(NSUP - 1)


def mlp_half(nc, outer, tag, c0, groups, tiles, h2T, x2, w_up, w_dn, fg, y_out):
    W = sum(n for _, n in groups)
    ng, nt = len(groups), len(tiles)
    NU, ND = ng, (4 if 2 * nt % 4 == 0 else 3)
    with ExitStack() as ctx:
        s = Scope(nc, ctx, outer)
        n_ = lambda x: f"{tag}_{x}"
        hh = s.sb(n_("hh"), [P, KC, W], F32R)
        hl = s.sb(n_("hl"), [P, KC, W], F32R)
        y = s.sb(n_("y"), [P, nt, D])
        uh = s.sb(n_("uh"), [P, 2, SUP, W], F32R)
        ul = s.sb(n_("ul"), [P, 2, SUP, W], F32R)
        wur = s.sb(n_("wur"), [P, 2, KC, P])
        wuh = s.sb(n_("wuh"), [P, 2, KC, P], F32R)
        wul = s.sb(n_("wul"), [P, 2, KC, P], F32R)
        wdr = s.sb(n_("wdr"), [P, 2, D])
        wdh = s.sb(n_("wdh"), [P, 2, D], F32R)
        wdl = s.sb(n_("wdl"), [P, 2, D], F32R)
        r = s.sb(n_("r"), [P, 2, 512])
        sq = s.sb(n_("sq"), [P, 2, 512])
        fgb = s.sb(n_("fg"), [P, D])
        eps = s.sb(n_("eps"), [P, 1])
        st = s.sb(n_("stat"), [P, 3, nt])
        ub = [s.ps(n_(f"ub{i}"), [P, 512]) for i in range(NU)]
        db = [s.ps(n_(f"db{i}"), [P, 512]) for i in range(ND)]
        row_in = [s.sem(n_(f"row_in{i}")) for i in range(2)]
        y_in = s.sem(n_("y_in"))
        fg_in = s.sem(n_("fg_in"))
        eps_set = s.sem(n_("eps_set"))
        wu_in = [s.sem(n_(f"wu_in{i}")) for i in range(2)]
        wd_in = [s.sem(n_(f"wd_in{i}")) for i in range(2)]
        h_high = s.sem(n_("h_high"))
        h_low = s.sem(n_("h_low"))
        wu_high = s.sem(n_("wu_high"))
        wu_low = s.sem(n_("wu_low"))
        wd_high = s.sem(n_("wd_high"))
        wd_low = s.sem(n_("wd_low"))
        up_done = s.sem(n_("up_done"))
        relued = s.sem(n_("relued"))
        u_high = s.sem(n_("u_high"))
        u_sq = s.sem(n_("u_sq"))
        u_low = s.sem(n_("u_low"))
        down_done = s.sem(n_("down_done"))
        y_added = s.sem(n_("y_added"))
        squared = s.sem(n_("squared"))
        rooted = s.sem(n_("rooted"))
        inverted = s.sem(n_("inverted"))
        normed = s.sem(n_("normed"))
        out_st = s.sem(n_("out_st"))
        block = ctx.enter_context(nc.Block())
        rows = [(k, g) for k in range(KC) for g in range(ng)]

        @block.sync
        def _(sp):
            for j in range(2):
                sp.dma_start(wur[:, j], w_up[j]).then_inc(wu_in[j], 16)
            for a, (k, g) in enumerate(rows):
                g0, n = groups[g]
                if a >= 2:
                    sp.wait_ge(h_low, a - 1)
                sp.dma_start(r[:, a % 2, 0:n], h2T[k, :, c0 + g0:c0 + g0 + n]).then_inc(row_in[a % 2], 16)
            for j in range(2):
                sp.dma_start(wdr[:, j], w_dn[j]).then_inc(wd_in[j], 16)
            for a, (t0, n) in enumerate(tiles):
                sp.dma_start(y[0:n, a, :], x2[c0 + t0:c0 + t0 + n, :]).then_inc(y_in, 16)
            sp.dma_start(fgb[:, :], fg).then_inc(fg_in, 16)
            with sp.Fori(0, FFB // 2 - 1) as i:
                for j in range(2):
                    sp.wait_ge(wu_low, 2 * i + j + 1)
                    sp.dma_start(wur[:, j], w_up[2 * i + j + 2]).then_inc(wu_in[j], 16)
                for j in range(2):
                    sp.wait_ge(wd_low, 2 * i + j + 1)
                    sp.dma_start(wdr[:, j], w_dn[2 * i + j + 2]).then_inc(wd_in[j], 16)
            for a, (t0, n) in enumerate(tiles):
                sp.wait_ge(normed, a + 1)
                sp.dma_start(y_out[c0 + t0:c0 + t0 + n, :], y[0:n, a, :]).then_inc(out_st, 16)
            sp.wait_ge(out_st, 16 * nt)

        def passes(pe, out, wh, wl, mh, ml, first, last):
            pe.matmul(out, wh, mh, start=first, stop=False)
            pe.matmul(out, wh, ml, start=False, stop=False)
            return pe.matmul(out, wl, mh, start=False, stop=last)

        @block.tensor
        def _(pe):
            pe.wait_ge(h_low, len(rows))

            def up(sup, par, first):
                for j in range(SUP):
                    pe.wait_ge(wu_low, sup * SUP + j + 1)
                    for g, (g0, n) in enumerate(groups):
                        if not (first and j == 0):
                            pe.wait_ge(relued, (sup * SUP + j - 1) * ng + g + 1)
                        for k in range(KC):
                            mm = passes(pe, ub[g][:, 0:n], wuh[:, j, k, :], wul[:, j, k, :],
                                        hh[:, k, g0:g0 + n], hl[:, k, g0:g0 + n], k == 0, k == KC - 1)
                        mm.then_inc(up_done, 1)

            def down(sup, par, first):
                pe.wait_ge(u_low, (sup + 1) * SUP * ng)
                pe.wait_ge(wd_low, (sup + 1) * SUP)
                for a, (t0, n) in enumerate(tiles):
                    for h in range(2):
                        b = 2 * a + h
                        if not (first and b < ND):
                            pe.wait_ge(y_added, sup * 2 * nt + b - ND + 1)
                        for j in range(SUP):
                            mm = passes(pe, db[b % ND][0:n, :], uh[:, par, j, t0:t0 + n], ul[:, par, j, t0:t0 + n],
                                        wdh[:, j, h * 512:(h + 1) * 512], wdl[:, j, h * 512:(h + 1) * 512],
                                        j == 0, j == SUP - 1)
                        mm.then_inc(down_done, 1)

            def body(sup, par=None):
                first = par is None and sup == 0
                par = sup % 2 if par is None else par
                up(sup, par, first)
                if not first:
                    down(sup - 1, 1 - par, isinstance(sup, int) and sup == 1)

            super_loop(pe, body)
            down(NSUP - 1, (NSUP - 1) % 2, False)

        @block.scalar
        def _(act):
            for a, (k, g) in enumerate(rows):
                g0, n = groups[g]
                act.wait_ge(row_in[a % 2], 16 * (a // 2 + 1))
                act.activation(hh[:, k, g0:g0 + n], r[:, a % 2, 0:n], ACT.Copy).then_inc(h_high, 1)

            def high_up(pair, j, n_before, first=False):
                act.wait_ge(wu_in[j], (pair + 1) * 16)
                if not first:
                    act.wait_ge(up_done, n_before)
                act.activation(wuh[:, j], wur[:, j], ACT.Copy).then_inc(wu_high, 1)

            def high_u(sup, j, par, first):
                for g, (g0, n) in enumerate(groups):
                    q = (j * ng + g) % 2
                    done = (sup * SUP + j) * ng + g
                    act.wait_ge(up_done, done + 1)
                    if not (first and j * ng + g < 2):
                        act.wait_ge(u_sq, done - 1)
                    act.activation(r[:, q, 0:n], ub[g][:, 0:n], ACT.Relu).then_inc(relued, 1)
                    act.wait_ge(relued, done + 1)
                    act.activation(uh[:, par, j, g0:g0 + n], r[:, q, 0:n], ACT.Square).then_inc(u_high, 1)

            def body(sup, par=None):
                first = par is None and sup == 0
                last = par is None and sup == NSUP - 1
                par = sup % 2 if par is None else par
                high_up(sup, 1, sup * SUP * ng, first)
                if not (isinstance(sup, int) and sup < 2):
                    act.wait_ge(down_done, (sup - 1) * 2 * nt)
                high_u(sup, 0, par, first)
                if not last:
                    high_up(sup + 1, 0, (sup * SUP + 1) * ng)
                high_u(sup, 1, par, False)
                if not first:
                    act.wait_ge(down_done, sup * 2 * nt)
                for j in range(SUP):
                    act.wait_ge(wd_in[j], (sup + 1) * 16)
                    act.activation(wdh[:, j], wdr[:, j], ACT.Copy).then_inc(wd_high, 1)

            high_up(0, 0, 0, True)
            super_loop(act, body)
            act.wait_ge(eps_set, 1)
            act.wait_ge(y_added, NSUP * 2 * nt)
            for a, (t0, n) in enumerate(tiles):
                if a:
                    act.wait_ge(squared, a)
                for_junk = uh[0:n, 0, :, :].rearrange("p a b -> p (a b)")[:, 0:D]
                act.activation(for_junk, y[0:n, a, :], ACT.Square, accum_out=st[0:n, 0, a:a + 1]).then_inc(squared, 1)
            act.wait_ge(squared, nt)
            for a, (t0, n) in enumerate(tiles):
                act.activation(st[0:n, 1, a:a + 1], st[0:n, 0, a:a + 1], ACT.Sqrt,
                               bias=eps[0:n, 0:1], scale=1.0 / D).then_inc(rooted, 1)

        @block.vector
        def _(dve):
            dve.memset(eps[:, :], EPS).then_inc(eps_set, 1)
            for a, (k, g) in enumerate(rows):
                g0, n = groups[g]
                dve.wait_ge(h_high, a + 1)
                dve.tensor_tensor(hl[:, k, g0:g0 + n], r[:, a % 2, 0:n], hh[:, k, g0:g0 + n].bitcast(F32),
                                  ALU.subtract).then_inc(h_low, 1)

            def low_up(blk, j):
                dve.wait_ge(wu_high, blk + 1)
                dve.tensor_tensor(wul[:, j], wur[:, j], wuh[:, j].bitcast(F32), ALU.subtract).then_inc(wu_low, 1)

            def low_u(sup, j, par, first):
                for g, (g0, n) in enumerate(groups):
                    q = (j * ng + g) % 2
                    done = (sup * SUP + j) * ng + g
                    dve.wait_ge(relued, done + 1)
                    if not (first and j * ng + g < 2):
                        dve.wait_ge(u_low, done - 1)
                    dve.tensor_tensor(sq[:, q, 0:n], r[:, q, 0:n], r[:, q, 0:n], ALU.mult).then_inc(u_sq, 1)
                    dve.wait_ge(u_sq, done + 1)
                    dve.wait_ge(u_high, done + 1)
                    dve.tensor_tensor(ul[:, par, j, g0:g0 + n], sq[:, q, 0:n], uh[:, par, j, g0:g0 + n].bitcast(F32),
                                      ALU.subtract).then_inc(u_low, 1)

            def add_down(sup, first):
                if first:
                    dve.wait_ge(y_in, 16 * nt)
                for a, (t0, n) in enumerate(tiles):
                    for h in range(2):
                        b = 2 * a + h
                        dve.wait_ge(down_done, sup * 2 * nt + b + 1)
                        ys = y[0:n, a, h * 512:(h + 1) * 512]
                        if not first:
                            dve.wait_ge(y_added, (sup - 1) * 2 * nt + b + 1)
                        dve.tensor_tensor(ys, ys, db[b % ND][0:n, :], ALU.add).then_inc(y_added, 1)

            def body(sup, par=None):
                first = par is None and sup == 0
                last = par is None and sup == NSUP - 1
                par = sup % 2 if par is None else par
                low_up(sup * SUP + 1, 1)
                low_u(sup, 0, par, first)
                if not last:
                    low_up(sup * SUP + 2, 0)
                low_u(sup, 1, par, False)
                if not first:
                    add_down(sup - 1, isinstance(sup, int) and sup == 1)
                for j in range(SUP):
                    dve.wait_ge(wd_high, sup * SUP + j + 1)
                    dve.tensor_tensor(wdl[:, j], wdr[:, j], wdh[:, j].bitcast(F32), ALU.subtract).then_inc(wd_low, 1)

            low_up(0, 0)
            super_loop(dve, body)
            add_down(NSUP - 1, False)
            dve.wait_ge(fg_in, 16)
            for a, (t0, n) in enumerate(tiles):
                dve.wait_ge(rooted, a + 1)
                dve.reciprocal(st[0:n, 2, a:a + 1], st[0:n, 1, a:a + 1]).then_inc(inverted, 1)
                dve.wait_ge(inverted, a + 1)
                ys = y[0:n, a, :]
                dve.scalar_tensor_tensor(out=ys, in0=ys, scalar=st[0:n, 2, a:a + 1], in1=fgb[0:n, :],
                                         op0=ALU.mult, op1=ALU.mult).then_inc(normed, 1)


def decoder_trunk(nc, A):
    with ExitStack() as outer:
        mixT = nc.dram_tensor("mixT", (KC, P, T), F32).ap()
        x2 = nc.dram_tensor("x2", (T, D), F32).ap()
        h2T = nc.dram_tensor("h2T", (KC, P, T), F32).ap()
        cst = {k[4:]: v for k, v in A.items() if k.startswith("cst_")}
        wts = {"w2": A["lora"], "g2": A["c_g2"]}
        project(nc, outer, A["xT"], A["g1"], A["cst_ones"], A["w_fm"], A["w_v"], A["projT"], A["vtok"])
        prompt_attention(nc, outer, A["projT"], A["vtok"], A["cst_strip_a"], A["cst_strip_b"], A["sinks"],
                         A["cst_ident"], mixT)
        sample_attention(nc, outer, A["projT"], A["vtok"], A["kbT"], A["vb"], A["kaT"], A["va"], A["cst_mask_b"],
                         A["cst_mask_a"], A["sink_a"], A["cst_ident"], mixT)
        zc, mixC = A["projT"][ZC0:FMB], mixT[PAIRS:KC]
        rwkv(nc, outer, "cp", False, zc, None, None, cst, wts, mixC, 0, A["state_p"])
        rwkv(nc, outer, "cs", True, zc, A["shift0"], A["state0"], cst, wts, mixC, SEQ, A["state_s"])
        out_project(nc, outer, mixT, A["x"], A["w_o"], A["g2"], A["cst_ident"], x2, h2T)
        tiles = [(P * i, P) for i in range(8)]
        mlp_half(nc, outer, "ma", 0, [(0, 512), (512, 512)], tiles, h2T, x2, A["w_up"], A["w_dn"], A["fg"], A["y"])
        mlp_half(nc, outer, "mb", SEQ // 2, [(0, 352), (352, 352), (704, 352)], tiles + [(SEQ // 2, NS)], h2T, x2,
                 A["w_up"], A["w_dn"], A["fg"], A["y"])


def kernel(**inputs):
    import concourse.bacc as bacc
    from concourse.bass_utils import run_bass_kernel_spmd as run

    I = {k: np.asarray(v) for k, v in inputs.items()}
    nc = bacc.Bacc("TRN2", target_bir_lowering=False, num_devices=1)
    arrays, A = {}, {}

    def give(name, a):
        a = np.ascontiguousarray(a)
        arrays[name] = a
        A[name] = nc.dram_tensor(name, a.shape, mybir.dt.from_np(a.dtype), kind="ExternalInput").ap()

    cols = lambda a, n: a.reshape(n, P).T
    x = np.concatenate([I["x_prompt"][0], I["x_sample"].reshape(NS, D)], 0)
    give("x", x)
    give("xT", x.T.reshape(KC, P, T).transpose(1, 0, 2))
    give("g1", cols(I["norm1_g"][0], KC))
    give("g2", cols(I["norm2_g"][0], KC))
    give("fg", np.broadcast_to(I["final_norm_g"][None], (P, D)))
    w_in = I["w_in"][0].reshape(KC, P, 24, P)
    v_blocks = [3, 10, 11, 12]
    give("w_fm", w_in[:, :, [b for b in range(24) if b not in v_blocks]].transpose(2, 1, 0, 3))
    give("w_v", w_in[:, :, v_blocks].transpose(1, 0, 2, 3).reshape(P, KC, NV))
    give("w_o", I["w_out"][0].reshape(KC, P, D).transpose(1, 0, 2))
    give("w_up", I["mlp_up"][0].reshape(KC, P, FFB, P).transpose(2, 1, 0, 3))
    give("w_dn", I["mlp_down"][0].reshape(FFB, P, D))
    give("sinks", np.broadcast_to(I["a_sink"], (P, 4)))
    give("sink_a", np.broadcast_to(np.repeat(I["a_sink"][0], NQ)[:, None, None], (4 * NQ, NB, 1)))
    give("lora", np.concatenate([I["c_w2"][0], I["c_a2"][0]], 0))
    give("c_g2", I["c_g2"][0])
    give("cst_par", np.concatenate([cols(I["c_mu"][0], NZ)] + [cols(I[k][0].reshape(-1), NP3) for k in
                                   ("c_w0", "c_a0", "c_k_k", "c_k_a", "c_ln_w", "c_ln_b", "c_r_k")], 1))
    order = sample_order()
    kb = I["cache_b_k"][0][:, order[:NKC]].reshape(NB, NKC, B_PAIRS, P)
    give("kbT", kb.transpose(0, 3, 2, 1))
    give("vb", I["cache_b_v"][0][:, order[:NKC]].reshape(NB, NTB, P, 384).transpose(0, 2, 1, 3))
    give("kaT", I["cache_a_k"][0].reshape(NB, A_WIN, P).transpose(2, 0, 1))
    give("va", I["cache_a_v"][0].reshape(NB, A_WIN, P).transpose(1, 0, 2))
    give("shift0", I["state_c_shift"][0].reshape(NB, NZ, P).transpose(2, 1, 0)[..., None])
    give("state0", I["state_c_wkv"][0].reshape(NB, NP3, 2, HD, HD).transpose(2, 4, 1, 0, 3).reshape(P, NP3, NB, HD))
    strip_a, strip_b = strips()
    mask_b, mask_a = sample_masks()
    for name, a in dict(rwkv_constants(), ones=np.ones((P, P), np.float32), ident=np.eye(P, dtype=np.float32),
                        strip_a=strip_a, strip_b=strip_b, mask_b=mask_b, mask_a=mask_a).items():
        give("cst_" + name, a)
    for name, shape in (("y", (T, D)), ("projT", (FMB, P, T)), ("vtok", (T, NV)), ("state_p", (P, NP3, 1, HD)),
                        ("state_s", (P, NP3, NB, HD))):
        A[name] = nc.dram_tensor("out_" + name, shape, F32, kind="ExternalOutput").ap()
    decoder_trunk(nc, A)
    r = run(nc, [arrays], core_ids=[0]).results[0]
    y, projT, vtok = r["out_y"], r["out_projT"], r["out_vtok"]

    def rows(blocks, lo, hi, *shape):
        return np.ascontiguousarray(projT[blocks][:, :, lo:hi].transpose(2, 0, 1)).reshape(*shape)

    def values(c0, c1, lo, hi, *shape):
        return np.ascontiguousarray(vtok[lo:hi, c0:c1]).reshape(*shape)

    def state(a, n):
        return np.ascontiguousarray(a.reshape(2, HD, NP3, n, HD).transpose(3, 2, 0, 4, 1)).reshape(1, n, 6, HD, HD)

    ka, kb, zc = slice(2, 3), slice(6, 9), slice(ZC0, FMB)
    return (y[:SEQ].reshape(1, SEQ, D), y[SEQ:].reshape(NB, NQ, D),
            rows(ka, SEQ - P, SEQ, 1, 1, P, 2, HD), values(0, P, SEQ - P, SEQ, 1, 1, P, 2, HD),
            rows(kb, 0, SEQ, 1, 1, SEQ, 6, HD), values(P, NV, 0, SEQ, 1, 1, SEQ, 6, HD),
            state(r["out_state_p"], 1), rows(zc, SEQ - 1, SEQ, 1, 1, NZ * P),
            rows(ka, SEQ, T, 1, NB, NQ, 2, HD), values(0, P, SEQ, T, 1, NB, NQ, 2, HD),
            rows(kb, SEQ, T, 1, NB, NQ, 6, HD), values(P, NV, SEQ, T, 1, NB, NQ, 6, HD),
            state(r["out_state_s"], NB),
            np.ascontiguousarray(rows(zc, SEQ, T, NB, NQ, NZ * P)[:, NQ - 1]).reshape(1, NB, NZ * P))
```

```python
from contextlib import ExitStack

import numpy as np
import concourse.bass as bass
from concourse import mybir

F32 = mybir.dt.float32
F32R = mybir.dt.float32r
ACT = mybir.ActivationFunctionType
ALU = mybir.AluOpType
AX = mybir.AxisListType

P = 128
D = 1024
KC = D // P
SEQ, NB, NQ = 2048, 8, 4
NS = NB * NQ
T = SEQ + NS
TG = 416
NG = T // TG
HD = 64
FMB = 20
ZC0 = 9
NV = 512
EPS = 1e-5


class Scope:

    def __init__(self, nc, ctx, outer):
        self.nc, self.ctx, self.outer = nc, ctx, outer

    def sb(self, name, shape, dt=F32):
        return self.ctx.enter_context(self.nc.sbuf_tensor(name, shape, dt))

    def ps(self, name, shape):
        return self.ctx.enter_context(self.nc.psum_tensor(name, shape, F32))

    def sem(self, name):
        return self.outer.enter_context(self.nc.semaphore(name))


def project(nc, outer, xT, g1, ones, w_fm, w_v, projT, vtok):
    with ExitStack() as ctx:
        s = Scope(nc, ctx, outer)
        xh = s.sb("p1_xh", [P, KC, T], F32R)
        xl = s.sb("p1_xl", [P, KC, T], F32R)
        rs = s.sb("p1_rs", [P, TG])
        g = s.sb("p1_g", [P, KC])
        on = s.sb("p1_ones", [P, P])
        eps = s.sb("p1_eps", [P, 1])
        wr = s.sb("p1_wr", [P, KC, P])
        wh = [s.sb(f"p1_wh{i}", [P, KC, P], F32R) for i in range(2)]
        wl = [s.sb(f"p1_wl{i}", [P, KC, P], F32R) for i in range(2)]
        ob = [s.sb(f"p1_ob{i}", [P, NV]) for i in range(NG)]
        with ExitStack() as start:
            xs = [start.enter_context(nc.sbuf_tensor(f"p1_xs{i}", [P, KC, TG], F32)) for i in range(2)]
            sq = start.enter_context(nc.sbuf_tensor("p1_sq", [P, KC, TG], F32))
        wvh = s.sb("p1_wvh", [P, KC, NV], F32R)
        wvl = s.sb("p1_wvl", [P, KC, NV], F32R)
        bank = [s.ps(f"p1_bank{i}", [P, 512]) for i in range(NG)]
        sbank = s.ps("p1_sum", [P, 512])
        vbank = [s.ps(f"p1_vbank{i}", [P, NV]) for i in range(2)]
        x_in = [s.sem(f"p1_x_in{i}") for i in range(2)]
        consts_in = s.sem("p1_consts_in")
        eps_set = s.sem("p1_eps_set")
        w_in = s.sem("p1_w_in")
        squared = s.sem("p1_squared")
        summed = s.sem("p1_summed")
        rooted = s.sem("p1_rooted")
        norm_step = s.sem("p1_norm_step")
        h_high = s.sem("p1_h_high")
        h_low = s.sem("p1_h_low")
        w_high = s.sem("p1_w_high")
        w_low = s.sem("p1_w_low")
        block_done = s.sem("p1_block_done")
        evac = s.sem("p1_evac")
        stored = [s.sem(f"p1_stored{i}") for i in range(NG)]
        v_done = s.sem("p1_v_done")
        v_evac = s.sem("p1_v_evac")
        NT = SEQ // P + 1
        tiles = [(P * i, P) for i in range(SEQ // P)] + [(SEQ, NS)]
        start_steps = [[(0, gi)] + ([(1, gi - 1)] if gi else []) for gi in range(NG)]
        start_steps[-1].append((1, NG - 1))
        start_order = [bg for step in start_steps for bg in step]
        cols = lambda gi: slice(gi * TG, (gi + 1) * TG)
        w0_free = start_order.index((0, NG - 1)) + 1
        VP = KC * NV // (KC * P)
        vpart = lambda ap, i: ap[:, i * KC // VP:(i + 1) * KC // VP, :].rearrange("p k n -> p (k n)")
        block = ctx.enter_context(nc.Block())

        @block.sync
        def _(sp):
            def load_x(gi):
                if gi >= 2:
                    sp.wait_ge(h_low, gi - 1)
                sp.dma_start(xs[gi % 2][:, :, :], xT[:, :, cols(gi)]).then_inc(x_in[gi % 2], 16)

            load_x(0)
            sp.dma_start(on[:, :], ones).then_inc(consts_in, 16)
            sp.dma_start(g[:, :], g1).then_inc(consts_in, 16)
            load_x(1)
            sp.dma_start(wr[:, :, :], w_fm[0]).then_inc(w_in, 16)
            sp.wait_ge(w_low, 1)
            sp.dma_start(wr[:, :, :], w_fm[1]).then_inc(w_in, 16)
            for gi in range(2, NG):
                load_x(gi)
            sp.wait_ge(w_low, 2)
            sp.dma_start(wr[:, :, :], w_fm[2]).then_inc(w_in, 16)
            for n, (b, gi) in enumerate(start_order):
                sp.wait_ge(evac, n + 1)
                sp.dma_start(projT[b, :, cols(gi)], ob[n % NG][:, 0:TG]).then_inc(stored[n % NG], 16)
            sp.wait_ge(w_low, 3)
            sp.dma_start(wr[:, :, :], w_fm[3]).then_inc(w_in, 16)
            with sp.Fori(1, FMB // 2 - 1) as i:
                for j in range(2):
                    for gi in range(NG):
                        sp.wait_ge(evac, (2 * i + j) * NG + gi + 1)
                        sp.dma_start(projT[2 * i + j, :, cols(gi)], ob[gi][:, 0:TG]).then_inc(stored[gi], 16)
                        if gi == 2:
                            sp.wait_ge(w_low, 2 * i + j + 2)
                            sp.dma_start(wr[:, :, :], w_fm[2 * i + j + 2]).then_inc(w_in, 16)
            for b in range(FMB - 2, FMB):
                for gi in range(NG):
                    sp.wait_ge(evac, b * NG + gi + 1)
                    sp.dma_start(projT[b, :, cols(gi)], ob[gi][:, 0:TG]).then_inc(stored[gi], 16)
                    if b == FMB - 1 and gi < VP:
                        sp.wait_ge(w_low, FMB + gi)
                        sp.dma_start(wr[:, :, :].rearrange("p k n -> p (k n)"), vpart(w_v, gi)).then_inc(w_in, 16)
            for t, (r0, n) in enumerate(tiles):
                sp.wait_ge(v_evac, t + 1)
                sp.dma_start(vtok[r0:r0 + n, :], ob[t % NG][0:n, :]).then_inc(stored[t % NG], 16)
            for gi in range(NG):
                sp.wait_ge(stored[gi], 16 * (FMB + len(range(gi, NT, NG))))

        def passes(pe, out, wh_, wl_, mh, ml, k):
            pe.matmul(out, wh_, mh, start=(k == 0), stop=False)
            pe.matmul(out, wh_, ml, start=False, stop=False)
            return pe.matmul(out, wl_, mh, start=False, stop=(k == KC - 1))

        @block.tensor
        def _(pe):
            def sum_squares(gi):
                pe.wait_ge(squared, gi + 1)
                if gi:
                    pe.wait_ge(rooted, gi)
                for k in range(KC):
                    mm = pe.matmul(sbank[:, 0:TG], on[:, :], sq[:, k, :],
                                   start=(k == 0), stop=(k == KC - 1))
                mm.then_inc(summed, 1)

            def product(j, gi, b):
                for k in range(KC):
                    mm = passes(pe, bank[b][:, 0:TG], wh[j][:, k, :], wl[j][:, k, :],
                                xh[:, k, cols(gi)], xl[:, k, cols(gi)], k)
                mm.then_inc(block_done, 1)

            pe.wait_ge(consts_in, 32)
            sum_squares(0)
            n = 0
            for gi in range(NG):
                if gi + 1 < NG:
                    sum_squares(gi + 1)
                pe.wait_ge(h_low, gi + 1)
                for b, gb in start_steps[gi]:
                    pe.wait_ge(w_low, b + 1)
                    if n >= NG:
                        pe.wait_ge(evac, n - NG + 1)
                    product(b, gb, n % NG)
                    n += 1
            with pe.Fori(1, FMB // 2) as i:
                for j in range(2):
                    pe.wait_ge(w_low, 2 * i + j + 1)
                    for gi in range(NG):
                        pe.wait_ge(evac, (2 * i + j - 1) * NG + gi + 1)
                        product(j, gi, gi)
            pe.wait_ge(w_low, FMB + VP)
            for t, (r0, n) in enumerate(tiles):
                if t >= 2:
                    pe.wait_ge(v_evac, t - 1)
                for k in range(KC):
                    mm = passes(pe, vbank[t % 2][0:n, :], xh[:, k, r0:r0 + n], xl[:, k, r0:r0 + n],
                                wvh[:, k, :], wvl[:, k, :], k)
                mm.then_inc(v_done, 1)

        @block.scalar
        def _(act):
            def square(gi):
                act.wait_ge(x_in[gi % 2], 16 * (gi // 2 + 1))
                if gi:
                    act.wait_ge(summed, gi)
                act.activation(sq[:, :, :], xs[gi % 2][:, :, :], ACT.Square).then_inc(squared, 1)

            def high_w(n, j):
                act.wait_ge(w_in, (n + 1) * 16)
                act.activation(wh[j][:, :, :], wr[:, :, :], ACT.Copy).then_inc(w_high, 1)

            act.wait_ge(eps_set, 1)
            square(0)
            n = 0
            for gi in range(NG):
                if gi + 1 < NG:
                    square(gi + 1)
                act.wait_ge(summed, gi + 1)
                if gi:
                    act.wait_ge(norm_step, 2 * gi)
                act.activation(rs[:, :], sbank[:, 0:TG], ACT.Sqrt, bias=eps[:, 0:1], scale=1.0 / D).then_inc(rooted, 1)
                if gi == 0:
                    high_w(0, 0)
                act.wait_ge(norm_step, 2 * gi + 2)
                act.activation(xh[:, :, cols(gi)], xs[gi % 2][:, :, :], ACT.Copy).then_inc(h_high, 1)
                if gi == 0:
                    high_w(1, 1)
                for _ in (start_steps[gi - 1] if gi else []) + (start_steps[gi] if gi == NG - 1 else []):
                    act.wait_ge(block_done, n + 1)
                    if n >= NG:
                        act.wait_ge(stored[n % NG], 16 * (n // NG))
                    act.activation(ob[n % NG][:, 0:TG], bank[n % NG][:, 0:TG], ACT.Copy).then_inc(evac, 1)
                    n += 1
                    if n == w0_free + 1:
                        high_w(2, 0)

            def copy_block(i, j, more):
                for gi in range(NG):
                    act.wait_ge(stored[gi], (2 * i + j) * 16)
                    act.wait_ge(block_done, (2 * i + j) * NG + gi + 1)
                    act.activation(ob[gi][:, 0:TG], bank[gi][:, 0:TG], ACT.Copy).then_inc(evac, 1)
                    if gi == 0 and more:
                        high_w(2 * i + j + 1, 1 - j)
                    if gi < VP and not more:
                        act.wait_ge(w_in, (FMB + gi + 1) * 16)
                        act.activation(vpart(wvh, gi), wr[:, :, :].rearrange("p k n -> p (k n)"), ACT.Copy).then_inc(w_high, 1)

            with act.Fori(1, FMB // 2 - 1) as i:
                copy_block(i, 0, True)
                copy_block(i, 1, True)
            copy_block(FMB // 2 - 1, 0, True)
            copy_block(FMB // 2 - 1, 1, False)

        @block.vector
        def _(dve):
            def low_w(n, j):
                dve.wait_ge(w_high, n + 1)
                dve.tensor_tensor(wl[j][:, :, :], wr[:, :, :], wh[j][:, :, :].bitcast(F32),
                                  ALU.subtract).then_inc(w_low, 1)

            dve.memset(eps[:, :], EPS).then_inc(eps_set, 1)
            dve.wait_ge(consts_in, 32)
            for gi in range(NG):
                dve.wait_ge(rooted, gi + 1)
                dve.reciprocal(rs[:, :], rs[:, :]).then_inc(norm_step, 1)
                dve.wait_ge(norm_step, 2 * gi + 1)
                for k in range(KC):
                    xk = xs[gi % 2][:, k, :]
                    mul = dve.scalar_tensor_tensor(out=xk, in0=xk, scalar=g[:, k:k + 1], in1=rs[:, :],
                                                   op0=ALU.mult, op1=ALU.mult)
                mul.then_inc(norm_step, 1)
                if gi == 0:
                    low_w(0, 0)
                dve.wait_ge(norm_step, 2 * gi + 2)
                dve.wait_ge(h_high, gi + 1)
                dve.tensor_tensor(xl[:, :, cols(gi)], xs[gi % 2][:, :, :], xh[:, :, cols(gi)].bitcast(F32),
                                  ALU.subtract).then_inc(h_low, 1)
                if gi == 0:
                    low_w(1, 1)
            low_w(2, 0)
            low_w(3, 1)
            with dve.Fori(2, FMB // 2) as i:
                for j in range(2):
                    low_w(2 * i + j, j)
            for i in range(VP):
                dve.wait_ge(w_high, FMB + i + 1)
                dve.tensor_tensor(vpart(wvl, i), wr[:, :, :].rearrange("p k n -> p (k n)"), vpart(wvh, i).bitcast(F32),
                                  ALU.subtract).then_inc(w_low, 1)
            for t, (r0, n) in enumerate(tiles):
                dve.wait_ge(v_done, t + 1)
                dve.wait_ge(stored[t % NG], 16 * (FMB + t // NG))
                dve.tensor_copy(ob[t % NG][0:n, :], vbank[t % 2][0:n, :]).then_inc(v_evac, 1)


TQ = SEQ // P
SCALE = HD ** -0.5
A_PAIRS, B_PAIRS = 2, 3
PAIRS = A_PAIRS + B_PAIRS
QB = [0, 1, 3, 4, 5]
KB = [2, 2, 6, 7, 8]
LAG = 2


def prompt_attention(nc, outer, projT, vtok, strip_a, strip_b, sinks, ident, mixT):
    jobs = [(u, t, h) for u in range(PAIRS) for t in range(TQ) for h in range(2)]
    first_block = lambda u, t: max(0, t - 1) if u < A_PAIRS else 0
    groups, done_groups = [], []
    for u, t, h in jobs:
        b0 = first_block(u, t)
        groups.append([(b, min(4, t + 1 - b)) for b in range(b0, t + 1, 4)])
        done_groups.append((done_groups[-1] if done_groups else 0) + len(groups[-1]))
    before = lambda n: done_groups[n] - len(groups[n])
    with ExitStack() as ctx:
        s = Scope(nc, ctx, outer)
        q = [s.sb(f"p2_q{i}", [P, 2, SEQ]) for i in range(2)]
        k = [s.sb(f"p2_k{i}", [P, SEQ]) for i in range(2)]
        v = [s.sb(f"p2_v{i}", [P, TQ, P]) for i in range(2)]
        mo = [s.sb(f"p2_mo{i}", [P, SEQ]) for i in range(2)]
        sa = s.sb("p2_strip_a", [P, 2 * P])
        sbm = s.sb("p2_strip_b", [P, SEQ])
        idt = s.sb("p2_ident", [P, P])
        sink = s.sb("p2_sink", [P, 4])
        sink8 = s.sb("p2_sink8", [P, 4])
        row = [s.sb(f"p2_row{i}", [P, SEQ]) for i in range(3)]
        pt = s.sb("p2_pt", [P, 4, 4, P])
        mx = s.sb("p2_mx", [P, 2, 4])
        mr = s.sb("p2_mr", [P, 2])
        nb = s.sb("p2_nb", [P, 4])
        den = s.sb("p2_den", [P, 4])
        sex = s.sb("p2_sex", [P, 4])
        rec = s.sb("p2_rec", [P, 4])
        on = s.sb("p2_on", [P, 2, P])
        sbank = [s.ps(f"p2_s{i}", [P, 512]) for i in range(3)]
        tbank = [s.ps(f"p2_t{i}", [P, 4, P]) for i in range(2)]
        obank = [s.ps(f"p2_o{i}", [P, P]) for i in range(2)]
        xbank = s.ps("p2_x", [P, P])
        consts_in = s.sem("p2_consts_in")
        q_zeroed = s.sem("p2_q_zeroed")
        pair_in = [s.sem(f"p2_pair_in{i}") for i in range(2)]
        scored = s.sem("p2_scored")
        masked = s.sem("p2_masked")
        reduced = s.sem("p2_reduced")
        biased = s.sem("p2_biased")
        sink_set = s.sem("p2_sink_set")
        expd = s.sem("p2_expd")
        turned = s.sem("p2_turned")
        t_copied = s.sem("p2_t_copied")
        used = s.sem("p2_used")
        summed_a = s.sem("p2_summed_a")
        inverted = s.sem("p2_inverted")
        normed = s.sem("p2_normed")
        o_turned = s.sem("p2_o_turned")
        o_copied = s.sem("p2_o_copied")
        m_stored = [s.sem(f"p2_m_stored{i}") for i in range(2)]
        slots = []
        for n in range(len(jobs) + LAG):
            sizes = [len(groups[m]) for m in (n, n - LAG) if 0 <= m < len(jobs)]
            slots += [(n, i) for i in range(max(sizes))]
        block = ctx.enter_context(nc.Block())
        hp = lambda h: slice(HD * h, HD * (h + 1))

        @block.sync
        def _(sp):
            def load(u):
                if u >= 2:
                    sp.wait_ge(used, done_groups[2 * TQ * (u - 1) - 1])
                sem = pair_in[u % 2]
                for h in range(2):
                    sp.dma_start(q[u % 2][hp(h), h, :], projT[QB[u], hp(h), 0:SEQ]).then_inc(sem, 16)
                if u < A_PAIRS:
                    for h in range(2):
                        sp.dma_start(k[u % 2][hp(h), :], projT[KB[u], hp(u), 0:SEQ]).then_inc(sem, 16)
                    for h in range(2):
                        sp.dma_start(v[u % 2][:, :, hp(h)],
                                     vtok[0:SEQ, hp(u)].rearrange("(t p) c -> p t c", p=P)).then_inc(sem, 16)
                else:
                    sp.dma_start(k[u % 2][:, :], projT[KB[u], :, 0:SEQ]).then_inc(sem, 16)
                    c = P * (u - A_PAIRS + 1)
                    sp.dma_start(v[u % 2][:, :, :],
                                 vtok[0:SEQ, c:c + P].rearrange("(t p) c -> p t c", p=P)).then_inc(sem, 16)

            load(0)
            sp.dma_start(sa[:, :], strip_a).then_inc(consts_in, 16)
            sp.dma_start(sbm[:, :], strip_b).then_inc(consts_in, 16)
            sp.dma_start(idt[:, :], ident).then_inc(consts_in, 16)
            sp.dma_start(sink[:, :], sinks).then_inc(consts_in, 16)
            load(1)
            for u in range(PAIRS):
                if u + 2 < PAIRS:
                    load(u + 2)
                sp.wait_ge(o_copied, TQ * (u + 1))
                sp.dma_start(mixT[u, :, 0:SEQ], mo[u % 2][:, :]).then_inc(m_stored[u % 2], 16)
            sp.wait_ge(m_stored[0], 16 * 3)
            sp.wait_ge(m_stored[1], 16 * 2)

        n_dma = [6 if u < A_PAIRS else 4 for u in range(PAIRS)]
        pair_value = [16 * sum(n_dma[w] for w in range(u % 2, u + 1, 2)) for u in range(PAIRS)]
        @block.tensor
        def _(pe):
            pe.wait_ge(consts_in, 64)
            pe.wait_ge(q_zeroed, 4)

            def score(n, i):
                u, t, h = jobs[n]
                b, nb_ = groups[n][i]
                c = before(n) + i
                if c >= 3:
                    pe.wait_ge(masked, c - 2)
                pe.matmul(sbank[c % 3][:, 0:nb_ * P], q[u % 2][:, h, t * P:(t + 1) * P],
                          k[u % 2][:, b * P:(b + nb_) * P], start=True, stop=True).then_inc(scored, 1)

            def turn(n, i):
                b, nb_ = groups[n][i]
                at = before(n) + i
                if i == 0:
                    pe.wait_ge(expd, n + 1)
                if at >= 2:
                    pe.wait_ge(t_copied, at - 1)
                c0 = (b - groups[n][0][0]) * P
                for j in range(nb_):
                    tr = pe.transpose(tbank[at % 2][:, j, :], row[n % 3][:, c0 + j * P:c0 + (j + 1) * P], idt[:, :])
                tr.then_inc(turned, 1)

            def times_v(n, i):
                u, t, h = jobs[n]
                b, nb_ = groups[n][i]
                c = before(n) + i
                if i == 0 and n >= 2:
                    pe.wait_ge(normed, n - 1)
                pe.wait_ge(t_copied, c + 1)
                for j in range(nb_):
                    mm = pe.matmul(obank[n % 2][:, :], pt[:, c % 4, j, :], v[u % 2][:, b + j, :],
                                   start=(i == 0 and j == 0), stop=(b + j == t))
                mm.then_inc(used, 1)

            def turn_out(m):
                pe.wait_ge(normed, 2 * m + 2)
                if m:
                    pe.wait_ge(o_copied, m)
                pe.transpose(xbank[:, :], on[:, m % 2, :], idt[:, :]).then_inc(o_turned, 1)

            pending = None
            for n, i in slots:
                if i == 0 and n < len(jobs) and jobs[n][1:] == (0, 0):
                    u = jobs[n][0]
                    pe.wait_ge(pair_in[u % 2], pair_value[u])
                if n < len(jobs) and i < len(groups[n]):
                    score(n, i)
                if 0 <= n - LAG < len(jobs) and i < len(groups[n - LAG]):
                    turn(n - LAG, i)
                    if pending:
                        times_v(*pending)
                    pending = (n - LAG, i)
                if i == 0 and n - LAG >= 2 and (n - LAG) % 2 == 0:
                    turn_out((n - LAG) // 2 - 1)
            times_v(*pending)
            turn_out(len(jobs) // 2 - 1)

        @block.scalar
        def _(act):
            act.wait_ge(consts_in, 64)
            for n, (u, t, h) in enumerate(jobs):
                act.wait_ge(biased, n + 1)
                if n >= 4:
                    act.wait_ge(normed, n - 3)
                w = (t + 1 - groups[n][0][0]) * P
                ex = act.activation(row[n % 3][:, 0:w], row[n % 3][:, 0:w], ACT.Exp, bias=nb[:, n % 4:n % 4 + 1],
                                    scale=SCALE, accum_out=den[:, n % 4:n % 4 + 1])
                ex.then_inc(expd, 1)
                if u < A_PAIRS:
                    act.activation(sex[:, n % 4:n % 4 + 1], sink[:, 2 * u + h:2 * u + h + 1], ACT.Exp,
                                   bias=nb[:, n % 4:n % 4 + 1]).then_inc(sink_set, 1)

        @block.gpsimd
        def _(pool):
            for h in range(2):
                pool.memset(q[1][hp(1 - h), h, :], 0.0).then_inc(q_zeroed, 1)

        @block.vector
        def _(dve):
            for h in range(2):
                dve.memset(q[0][hp(1 - h), h, :], 0.0).then_inc(q_zeroed, 1)
            dve.wait_ge(consts_in, 64)
            dve.tensor_scalar(sink8[:, :], sink[:, :], 1.0 / SCALE, None, ALU.mult).then_inc(reduced, 1)

            def mask(n, i):
                u, t, h = jobs[n]
                b0 = groups[n][0][0]
                strip = sa if u < A_PAIRS else sbm
                off = (1 if u < A_PAIRS else TQ - 1) - t
                if i == 0 and n >= 3:
                    dve.wait_ge(turned, done_groups[n - 3])
                b, nb_ = groups[n][i]
                c = before(n) + i
                dve.wait_ge(scored, c + 1)
                dve.tensor_tensor_reduce(row[n % 3][:, (b - b0) * P:(b - b0 + nb_) * P], sbank[c % 3][:, 0:nb_ * P],
                                         strip[:, (b + off) * P:(b + off + nb_) * P], 1.0, -3.0e38, ALU.add, ALU.max,
                                         mx[:, n % 2, i:i + 1]).then_inc(masked, 1)

            def bias(n):
                u, t, h = jobs[n]
                dve.wait_ge(masked, done_groups[n])
                dve.tensor_reduce(mr[:, n % 2:n % 2 + 1], mx[:, n % 2, 0:len(groups[n])], AX.X, ALU.max).then_inc(reduced, 1)
                dve.wait_ge(reduced, n + 2)
                if n >= 4:
                    dve.wait_ge(expd, n - 3)
                    if jobs[n - 4][0] < A_PAIRS:
                        dve.wait_ge(sink_set, n - 3)
                if u < A_PAIRS:
                    dve.tensor_scalar(nb[:, n % 4:n % 4 + 1], mr[:, n % 2:n % 2 + 1], sink8[:, 2 * u + h:2 * u + h + 1],
                                      -SCALE, ALU.max, ALU.mult).then_inc(biased, 1)
                else:
                    dve.tensor_scalar(nb[:, n % 4:n % 4 + 1], mr[:, n % 2:n % 2 + 1], -SCALE, None,
                                      ALU.mult).then_inc(biased, 1)

            def copy_group(n, i):
                b, nb_ = groups[n][i]
                c = before(n) + i
                dve.wait_ge(turned, c + 1)
                if c >= 4:
                    dve.wait_ge(used, c - 3)
                dve.tensor_copy(pt[:, c % 4, 0:nb_, :], tbank[c % 2][:, 0:nb_, :]).then_inc(t_copied, 1)

            def normalise(n):
                u, t, h = jobs[n]
                a = n % 4
                if u < A_PAIRS:
                    dve.wait_ge(sink_set, n + 1)
                    dve.wait_ge(expd, n + 1)
                    dve.tensor_tensor(den[:, a:a + 1], den[:, a:a + 1], sex[:, a:a + 1], ALU.add).then_inc(summed_a, 1)
                    dve.wait_ge(summed_a, n + 1)
                dve.reciprocal(rec[:, a:a + 1], den[:, a:a + 1]).then_inc(inverted, 1)
                dve.wait_ge(inverted, n + 1)
                dve.wait_ge(used, done_groups[n])
                m = n // 2
                if m >= 2:
                    dve.wait_ge(o_turned, m - 1)
                dve.tensor_scalar(on[:, m % 2, hp(h)], obank[n % 2][:, hp(h)], rec[:, a:a + 1], None, ALU.mult).then_inc(normed, 1)

            def copy_out(m):
                u, t, _ = jobs[2 * m]
                dve.wait_ge(o_turned, m + 1)
                if t == 0 and u >= 2:
                    dve.wait_ge(m_stored[u % 2], 16 * (u // 2))
                dve.tensor_copy(mo[u % 2][:, t * P:(t + 1) * P], xbank[:, :]).then_inc(o_copied, 1)

            for n, i in slots:
                if n < len(jobs) and i < len(groups[n]):
                    mask(n, i)
                    if i == len(groups[n]) - 1:
                        bias(n)
                if 0 <= n - LAG < len(jobs) and i < len(groups[n - LAG]):
                    copy_group(n - LAG, i)
                if i == 0 and 0 <= n - LAG - 1:
                    normalise(n - LAG - 1)
                if i == 0 and n - LAG >= 2 and (n - LAG) % 2 == 0:
                    copy_out((n - LAG) // 2 - 1)
            normalise(len(jobs) - 1)
            copy_out(len(jobs) // 2 - 1)


def strips():
    def strip(blocks, offset):
        dist = np.arange(P)[:, None] + (blocks - 1) * P - np.arange(blocks * P)[None, :]
        return offset(dist)
    return strip(2, offset_a).astype(np.float32), strip(TQ, offset_b).astype(np.float32)


def offset_a(dist):
    return np.where((dist >= 0) & (dist <= 128), 0.0, -1e30)


def offset_b(dist):
    count = sum(((dist >= 0) & (dist <= win) & (dist % d == 0)).astype(np.float64)
                for win, d in ((128, 1), (512, 4), (2048, 16)))
    return np.where(count > 0, np.log(np.maximum(count, 1)) / SCALE, -1e30)




NKC = 896
NKB = NKC + NQ
NTB = NKC // P
A_WIN = 128
NKA = A_WIN + NQ + 1


def sample_attention(nc, outer, projT, vtok, kbT, vb, kaT, va, mask_b, mask_a, sink_a, ident, mixT):
    RB, RA = 6 * NQ, 4 * NQ
    NBUF = 3
    with ExitStack() as ctx:
        s = Scope(nc, ctx, outer)
        qb = s.sb("p3_qb", [P, B_PAIRS, NS])
        kn = s.sb("p3_kn", [P, B_PAIRS, NS])
        qa = s.sb("p3_qa", [P, 2, NS])
        kna = s.sb("p3_kna", [P, NS])
        vn = s.sb("p3_vn", [NQ, NB, NV])
        qz = s.sb("p3_qz", [P, NB, B_PAIRS, RB])
        qza = s.sb("p3_qza", [P, NB, RA])
        kc = [s.sb(f"p3_kc{i}", [P, B_PAIRS, NKC]) for i in range(NBUF)]
        vc = [s.sb(f"p3_vc{i}", [P, NTB, 384]) for i in range(NBUF)]
        kca = s.sb("p3_kca", [P, NB, A_WIN])
        vca = s.sb("p3_vca", [P, NB, P])
        mb = s.sb("p3_mb", [RB, NKB])
        ma = s.sb("p3_ma", [RA, NB, NKA - 1])
        ska = s.sb("p3_ska", [RA, NB, 1])
        idt = s.sb("p3_ident", [P, P])
        rw = [s.sb(f"p3_row{i}", [RB, NKB]) for i in range(2)]
        pr = [s.sb(f"p3_prob{i}", [RB, NKB]) for i in range(2)]
        mx = s.sb("p3_mx", [RB, NB, 4])
        st = s.sb("p3_st", [RB, NB, 4])
        pt = [s.sb(f"p3_pt{i}", [P, NTB + 1, RB]) for i in range(2)]
        ra = s.sb("p3_ra", [RA, NB, NKA])
        sta = s.sb("p3_sta", [RA, 3, NB])
        pta = s.sb("p3_pta", [P, NB, RA])
        ptn = s.sb("p3_ptn", [NQ, NB, RA])
        mo = s.sb("p3_mo", [P, PAIRS, NS])
        sbank = [s.ps(f"p3_s{i}", [P, 512]) for i in range(4)]
        tbank = s.ps("p3_t", [P, NTB + 1, RB])
        obank = s.ps("p3_o", [P, B_PAIRS, 8])
        tabank = s.ps("p3_ta", [P, 2, NB, RA])
        oabank = s.ps("p3_oa", [P, NB, RA])
        c_in = s.sem("p3_c_in")
        a_in = s.sem("p3_a_in")
        cache_in = [s.sem(f"p3_cache_in{i}") for i in range(NBUF)]
        q_step = s.sem("p3_q_step")
        scored = s.sem("p3_scored")
        masked = s.sem("p3_masked")
        reduced = s.sem("p3_reduced")
        biased = s.sem("p3_biased")
        expd = s.sem("p3_expd")
        inverted = s.sem("p3_inverted")
        normed = s.sem("p3_normed")
        turned = s.sem("p3_turned")
        t_copied = s.sem("p3_t_copied")
        summed = s.sem("p3_summed")
        o_copied = s.sem("p3_o_copied")
        a_scored = s.sem("p3_a_scored")
        a_step = s.sem("p3_a_step")
        a_expd = s.sem("p3_a_expd")
        a_turned = s.sem("p3_a_turned")
        a_copied = s.sem("p3_a_copied")
        a_summed = s.sem("p3_a_summed")
        stored = s.sem("p3_stored")
        block = ctx.enter_context(nc.Block())
        half = lambda h: slice(HD * h, HD * h + HD)
        consts = ([(qa[half(u), h, :], projT[u, half(h), SEQ:T]) for u in range(2) for h in range(2)]
                  + [(qb[:, :, :], projT[3:6, :, SEQ:T].rearrange("u p t -> p u t")),
                     (kn[:, :, :], projT[6:9, :, SEQ:T].rearrange("u p t -> p u t")), (kna[:, :], projT[2, :, SEQ:T]),
                     (vn[:, :, :], vtok[SEQ:T, :].rearrange("(b q) c -> q b c", q=NQ)), (mb[:, :], mask_b),
                     (idt[:, :], ident)])
        consts_a = [(kca[:, :, :], kaT), (vca[:, :, :], va), (ma[:, :, :], mask_a), (ska[:, :, :], sink_a)]

        @block.sync
        def _(sp):
            for dst, src in consts:
                sp.dma_start(dst, src).then_inc(c_in, 16)
            for b in range(NB):
                if b == 2:
                    for dst, src in consts_a:
                        sp.dma_start(dst, src).then_inc(a_in, 16)
                if b >= NBUF:
                    sp.wait_ge(summed, b - NBUF + 1)
                sp.dma_start(kc[b % NBUF][:, :, :], kbT[b]).then_inc(cache_in[b % NBUF], 16)
                sp.dma_start(vc[b % NBUF][:, :, :], vb[b]).then_inc(cache_in[b % NBUF], 16)
            sp.wait_ge(o_copied, NB)
            sp.wait_ge(a_copied, 3)
            sp.dma_start(mixT[0:PAIRS, :, SEQ:T].rearrange("u p t -> p u t"), mo[:, :, :]).then_inc(stored, 16)
            sp.wait_ge(stored, 16)

        @block.tensor
        def _(pe):
            pe.wait_ge(c_in, 16 * len(consts))
            pe.wait_ge(q_step, 3)

            def scores(b):
                pe.wait_ge(cache_in[b % NBUF], 32 * (b // NBUF + 1))
                if b >= 2:
                    pe.wait_ge(masked, 2 * (b - 1))
                lo, hi = sbank[2 * (b % 2)], sbank[2 * (b % 2) + 1]
                for p in range(B_PAIRS):
                    pe.matmul(lo[0:RB, :], qz[:, b, p, :], kc[b % NBUF][:, p, 0:512], start=(p == 0), stop=(p == 2))
                for p in range(B_PAIRS):
                    pe.matmul(hi[0:RB, 0:NKC - 512], qz[:, b, p, :], kc[b % NBUF][:, p, 512:NKC], start=(p == 0), stop=(p == 2))
                for p in range(B_PAIRS):
                    mm = pe.matmul(hi[0:RB, NKC - 512:NKB - 512], qz[:, b, p, :], kn[:, p, NQ * b:NQ * (b + 1)],
                                   start=(p == 0), stop=(p == 2))
                mm.then_inc(scored, 1)

            def values(b):
                pe.wait_ge(normed, b + 1)
                if b:
                    pe.wait_ge(t_copied, b)
                for t in range(NTB):
                    pe.transpose(tbank[:, t, :], pr[b % 2][:, t * P:(t + 1) * P], idt[0:RB, 0:RB])
                pe.transpose(tbank[0:NQ, NTB, :], pr[b % 2][:, NKC:NKB], idt[0:RB, 0:RB]).then_inc(turned, 1)
                pe.wait_ge(t_copied, b + 1)
                if b:
                    pe.wait_ge(o_copied, b)
                for p in range(B_PAIRS):
                    for t in range(NTB):
                        pe.matmul(obank[:, p, :], vc[b % NBUF][:, t, p * P:(p + 1) * P], pt[b % 2][:, t, 8 * p:8 * p + 8],
                                  start=(t == 0), stop=False)
                    mm = pe.matmul(obank[:, p, :], vn[:, b, (p + 1) * P:(p + 2) * P], pt[b % 2][0:NQ, NTB, 8 * p:8 * p + 8],
                                   start=False, stop=True)
                mm.then_inc(summed, 1)

            scores(0)
            for b in range(NB):
                if b + 1 < NB:
                    scores(b + 1)
                values(b)
            pe.wait_ge(masked, 2 * NB)
            pe.wait_ge(a_in, 16 * len(consts_a))
            for b in range(NB):
                o = sbank[b // 2][0:RA, (b % 2) * 256:(b % 2) * 256 + NKA - 1]
                pe.matmul(o[:, 0:A_WIN], qza[:, b, :], kca[:, b, :], start=True, stop=True)
                mm = pe.matmul(o[:, A_WIN:NKA - 1], qza[:, b, :], kna[:, NQ * b:NQ * (b + 1)], start=True, stop=True)
            mm.then_inc(a_scored, 1)
            pe.wait_ge(a_step, 6)
            for b in range(NB):
                pe.transpose(tabank[:, 0, b, :], ra[:, b, 0:A_WIN], idt[0:RA, 0:RA])
                tr = pe.transpose(tabank[0:NQ, 1, b, :], ra[:, b, A_WIN:NKA - 1], idt[0:RA, 0:RA])
            tr.then_inc(a_turned, 1)
            pe.wait_ge(a_copied, 2)
            for b in range(NB):
                pe.matmul(oabank[:, b, :], vca[:, b, :], pta[:, b, :], start=True, stop=False)
                mm = pe.matmul(oabank[:, b, :], vn[:, b, 0:P], ptn[:, b, :], start=False, stop=True)
            mm.then_inc(a_summed, 1)

        @block.scalar
        def _(act):
            for b in range(NB):
                act.wait_ge(biased, b + 1)
                if b >= 2:
                    act.wait_ge(turned, b - 1)
                act.activation(pr[b % 2][:, :], rw[b % 2][:, :], ACT.Exp, bias=st[:, b, 1:2], scale=SCALE,
                               accum_out=st[:, b, 2:3]).then_inc(expd, 1)
                act.wait_ge(turned, b + 1)
                if b >= 2:
                    act.wait_ge(summed, b - 1)
                act.activation(pt[b % 2][:, 0:NTB, :], tbank[:, 0:NTB, :], ACT.Copy)
                act.activation(pt[b % 2][0:NQ, NTB, :], tbank[0:NQ, NTB, :], ACT.Copy).then_inc(t_copied, 1)
            act.wait_ge(a_step, 3)
            act.activation(ra[:, :, :], ra[:, :, :], ACT.Exp, scale=SCALE).then_inc(a_expd, 1)

        @block.vector
        def _(dve):
            dve.memset(qz[:, :, :, :].rearrange("p a b c -> p (a b c)"), 0.0).then_inc(q_step, 1)
            dve.memset(qza[:, :, :].rearrange("p a b -> p (a b)"), 0.0).then_inc(q_step, 1)
            dve.wait_ge(q_step, 2)
            dve.wait_ge(c_in, 16 * len(consts))
            rows = lambda ap: ap.rearrange("p (b q) -> p b q", q=NQ)
            for h in range(2):
                for p in range(B_PAIRS):
                    c = 8 * p + NQ * h
                    dve.tensor_copy(qz[half(h), :, p, c:c + NQ], rows(qb[half(h), p, :]))
                for u in range(2):
                    c = 8 * u + NQ * h
                    i = dve.tensor_copy(qza[half(u), :, c:c + NQ], rows(qa[half(u), h, :]))
            i.then_inc(q_step, 1)

            def normalise(b):
                dve.wait_ge(expd, b + 1)
                dve.reciprocal(st[:, b, 3:4], st[:, b, 2:3]).then_inc(inverted, 1)
                dve.wait_ge(inverted, b + 1)
                dve.tensor_scalar(pr[b % 2][:, :], pr[b % 2][:, :], st[:, b, 3:4], None, ALU.mult).then_inc(normed, 1)

            def copy_out(b):
                dve.wait_ge(summed, b + 1)
                for h in range(2):
                    i = dve.tensor_copy(mo[half(h), A_PAIRS:PAIRS, NQ * b:NQ * (b + 1)],
                                        obank[half(h), :, NQ * h:NQ * (h + 1)])
                i.then_inc(o_copied, 1)

            def mask(b):
                dve.wait_ge(scored, b + 1)
                if b >= 2:
                    dve.wait_ge(expd, b - 1)
                for j, (c0, c1) in enumerate(((0, 512), (512, NKB))):
                    dve.tensor_tensor_reduce(rw[b % 2][:, c0:c1], sbank[2 * (b % 2) + j][0:RB, 0:c1 - c0], mb[:, c0:c1],
                                             1.0, -3.0e38, ALU.add, ALU.max, mx[:, b, j:j + 1]).then_inc(masked, 1)
                dve.wait_ge(masked, 2 * b + 2)
                dve.tensor_reduce(st[:, b, 0:1], mx[:, b, 0:2], AX.X, ALU.max).then_inc(reduced, 1)
                dve.wait_ge(reduced, b + 1)
                dve.tensor_scalar(st[:, b, 1:2], st[:, b, 0:1], -SCALE, None, ALU.mult).then_inc(biased, 1)

            mask(0)
            for b in range(NB):
                normalise(b)
                if b + 1 < NB:
                    mask(b + 1)
                copy_out(b)
            dve.wait_ge(a_in, 16 * len(consts_a))
            dve.wait_ge(a_scored, 1)
            for j in range(NB // 2):
                i = dve.tensor_tensor(ra[:, 2 * j:2 * j + 2, 0:NKA - 1],
                                      sbank[j][0:RA, :].rearrange("p (b k) -> p b k", b=2)[:, :, 0:NKA - 1],
                                      ma[:, 2 * j:2 * j + 2, :], ALU.add)
            dve.tensor_scalar(ra[:, :, NKA - 1:NKA], ska[:, :, :], 1.0 / SCALE, None, ALU.mult).then_inc(a_step, 1)
            dve.wait_ge(a_step, 1)
            dve.tensor_reduce(sta[:, 0, :], ra[:, :, :], AX.X, ALU.max).then_inc(a_step, 1)
            dve.wait_ge(a_step, 2)
            per_row = lambda k: sta[:, k, :].unsqueeze(2).broadcast_to([RA, NB, NKA])
            dve.tensor_tensor(ra[:, :, :], ra[:, :, :], per_row(0), ALU.subtract).then_inc(a_step, 1)
            dve.wait_ge(a_expd, 1)
            dve.tensor_reduce(sta[:, 1, :], ra[:, :, :], AX.X, ALU.add).then_inc(a_step, 1)
            dve.wait_ge(a_step, 4)
            dve.reciprocal(sta[:, 2, :], sta[:, 1, :]).then_inc(a_step, 1)
            dve.wait_ge(a_step, 5)
            dve.tensor_tensor(ra[:, :, :], ra[:, :, :], per_row(2), ALU.mult).then_inc(a_step, 1)
            dve.wait_ge(a_turned, 1)
            dve.tensor_copy(pta[:, :, :], tabank[:, 0, :, :]).then_inc(a_copied, 1)
            dve.tensor_copy(ptn[:, :, :], tabank[0:NQ, 1, :, :]).then_inc(a_copied, 1)
            dve.wait_ge(a_summed, 1)
            for u in range(2):
                for h in range(2):
                    c = 8 * u + NQ * h
                    i = dve.tensor_copy(rows(mo[half(h), u, :]), oabank[half(u), :, c:c + NQ])
            i.then_inc(a_copied, 1)


def sample_order():
    i = np.arange(2048)
    far = (i < 1536) & (i % 16 < NQ)
    return np.concatenate([i[far], i[i >= 1536], i[(i < 1536) & ~far]])


def sample_masks():
    qn = np.arange(NQ)[:, None]
    index = np.concatenate([sample_order()[:NKC], 2048 + np.arange(NQ)])
    mb = offset_b(2048 + qn - index[None, :])
    ma = offset_a(A_WIN + qn - np.arange(A_WIN + NQ)[None, :])
    return (np.tile(mb, (6, 1)).astype(np.float32),
            np.ascontiguousarray(np.broadcast_to(np.tile(ma, (4, 1))[:, None, :], (4 * NQ, NB, NKA - 1))).astype(np.float32))


NP3 = 3
NZ = 11
GN_EPS = 64e-5
DECAY = float(np.exp(-0.5))


class Steps:

    def __init__(self, sem):
        self.sem, self.number, self.count, self.rehearse = sem, {}, 0, True

    def done(self, instruction, name, seg):
        self.count += 1
        if self.rehearse:
            self.number[name, seg] = self.count
        else:
            assert self.number[name, seg] == self.count, (name, seg)
            instruction.then_inc(self.sem, 1)

    def wait(self, eng, name, seg):
        if not isinstance(eng, Rehearsal) and (name, seg) in self.number:
            eng.wait_ge(self.sem, self.number[name, seg])


class Rehearsal:

    def __getattr__(self, name):
        return lambda *a, **k: self


def rwkv(nc, outer, tag, sample, src, shift0, state0, cst, wts, mixT, col0, state_out):
    nb, nq = (NB, NQ) if sample else (1, 256)
    W = nb * nq
    C = NS if sample else 64
    nseg = 1 if sample else SEQ // W
    nch = W // C
    nc_ = 1 if sample else 2
    ngr = nch // nc_
    U = nc_ * NP3
    levels = [2] if sample else [2, 4, 8, 16, 32]
    parts = [slice(0, C), slice(HD, HD + C)] if sample else [slice(0, P)]
    half = lambda h: slice(HD * h, HD * h + HD)
    rows = lambda h: slice(HD * h, HD * h + C)
    with ExitStack() as ctx:
        s = Scope(nc, ctx, outer)
        n_ = lambda x: f"{tag}_{x}"
        z = s.sb(n_("z"), [P, NZ, nb, nq + 1])
        d = s.sb(n_("d"), [P, NZ, W])
        th = s.sb(n_("th"), [P, W])
        sg = s.sb(n_("sg"), [P, W])
        big = lambda x: s.sb(n_(x), [P, NP3, W])
        several = lambda x, n: [big(f"{x}{i}") for i in range(n)]
        NPAR = 1 if sample else 2
        lw, av, kk, tA, tB, cs, cp, Dp, Di, kp, yc, tC = map(
            big, ("lw", "av", "kk", "tA", "tB", "cs", "cp", "Dp", "Di", "kp", "yc", "tC"))
        De_, be_, ka_, bv_, y_ = (several(x, NPAR) for x in ("De", "be", "ka", "bv", "y"))
        gg_ = several("gg", 1 if sample else 3)
        zs_ = [s.sb(n_(f"zs{i}"), [P, NZ, W]) for i in range(NPAR)]
        ar_ = [s.sb(n_(f"ar{i}"), [P, NP3, nch, 2, C]) for i in range(NPAR)]
        sh0 = s.sb(n_("sh0"), [P, NZ, nb, 1]) if sample else None
        znew = s.sb(n_("znew"), [P, NZ, W]) if sample else None
        am = s.sb(n_("am"), [P, NP3, NB, C]) if sample else None
        vm = s.sb(n_("vm"), [P, NP3, NB, HD]) if sample else None
        um = s.sb(n_("um"), [P, NP3, NB, HD]) if sample else None
        par = s.sb(n_("par"), [P, 32])
        omka = s.sb(n_("omka"), [P, NP3])
        w2 = s.sb(n_("w2"), [P, 384])
        g2 = s.sb(n_("g2"), [P, 384])
        hones = s.sb(n_("hones"), [P, P])
        hmean = s.sb(n_("hmean"), [P, P])
        rko = s.sb(n_("rko"), [P, NP3, P])
        id64 = s.sb(n_("id64"), [P, HD])
        mAB = s.sb(n_("mAB"), [P, NP3, 2, C])
        mT1 = s.sb(n_("mT1"), [P, U, C])
        mM1 = s.sb(n_("mM1"), [P, U, C])
        idU = s.sb(n_("idU"), [P, U, C])
        mL = s.sb(n_("mL"), [P, len(levels), U, C])
        scm = s.sb(n_("scm"), [P, W])
        cc = s.sb(n_("cc"), [P, 1])
        rm = s.sb(n_("rm"), [P, NB]) if sample else None
        GA = s.sb(n_("GA"), [P, 2, nc_, NP3, 2, C])
        GB = s.sb(n_("GB"), [P, 2, nc_, NP3, 2, C])
        Tm = s.sb(n_("Tm"), [P, U, C])
        Tt = s.sb(n_("Tt"), [P, 2, U, C])
        Ys = s.sb(n_("Ys"), [P, U, C])
        ML = s.sb(n_("ML"), [P, len(levels), U, C])
        tok = s.sb(n_("tok"), [P, 2, 3, U, HD])
        rh = s.sb(n_("rh"), [P, NP3, HD])
        uu = s.sb(n_("uu"), [P, NP3, HD])
        NS0 = 1 if sample else 2
        S0 = s.sb(n_("S0"), [P, NS0, NP3, nb, HD])
        S1 = s.sb(n_("S1"), [P, NP3, nb, HD])
        pb = [s.ps(n_(f"pb{i}"), [P, 512]) for i in range(3)]
        q = [s.ps(n_(f"q{i}"), [P, 512]) for i in range(5)]
        c_in = s.sem(n_("c_in"))
        z_in = s.sem(n_("z_in"))
        shift_in = s.sem(n_("shift_in")) if sample else None
        stored = s.sem(n_("stored"))
        V = Steps(s.sem(n_("vector_step")))
        S = Steps(s.sem(n_("scalar_step")))
        E = Steps(s.sem(n_("tensor_step")))
        G = Steps(s.sem(n_("pool_step")))
        zeroed = s.sem(n_("zeroed"))
        MU, W0, A0, KK, KA, LNW, LNB, RK = 0, 11, 14, 17, 20, 23, 26, 29
        pv = lambda base, p, sl=slice(0, P): par[sl, base + p:base + p + 1]
        consts = [(par[:, :], cst["par"]), (w2[:, :], wts["w2"]), (g2[:, :], wts["g2"]), (hones[:, :], cst["hones"]),
                  (hmean[:, :], cst["hmean"]), (id64[:, :], cst["id64"]), (mAB[:, :, :, :], cst[tag + "AB"]),
                  (mT1[:, :, :], cst[tag + "T1"]), (mM1[:, :, :], cst[tag + "M1"]), (idU[:, :, :], cst[tag + "I"]),
                  (mL[:, :, :, :], cst[tag + "L"]), (scm[:, :], cst[tag + "scan"])]
        if sample:
            consts += [(rm[:, :], cst["rowmask"]), (S0[:, 0], state0)]
        bank = lambda i, n, w: q[i][:, 0:n * w].rearrange("p (u w) -> p u w", u=n)
        unit = lambda ap, g: ap[:, :, g * nc_ * C:(g + 1) * nc_ * C]
        hops = [] if sample else [(c, k) for c in range(nc_) for k in ("rhs", "u", "y")]
        LL = len(levels)
        PIECES = 10
        last_c = nc_ - 1

        def walk(levels_of, hop, prepare, finish, special):
            for i in range(PIECES):
                prepare(0, i)
            for G_ in range(nseg * ngr + 1):
                seg, g = divmod(G_, ngr)
                before_ = divmod(G_ - 1, ngr)
                left = [(*before_, c, k) for c, k in hops] if G_ else []

                def between(left=left):
                    if left:
                        hop(*left.pop(0))

                def after(l, seg=seg, g=g):
                    i = g * LL + l
                    if seg:
                        finish(seg - 1, i)
                    if seg + 1 < nseg:
                        prepare(seg + 1, i)

                if seg < nseg:
                    levels_of(seg, g, between, after)
                while left:
                    hop(*left.pop(0))
            special()
            for i in range(PIECES):
                finish(nseg - 1, i)

        def tensor_walk(e):
            W_ = lambda st, name, seg: st.wait(e, name, seg)

            def heads(n):
                return [(p, h) for p in range(n) for h in range(2)]

            def prepare(seg, i):
                zs = zs_[seg % NPAR]
                if i == 1:
                    W_(S, "tanh", seg); W_(V, "bv", seg - 1); W_(S, "sd", seg - 3)
                    for p in range(NP3):
                        mm = e.matmul(pb[p][:, 0:W], w2[0:64, p * P:(p + 1) * P], th[0:64, :], start=True, stop=True)
                    E.done(mm, "w_pre", seg)
                if i == 2:
                    W_(S, "lw", seg)
                    for p in range(NP3):
                        mm = e.matmul(pb[p][:, 0:W], w2[64:128, p * P:(p + 1) * P], zs[64:128, 9, :], start=True, stop=True)
                    E.done(mm, "a_pre", seg)
                if i == 3:
                    W_(S, "av", seg); W_(S, "sgate", seg)
                    for p in range(NP3):
                        mm = e.matmul(pb[p][:, 0:W], g2[:, p * P:(p + 1) * P], sg[:, :], start=True, stop=True)
                    E.done(mm, "g_pre", seg)
                if i == 4:
                    W_(S, "gg", seg); W_(V, "kk2", seg)
                    for p in range(NP3):
                        mm = e.matmul(pb[p][:, 0:W], hones[:, :], tC[:, p, :], start=True, stop=True)
                    E.done(mm, "kksum", seg)
                if i == 8:
                    W_(V, "ssmax", seg); W_(V, "rkp", seg); W_(S, "sd", seg - 2)
                    for p in range(NP3):
                        mm = e.matmul(pb[p][:, 0:W], rko[:, p, :], tA[:, p, :], start=True, stop=True)
                    E.done(mm, "bonus", seg)

            def finish(seg, i):
                if i == 5:
                    W_(S, ("y", nch - 1), seg); W_(V, "bv", seg); W_(V, "ssmax", seg + 2)
                    for p in range(NP3):
                        mm = e.matmul(pb[p][:, 0:W], hmean[:, :], y_[seg % NPAR][:, p, :], start=True, stop=True)
                    E.done(mm, "mean", seg)
                if i == 6:
                    W_(S, "ysq", seg); W_(V, "yc", seg)
                    for p in range(NP3):
                        mm = e.matmul(pb[p][:, 0:W], hmean[:, :], tB[:, p, :], start=True, stop=True)
                    E.done(mm, "var", seg)

            def previous(gc, seg):
                return (gc - 1, seg) if gc else (nch - 1, seg - 1)

            def hop(seg, g, c, k):
                gc = g * nc_ + c
                pc, ps = previous(gc, seg)
                pg = (seg * ngr + g) % 2
                ar = ar_[seg % NPAR]
                if k == "rhs":
                    W_(V, ("state", pc), ps); W_(S, ("y", pc), ps)
                    if seg == 0 and gc == 0:
                        e.wait_ge(zeroed, 2)
                    for p, h in heads(NP3):
                        o = q[3][rows(h), p * HD:(p + 1) * HD]
                        e.matmul(o, ar[half(h), p, gc, 0, :], S0[half(h), gc % 2, p, 0, :], start=True, stop=False)
                        mm = e.matmul(o, GB[rows(h), pg, c, p, 0, :], tok[rows(h), pg, 2, c * NP3 + p, :],
                                      start=False, stop=True)
                    E.done(mm, ("rhs", gc), seg)
                elif k == "u":
                    W_(S, ("rhs", gc), seg); W_(V, ("tt", g, LL - 1), seg); W_(V, ("state", pc), ps)
                    for p, h in heads(NP3):
                        mm = e.matmul(q[4][rows(h), p * HD:(p + 1) * HD], Tt[rows(h), pg, c * NP3 + p, :],
                                      rh[rows(h), p, :], start=True, stop=True)
                    E.done(mm, ("u", gc), seg)
                else:
                    W_(S, ("u", gc), seg)
                    for p, h in heads(NP3):
                        o = q[4][half(h), p * HD:(p + 1) * HD]
                        e.matmul(o, tok[rows(h), pg, 0, c * NP3 + p, :], uu[rows(h), p, :], start=True, stop=False)
                        mm = e.matmul(o, tok[rows(h), pg, 1, c * NP3 + p, :], tok[rows(h), pg, 2, c * NP3 + p, :],
                                      start=False, stop=True)
                    E.done(mm, ("s", gc), seg)
                    for p, h in heads(NP3):
                        o = q[3][half(h), p * C:(p + 1) * C]
                        e.matmul(o, S0[half(h), gc % 2, p, 0, :], ar[half(h), p, gc, 1, :], start=True, stop=False)
                        e.matmul(o, uu[rows(h), p, :], GA[rows(h), pg, c, p, 1, :], start=False, stop=False)
                        mm = e.matmul(o, tok[rows(h), pg, 2, c * NP3 + p, :], GB[rows(h), pg, c, p, 1, :],
                                      start=False, stop=True)
                    E.done(mm, ("y", gc), seg)

            def levels_of(seg, g, between, after):
                pg = (seg * ngr + g) % 2
                pgr, pse = (g - 1, seg) if g else (ngr - 1, seg - 1)
                ar, be, ka, zs = (x[seg % NPAR] for x in (ar_, be_, ka_, zs_))
                for name in ("rho", "alpha", "beta", "kappa"):
                    W_(V, name, seg)
                for c in range(nc_):
                    gc = g * nc_ + c
                    if c:
                        W_(V, ("gab", gc - 1), seg)
                    else:
                        W_(V, ("tt", pgr, LL - 1), pse); W_(V, ("t", pgr, LL - 2), pse)
                        W_(S, ("ys", pgr, LL - 1), pse)
                    for b, x in ((0, be), (1, ka)):
                        for p, h in heads(NP3):
                            mm = e.matmul(q[b][rows(h), p * 2 * C:(p + 1) * 2 * C], x[half(h), p, gc * C:(gc + 1) * C],
                                          ar[half(h), p, gc].rearrange("p a c -> p (a c)"), start=True, stop=True)
                    E.done(mm, ("gab", gc), seg)
                    if c == 0:
                        for c1 in range(nc_):
                            for p, h in heads(NP3):
                                u, gc1 = c1 * NP3 + p, g * nc_ + c1
                                mm = e.matmul(q[2][rows(h), u * C:(u + 1) * C], ar[half(h), p, gc1, 0, :],
                                              be[half(h), p, gc1 * C:(gc1 + 1) * C], start=True, stop=True)
                        E.done(mm, ("m", g), seg)
                for i, x in enumerate((be, ka, zs)):
                    if i == 0:
                        W_(V, ("T1", g), seg)
                    else:
                        W_(V, ("gab", g * nc_ + last_c), seg)
                    b = (2, 0, 1)[i]
                    for c1 in range(nc_):
                        for p, h in heads(NP3):
                            u = c1 * NP3 + p
                            f = x[half(h), p + (6 if i == 2 else 0), (g * nc_ + c1) * C:(g * nc_ + c1 + 1) * C]
                            mm = e.matmul(q[b][rows(h), u * HD:(u + 1) * HD], f, id64[half(h), :], start=True, stop=True)
                    E.done(mm, ("tok", g, i), seg)
                units = [(c * NP3 + p, h) for c in range(nc_) for p, h in heads(NP3)]
                col = lambda u: slice(u * C, (u + 1) * C)
                for l in range(LL):
                    if l:
                        W_(V, ("t", g, l - 1), seg)
                    else:
                        W_(S, ("tok", g, 1), seg); W_(G, ("tt2", g), seg); W_(V, ("T2", g), seg)
                    W_(G, ("ml", g, l), seg)
                    for u, h in units:
                        mm = e.matmul(q[0][rows(h), col(u)], ML[rows(h), l, u, :], Tm[rows(h), u, :], start=True, stop=True)
                    E.done(mm, ("yl", g, l), seg)
                    between()
                    W_(S, ("ys", g, l), seg)
                    if l:
                        W_(V, ("tt", g, l - 1), seg)
                    if l == 0:
                        W_(S, ("tok", g, 2), seg); W_(S, ("tok", g, 0), seg)
                    if l < LL - 1:
                        for u, h in units:
                            mm = e.matmul(q[1][rows(h), col(u)], Tt[rows(h), pg, u, :], Ys[rows(h), u, :], start=True, stop=True)
                        E.done(mm, ("dt", g, l), seg)
                    for u, h in units:
                        mm = e.matmul(q[2][rows(h), col(u)], Ys[rows(h), u, :], Tt[rows(h), pg, u, :], start=True, stop=True)
                    E.done(mm, ("dtt", g, l), seg)
                    after(l)

            def special():
                if not sample:
                    return
                ar = ar_[0]
                W_(V, "am", 0); W_(V, "vm", 0); W_(V, ("tt", 0, LL - 1), 0)
                for p, h in heads(NP3):
                    o = q[3][rows(h), p * HD:(p + 1) * HD]
                    for b in range(NB):
                        e.matmul(o, am[half(h), p, b, :], S0[half(h), 0, p, b, :], start=(b == 0), stop=False)
                    mm = e.matmul(o, GB[rows(h), 0, 0, p, 0, :], tok[rows(h), 0, 2, p, :], start=False, stop=True)
                E.done(mm, ("rhs", 0), 0)
                W_(S, ("rhs", 0), 0)
                for p, h in heads(NP3):
                    mm = e.matmul(q[4][rows(h), p * HD:(p + 1) * HD], Tt[rows(h), 0, p, :], rh[rows(h), p, :],
                                  start=True, stop=True)
                E.done(mm, ("u", 0), 0)
                W_(S, ("u", 0), 0); W_(V, "um", 0)
                for p, h in heads(NP3):
                    o = q[3][half(h), p * C:(p + 1) * C]
                    e.matmul(o, uu[rows(h), p, :], GA[rows(h), 0, 0, p, 1, :], start=True, stop=False)
                    e.matmul(o, tok[rows(h), 0, 2, p, :], GB[rows(h), 0, 0, p, 1, :], start=False, stop=False)
                    for b in range(NB):
                        mm = e.matmul(q[3][half(h), p * C + NQ * b:p * C + NQ * (b + 1)], S0[half(h), 0, p, b, :],
                                      ar[half(h), p, 0, 1, NQ * b:NQ * (b + 1)], start=False, stop=(b == NB - 1))
                E.done(mm, ("y", 0), 0)
                for p, h in heads(NP3):
                    o = q[p][half(h), 0:NB * HD]
                    e.matmul(o, tok[rows(h), 0, 0, p, :], um[rows(h), p].rearrange("p b v -> p (b v)"),
                             start=True, stop=False)
                    mm = e.matmul(o, tok[rows(h), 0, 1, p, :], vm[rows(h), p].rearrange("p b v -> p (b v)"),
                                  start=False, stop=True)
                E.done(mm, ("s", 0), 0)

            walk(levels_of, hop, prepare, finish, special)

        def scalar_walk(e):
            W_ = lambda st, name, seg: st.wait(e, name, seg)
            cols_ = lambda ap, c: ap[:, c * NP3:(c + 1) * NP3]

            def prepare(seg, i):
                zs, De, gg = zs_[seg % NPAR], De_[seg % NPAR], gg_[seg % len(gg_)]
                if i == 1:
                    W_(V, "mixed_w", seg); W_(E, "g_pre", seg - 1)
                    S.done(e.activation(th[0:64, :], zs[0:64, 9, :], ACT.Tanh), "tanh", seg)
                    S.done(e.activation(sg[:, :], zs[:, 10, :], ACT.Sigmoid), "sgate", seg)
                if i in (2, 3):
                    name, src_, dst, base = ((), (), ("lw", "w_pre", lw, W0), ("av", "a_pre", av, A0))[i]
                    W_(E, src_, seg)
                    if i == 2:
                        W_(V, "cprev", seg - 1)
                    else:
                        W_(V, "beta0", seg - 1)
                    for p in range(NP3):
                        a = e.activation(dst[:, p, :], pb[p][:, 0:W], ACT.Sigmoid, bias=pv(base, p))
                    S.done(a, name, seg)
                if i == 4:
                    W_(E, "g_pre", seg); W_(V, "out", seg - 3)
                    for p in range(NP3):
                        a = e.activation(gg[:, p, :], pb[p][:, 0:W], ACT.Copy)
                    S.done(a, "gg", seg)
                    W_(V, "cprev", seg); W_(V, ("state", nch - 1), seg - 2); W_(V, "kappa", seg - 1)
                    S.done(e.activation(De[:, :, :], cs[:, :, :], ACT.Exp, scale=-DECAY), "De", seg)
                    S.done(e.activation(Dp[:, :, :], cp[:, :, :], ACT.Exp, scale=-DECAY), "Dp", seg)
                    S.done(e.activation(Di[:, :, :], cs[:, :, :], ACT.Exp, scale=DECAY), "Di", seg)
                if i == 5:
                    W_(V, "ssmax", seg)
                    S.done(e.activation(tC[:, :, :], tC[:, :, :], ACT.Sqrt), "sroot", seg)

            def finish(seg, i):
                if i == 6:
                    W_(V, "yc", seg)
                    S.done(e.activation(tB[:, :, :], yc[:, :, :], ACT.Square), "ysq", seg)
                if i == 7:
                    W_(E, "var", seg)
                    for p in range(NP3):
                        a = e.activation(tB[:, p, :], pb[p][:, 0:W], ACT.Sqrt, bias=cc[:, 0:1])
                    S.done(a, "sd", seg)

            def hop(seg, g, c, k):
                gc = g * nc_ + c
                pc, ps = (gc - 1, seg) if gc else (nch - 1, seg - 1)
                W_(E, (k, gc), seg)
                if k == "rhs":
                    W_(E, ("u", pc), ps)
                    S.done(e.activation(rh[:, :, :], bank(3, NP3, HD), ACT.Copy), ("rhs", gc), seg)
                elif k == "u":
                    W_(E, ("y", pc), ps)
                    S.done(e.activation(uu[:, :, :], bank(4, NP3, HD), ACT.Copy), ("u", gc), seg)
                else:
                    W_(V, "yc", seg - 2)
                    S.done(e.activation(y_[seg % NPAR][:, :, gc * C:(gc + 1) * C], bank(3, NP3, C), ACT.Copy), ("y", gc), seg)

            def levels_of(seg, g, between, after):
                pg = (seg * ngr + g) % 2
                for i, b in enumerate((2, 0, 1)):
                    W_(E, ("tok", g, i), seg)
                    for sl in parts:
                        a = e.activation(tok[sl, pg, i], q[b][sl, 0:U * HD].rearrange("p (u w) -> p u w", u=U), ACT.Copy)
                    S.done(a, ("tok", g, i), seg)
                for l in range(LL):
                    W_(E, ("yl", g, l), seg)
                    if l:
                        W_(E, ("dtt", g, l - 1), seg)
                    for sl in parts:
                        a = e.activation(Ys[sl], q[0][sl, 0:U * C].rearrange("p (u w) -> p u w", u=U), ACT.Copy)
                    S.done(a, ("ys", g, l), seg)
                    between()
                    after(l)

            def special():
                if not sample:
                    return
                W_(E, ("rhs", 0), 0)
                for sl in parts:
                    a = e.activation(rh[sl], q[3][sl, 0:NP3 * HD].rearrange("p (u w) -> p u w", u=NP3), ACT.Copy)
                S.done(a, ("rhs", 0), 0)
                W_(E, ("u", 0), 0)
                for sl in parts:
                    a = e.activation(uu[sl], q[4][sl, 0:NP3 * HD].rearrange("p (u w) -> p u w", u=NP3), ACT.Copy)
                S.done(a, ("u", 0), 0)
                W_(E, ("y", 0), 0)
                S.done(e.activation(y_[0][:, :, 0:C], bank(3, NP3, C), ACT.Copy), ("y", 0), 0)

            walk(levels_of, hop, prepare, finish, special)

        def vector_walk(e):
            W_ = lambda st, name, seg: st.wait(e, name, seg)
            f4 = lambda ap: ap.rearrange("p (b q) -> p b q", b=nb)
            ct = lambda ap: ap.rearrange("p (c t) -> p c t", t=C)

            def prepare(seg, i):
                zs, De, be, ka, bv, ar = (x[seg % NPAR] for x in (zs_, De_, be_, ka_, bv_, ar_))
                own = lambda name: W_(V, name, seg)
                if i == 0:
                    e.wait_ge(z_in, 16 * (seg + 1))
                    if sample:
                        e.wait_ge(shift_in, 16)
                        e.tensor_copy(z[:, :, :, 0:1], sh0[:, :, :, :])
                        V.done(e.tensor_copy(z[:, :, :, 1:nq + 1], znew[:, :, :].rearrange("p z (b q) -> p z b q", b=nb)), "z", seg)
                        own("z")
                    V.done(e.tensor_tensor(d[:, :, :].rearrange("p z (b q) -> p z b q", b=nb) if sample else d[:, :, :],
                                           z[:, :, :, 0:nq] if sample else z[:, :, 0, 0:nq],
                                           z[:, :, :, 1:nq + 1] if sample else z[:, :, 0, 1:nq + 1], ALU.subtract), "shift", seg)
                    own("shift")
                    W_(E, "a_pre", seg - 2); W_(S, "sgate", seg - 2); W_(E, ("tok", ngr - 1, 2), seg - 2)
                for name, blocks in {0: (("mixed_w", range(9, NZ)),), 1: (("mixed", range(9)),)}.get(i, ()):
                    for b in blocks:
                        i_ = e.scalar_tensor_tensor(out=f4(zs[:, b, :]), in0=f4(d[:, b, :]), scalar=par[:, MU + b:MU + b + 1],
                                                    in1=z[:, b, :, 1:nq + 1], op0=ALU.mult, op1=ALU.add)
                    V.done(i_, name, seg)
                if i == 1:
                    own("mixed")
                    V.done(e.tensor_copy(z[:, :, 0, 0:1], z[:, :, 0, nq:nq + 1]), "carry", seg)
                if i == 2:
                    for p in range(NP3):
                        i_ = e.tensor_scalar(kk[:, p, :], zs[:, 3 + p, :], pv(KK, p), None, ALU.mult)
                    V.done(i_, "kk", seg)
                    own("kk")
                    V.done(e.tensor_tensor(tC[:, :, :], kk[:, :, :], kk[:, :, :], ALU.mult), "kk2", seg)
                if i == 3:
                    W_(S, "lw", seg); W_(S, "Di", seg - 1)
                    for p in range(NP3):
                        i_ = e.tensor_tensor_scan(cs[:, p, :], scm[:, :], lw[:, p, :], 0.0, ALU.mult, ALU.add)
                    V.done(i_, "scan", seg)
                    own("scan")
                    V.done(e.tensor_tensor(cp[:, :, :], cs[:, :, :], lw[:, :, :], ALU.subtract), "cprev", seg)
                if i == 4:
                    W_(S, "av", seg); W_(E, "bonus", seg - 1)
                    for p in range(NP3):
                        i_ = e.tensor_scalar(tA[:, p, :], av[:, p, :], pv(KA, p), omka[:, p:p + 1], ALU.mult, ALU.add)
                    V.done(i_, "kscale", seg)
                    own("kscale")
                    V.done(e.tensor_tensor(kp[:, :, :], zs[:, 3:6, :], tA[:, :, :], ALU.mult), "kp", seg)
                if i == 5:
                    W_(E, "kksum", seg)
                    for p in range(NP3):
                        i_ = e.tensor_scalar(tC[:, p, :], pb[p][:, 0:W], 1e-24, None, ALU.max)
                    V.done(i_, "ssmax", seg)
                    own("kp")
                    V.done(e.tensor_tensor(tA[:, :, :], kp[:, :, :], zs[:, 0:3, :], ALU.mult), "rkp", seg)
                if i == 6:
                    W_(S, "sroot", seg)
                    V.done(e.reciprocal(tC[:, :, :], tC[:, :, :]), "sinv", seg)
                if i == 7:
                    own("sinv")
                    V.done(e.tensor_tensor(kk[:, :, :], kk[:, :, :], tC[:, :, :], ALU.mult), "kkn", seg)
                    W_(S, "Di", seg); own("kkn")
                    W_(E, ("y", nch - 1), seg - 2)
                    for p in range(NP3):
                        i_ = e.tensor_tensor(ar[:, p, :, 0, :], ct(Dp[:, p, :]), ct(kk[:, p, :]), ALU.mult)
                    V.done(i_, "alpha", seg)
                    for p in range(NP3):
                        i_ = e.tensor_tensor(ar[:, p, :, 1, :], ct(De[:, p, :]), ct(zs[:, p, :]), ALU.mult)
                    V.done(i_, "rho", seg)
                    V.done(e.scalar_tensor_tensor(out=be[:, :, :], in0=kk[:, :, :], scalar=-1.0, in1=av[:, :, :],
                                                  op0=ALU.mult, op1=ALU.mult), "beta0", seg)
                if i == 9:
                    own("beta0")
                    V.done(e.tensor_tensor(be[:, :, :], be[:, :, :], Di[:, :, :], ALU.mult), "beta", seg)
                    V.done(e.tensor_tensor(ka[:, :, :], kp[:, :, :], Di[:, :, :], ALU.mult), "kappa", seg)
                    W_(E, "bonus", seg)
                    for p in range(NP3):
                        i_ = e.tensor_tensor(bv[:, p, :], zs[:, 6 + p, :], pb[p][:, 0:W], ALU.mult)
                    V.done(i_, "bv", seg)

            def finish(seg, i):
                own = lambda name: W_(V, name, seg)
                if i == 6:
                    W_(E, "mean", seg)
                    if seg:
                        e.wait_ge(stored, 16 * seg)
                    for p in range(NP3):
                        i_ = e.tensor_tensor(yc[:, p, :], y_[seg % NPAR][:, p, :], pb[p][:, 0:W], ALU.subtract)
                    V.done(i_, "yc", seg)
                if i == 8:
                    W_(S, "sd", seg)
                    V.done(e.reciprocal(tB[:, :, :], tB[:, :, :]), "rsd", seg)
                    own("rsd")
                    V.done(e.tensor_tensor(yc[:, :, :], yc[:, :, :], tB[:, :, :], ALU.mult), "yn", seg)
                if i == 9:
                    own("yn")
                    for p in range(NP3):
                        i_ = e.tensor_scalar(yc[:, p, :], yc[:, p, :], pv(LNW, p), pv(LNB, p), ALU.mult, ALU.add)
                    V.done(i_, "ln", seg)
                    own("ln")
                    V.done(e.tensor_tensor(yc[:, :, :], yc[:, :, :], bv_[seg % NPAR][:, :, :], ALU.add), "plus", seg)
                    own("plus")
                    V.done(e.tensor_tensor(yc[:, :, :], yc[:, :, :], gg_[seg % len(gg_)][:, :, :], ALU.mult), "out", seg)

            def hop(seg, g, c, k):
                if k != "y":
                    return
                gc = g * nc_ + c
                pc, ps = (gc - 1, seg) if gc else (nch - 1, seg - 1)
                W_(E, ("s", gc), seg); W_(V, ("state", pc), ps)
                V.done(e.tensor_tensor(S1[:, :, 0, :], S0[:, gc % 2, :, 0, :], bank(4, NP3, HD), ALU.add), ("sum", gc), seg)
                W_(V, ("sum", gc), seg); W_(E, ("y", pc), ps)
                for p in range(NP3):
                    i_ = e.tensor_scalar(S0[:, (gc + 1) % 2, p, 0, :], S1[:, p, 0, :],
                                         De_[seg % NPAR][:, p, gc * C + C - 1:gc * C + C], None, ALU.mult)
                V.done(i_, ("state", gc), seg)

            def levels_of(seg, g, between, after):
                G_ = seg * ngr + g
                pg = G_ % 2
                pgr, pse = (g - 1, seg) if g else (ngr - 1, seg - 1)
                old = divmod(G_ - 2, ngr)
                for c in range(nc_):
                    gc = g * nc_ + c
                    W_(E, ("gab", gc), seg)
                    if c == 0:
                        W_(E, ("y", old[1] * nc_ + last_c), old[0]); W_(G, ("ml", pgr, LL - 1), pse)
                    for sl in parts:
                        for i_, GX in enumerate((GA, GB)):
                            i = e.tensor_tensor(GX[sl, pg, c].rearrange("p a b c -> p (a b c)"), q[i_][sl, 0:NP3 * 2 * C],
                                                mAB[sl].rearrange("p a b c -> p (a b c)"), ALU.mult)
                    V.done(i, ("gab", gc), seg)
                    if c == 0:
                        W_(E, ("m", g), seg); W_(E, ("yl", pgr, LL - 1), pse)
                        for sl in parts:
                            i = e.tensor_tensor(Tm[sl], q[2][sl, 0:U * C].rearrange("p (u w) -> p u w", u=U), mT1[sl], ALU.mult)
                        V.done(i, ("T1", g), seg)
                        W_(V, ("T1", g), seg)
                        for sl in parts:
                            i = e.tensor_tensor(Tm[sl], Tm[sl], idU[sl], ALU.add)
                        V.done(i, ("T2", g), seg)
                W_(G, ("tt2", g), seg)
                of = lambda b, sl: q[b][sl, 0:U * C].rearrange("p (u w) -> p u w", u=U)
                for l in range(LL):
                    if l < LL - 1:
                        W_(E, ("dt", g, l), seg)
                        W_(V, ("t", g, l - 1) if l else ("T2", g), seg)
                        for sl in parts:
                            i = e.tensor_tensor(Tm[sl], Tm[sl], of(1, sl), ALU.add)
                        V.done(i, ("t", g, l), seg)
                    W_(E, ("dtt", g, l), seg)
                    if l:
                        W_(V, ("tt", g, l - 1), seg)
                    for sl in parts:
                        i = e.tensor_tensor(Tt[sl, pg], Tt[sl, pg], of(2, sl), ALU.add)
                    V.done(i, ("tt", g, l), seg)
                    between()
                    after(l)

            def special():
                if not sample:
                    return
                ar, De = ar_[0], De_[0]
                e.wait_ge(zeroed, 2)
                for b in range(NB):
                    i = e.tensor_copy(am[:, :, b, NQ * b:NQ * (b + 1)], ar[:, :, 0, 0, NQ * b:NQ * (b + 1)])
                V.done(i, "am", 0)
                W_(S, ("tok", 0, 2), 0)
                for name, dst in (("vm", vm), ("um", um)):
                    if name == "um":
                        W_(S, ("u", 0), 0)
                    for sl in parts:
                        for p in range(NP3):
                            rv = tok[sl, 0, 2, p, :] if name == "vm" else uu[sl, p, :]
                            n = sl.stop - sl.start
                            i = e.tensor_tensor(dst[sl, p], rv.unsqueeze(1).broadcast_to([n, NB, HD]),
                                                rm[sl].unsqueeze(2).broadcast_to([n, NB, HD]), ALU.mult)
                    V.done(i, name, 0)
                W_(E, ("s", 0), 0)
                for p in range(NP3):
                    i = e.tensor_tensor(S1[:, p], S0[:, 0, p], q[p][:, :].rearrange("p (b v) -> p b v", b=NB), ALU.add)
                V.done(i, "sum", 0)
                W_(V, "sum", 0)
                for p in range(NP3):
                    last_d = De[:, p, :].rearrange("p (b q) -> p b q", b=NB)[:, :, NQ - 1:NQ]
                    i = e.tensor_tensor(S1[:, p], S1[:, p], last_d.broadcast_to([P, NB, HD]), ALU.mult)
                V.done(i, ("state", 0), 0)

            walk(levels_of, hop, prepare, finish, special)

        def pool_walk(e):
            W_ = lambda st, name, seg: st.wait(e, name, seg)
            nothing = lambda *a: None

            def levels_of(seg, g, between, after):
                G_ = seg * ngr + g
                pg = G_ % 2
                pgr, pse = (g - 1, seg) if g else (ngr - 1, seg - 1)
                old = divmod(G_ - 2, ngr)
                W_(V, ("gab", g * nc_ + last_c), seg)
                W_(E, ("u", old[1] * nc_ + last_c), old[0])
                mt = lambda sl, c: GA[sl, pg, c, :, 0, :]
                for sl in parts:
                    for c in range(nc_):
                        i = e.tensor_tensor(Tt[sl, pg, c * NP3:(c + 1) * NP3], mt(sl, c), mM1[sl, c * NP3:(c + 1) * NP3], ALU.mult)
                G.done(i, ("tt1", g), seg)
                W_(G, ("tt1", g), seg)
                for sl in parts:
                    i = e.tensor_tensor(Tt[sl, pg], Tt[sl, pg], idU[sl], ALU.add)
                G.done(i, ("tt2", g), seg)
                for l in range(LL):
                    W_(E, ("yl", pgr, l), pse)
                    for sl in parts:
                        for c in range(nc_):
                            i = e.tensor_tensor(ML[sl, l, c * NP3:(c + 1) * NP3], mt(sl, c), mL[sl, l, c * NP3:(c + 1) * NP3], ALU.mult)
                    G.done(i, ("ml", g, l), seg)

            walk(levels_of, nothing, nothing, nothing, nothing)

        walks = ((tensor_walk, E), (scalar_walk, S), (vector_walk, V), (pool_walk, G))
        for program, steps in walks:
            program(Rehearsal())
        for _, steps in walks:
            steps.rehearse, steps.count = False, 0
        block = ctx.enter_context(nc.Block())

        @block.sync
        def _(sp):
            def store(seg):
                V.wait(sp, "out", seg)
                sp.dma_start(mixT[:, :, col0 + W * seg:col0 + W * (seg + 1)].rearrange("k p t -> p k t"), yc[:, :, :]).then_inc(stored, 16)

            if sample:
                sp.dma_start(znew[:, :, :], src[:, :, SEQ:T].rearrange("z p t -> p z t")).then_inc(z_in, 16)
                sp.dma_start(sh0[:, :, :, :], shift0).then_inc(shift_in, 16)
            else:
                sp.dma_start(z[:, :, 0, 1:nq + 1], src[:, :, 0:W].rearrange("z p t -> p z t")).then_inc(z_in, 16)
            for dst, src_ in consts:
                sp.dma_start(dst, src_).then_inc(c_in, 16)
            for seg in range(nseg):
                if seg:
                    V.wait(sp, "carry", seg - 1)
                    sp.dma_start(z[:, :, 0, 1:nq + 1], src[:, :, W * seg:W * (seg + 1)].rearrange("z p t -> p z t")).then_inc(z_in, 16)
                if seg > 1:
                    store(seg - 2)
            for seg in range(max(nseg - 2, 0), nseg):
                store(seg)
            V.wait(sp, ("state", nch - 1), nseg - 1)
            sp.dma_start(state_out, S1[:, :, :, :] if sample else S0[:, nch % 2]).then_inc(stored, 16)
            sp.wait_ge(stored, 16 * (nseg + 1))

        @block.tensor
        def _(pe):
            pe.wait_ge(c_in, 16 * len(consts))
            pe.wait_ge(zeroed, 1)
            tensor_walk(pe)

        @block.scalar
        def _(act):
            act.wait_ge(c_in, 16 * len(consts))
            act.wait_ge(zeroed, 1)
            scalar_walk(act)

        @block.vector
        def _(dve):
            dve.wait_ge(c_in, 16 * len(consts))
            dve.memset(cc[:, 0:1], GN_EPS)
            if not sample:
                dve.memset(z[:, :, 0, 0:1], 0.0)
            dve.tensor_scalar(omka[:, :], par[:, KA:KA + 3], -1.0, 1.0, ALU.mult, ALU.add)
            for p in range(NP3):
                i = dve.tensor_scalar(rko[:, p, :], hones[:, :], pv(RK, p), None, ALU.mult)
            i.then_inc(zeroed, 1)
            dve.wait_ge(zeroed, 1)
            if sample:
                dve.memset(am[:, :, :, :].rearrange("p a b c -> p (a b c)"), 0.0).then_inc(zeroed, 1)
            else:
                dve.memset(S0[:, 0].rearrange("p a b v -> p (a b v)"), 0.0).then_inc(zeroed, 1)
            vector_walk(dve)

        @block.gpsimd
        def _(pool):
            pool.wait_ge(c_in, 16 * len(consts))
            pool_walk(pool)


def rwkv_constants():
    out = {}
    for tag, C, group, U, levels, W in (("cp", 64, 64, 6, [2, 4, 8, 16, 32], 256), ("cs", NS, NQ, 3, [2], NS)):
        i = np.arange(P)[:, None] % HD
        j = np.arange(C)[None, :]
        live = (i < C) & (i // group == j // group)
        below = lambda a, b, n: (a // (2 * n) == b // (2 * n)) & (a // n % 2 == 0) & (b // n % 2 == 1)
        tile = lambda m, *dims: np.ascontiguousarray(np.broadcast_to(
            m.astype(np.float32).reshape((P,) + (1,) * len(dims) + m.shape[1:]), (P,) + dims + m.shape[1:]))
        out[tag + "AB"] = tile(np.stack([live & (i < j), live & (i <= j)], 1), NP3)
        out[tag + "M1"] = tile(live & below(i, j, 1), U)
        out[tag + "T1"] = tile(live & below(j, i, 1), U)
        out[tag + "I"] = tile(i == j, U)
        out[tag + "L"] = np.stack([tile(live & below(i, j, n), U) for n in levels], 1)
        out[tag + "scan"] = tile(np.arange(W)[None] % group != 0 + 0 * np.arange(P)[:, None])
    same = (np.arange(P)[:, None] // HD == np.arange(P)[None, :] // HD).astype(np.float32)
    out["hones"], out["hmean"] = same, same / HD
    out["id64"] = (np.arange(P)[:, None] % HD == np.arange(HD)[None, :]).astype(np.float32)
    out["rowmask"] = (np.arange(P)[:, None] % HD // NQ == np.arange(NB)[None, :]).astype(np.float32)
    return out


def out_project(nc, outer, mixT, xtok, w_o, g2, ident, x2, h2T):
    NT = SEQ // P + 1
    tiles = [(P * i, P) for i in range(SEQ // P)] + [(SEQ, NS)]
    with ExitStack() as ctx:
        s = Scope(nc, ctx, outer)
        WP = 2
        wr = [s.sb(f"p5_wr{i}", [P, KC // WP, D]) for i in range(WP)]
        wh = s.sb("p5_wh", [P, KC, D], F32R)
        wl = s.sb("p5_wl", [P, KC, D], F32R)
        g = s.sb("p5_g", [P, KC])
        idt = s.sb("p5_ident", [P, P])
        eps = s.sb("p5_eps", [P, 1])
        m = [s.sb(f"p5_mix{i}", [P, KC, P]) for i in range(2)]
        mh = [s.sb(f"p5_mh{i}", [P, KC, P], F32R) for i in range(2)]
        ml = [s.sb(f"p5_ml{i}", [P, KC, P], F32R) for i in range(2)]
        xt = [s.sb(f"p5_x{i}", [P, D]) for i in range(2)]
        junk = s.sb("p5_junk", [P, D])
        xn = [s.sb(f"p5_xn{i}", [P, D]) for i in range(2)]
        st = s.sb("p5_stat", [P, 4, 2])
        ht = [s.sb(f"p5_h{i}", [P, KC, P]) for i in range(2)]
        acc = [[s.ps(f"p5_acc{i}{h}", [P, 512]) for h in range(2)] for i in range(2)]
        tp = [s.ps(f"p5_tp{h}", [P, 4, P]) for h in range(2)]
        consts_in = s.sem("p5_consts_in")
        eps_set = s.sem("p5_eps_set")
        w_in = [s.sem(f"p5_w_in{i}") for i in range(WP)]
        w_high = s.sem("p5_w_high")
        w_low = s.sem("p5_w_low")
        mix_in = [s.sem(f"p5_mix_in{i}") for i in range(2)]
        x_in = [s.sem(f"p5_x_in{i}") for i in range(2)]
        m_high = s.sem("p5_m_high")
        m_low = s.sem("p5_m_low")
        producted = s.sem("p5_producted")
        added = s.sem("p5_added")
        stat_step = s.sem("p5_stat_step")
        inverted = s.sem("p5_inverted")
        scaled = s.sem("p5_scaled")
        turned = s.sem("p5_turned")
        h_out = s.sem("p5_h_out")
        x_stored = [s.sem(f"p5_x_stored{i}") for i in range(2)]
        h_stored = [s.sem(f"p5_h_stored{i}") for i in range(2)]
        block = ctx.enter_context(nc.Block())

        @block.sync
        def _(sp):
            def load_mix(t):
                r0, n = tiles[t]
                if t >= 2:
                    sp.wait_ge(m_low, t - 1)
                sp.dma_start(m[t % 2][:, :, 0:n], mixT[:, :, r0:r0 + n].rearrange("k p n -> p k n")).then_inc(mix_in[t % 2], 16)

            def load_x(t):
                r0, n = tiles[t]
                if t >= 2:
                    sp.wait_ge(scaled, t - 1)
                    sp.wait_ge(x_stored[t % 2], 16 * (t // 2))
                sp.dma_start(xt[t % 2][0:n, :], xtok[r0:r0 + n, :]).then_inc(x_in[t % 2], 16)

            load_mix(0)
            for i in range(WP):
                sp.dma_start(wr[i][:, :, :], w_o[:, i * KC // WP:(i + 1) * KC // WP, :]).then_inc(w_in[i], 16)
            load_mix(1)
            load_x(0)
            load_x(1)
            sp.dma_start(g[:, :], g2).then_inc(consts_in, 16)
            sp.dma_start(idt[:, :], ident).then_inc(consts_in, 16)
            load_mix(2)
            for t, (r0, n) in enumerate(tiles):
                sp.wait_ge(added, t + 1)
                sp.dma_start(x2[r0:r0 + n, :], xt[t % 2][0:n, :]).then_inc(x_stored[t % 2], 16)
                if t + 2 < NT:
                    load_x(t + 2)
                if t + 3 < NT:
                    load_mix(t + 3)
                sp.wait_ge(h_out, t + 1)
                sp.dma_start(h2T[:, :, r0:r0 + n].rearrange("k p n -> p k n"), ht[t % 2][:, :, 0:n]).then_inc(h_stored[t % 2], 16)
            for j in range(2):
                sp.wait_ge(x_stored[j], 16 * ((NT + 1 - j) // 2))
                sp.wait_ge(h_stored[j], 16 * ((NT + 1 - j) // 2))

        @block.tensor
        def _(pe):
            def turn(t):
                if t == 0:
                    pe.wait_ge(consts_in, 32)
                n = tiles[t][1]
                pe.wait_ge(scaled, t + 1)
                if t:
                    pe.wait_ge(h_out, t)
                for k in range(KC):
                    tr = pe.transpose(tp[k // 4][:, k % 4, 0:n], xn[t % 2][0:n, k * P:(k + 1) * P], idt[0:n, 0:n])
                tr.then_inc(turned, 1)

            for t, (r0, n) in enumerate(tiles):
                pe.wait_ge(m_low, t + 1)
                if t >= 2:
                    pe.wait_ge(added, t - 1)
                for h in range(2):
                    for k in range(KC):
                        if t == 0 and h == 0 and k % (KC // WP) == 0:
                            pe.wait_ge(w_low, k * WP // KC + 1)
                        o, cols = acc[t % 2][h][0:n, :], slice(h * 512, (h + 1) * 512)
                        high, low = mh[t % 2][:, k, 0:n], ml[t % 2][:, k, 0:n]
                        pe.matmul(o, high, wh[:, k, cols], start=(k == 0), stop=False)
                        pe.matmul(o, high, wl[:, k, cols], start=False, stop=False)
                        mm = pe.matmul(o, low, wh[:, k, cols], start=False, stop=(k == KC - 1))
                mm.then_inc(producted, 1)
                if t:
                    turn(t - 1)
            turn(NT - 1)

        @block.scalar
        def _(act):
            def high_m(t):
                n = tiles[t][1]
                act.wait_ge(mix_in[t % 2], 16 * (t // 2 + 1))
                if t >= 2:
                    act.wait_ge(producted, t - 1)
                act.activation(mh[t % 2][:, :, 0:n], m[t % 2][:, :, 0:n], ACT.Copy).then_inc(m_high, 1)

            act.wait_ge(eps_set, 1)
            high_m(0)
            for i in range(WP):
                act.wait_ge(w_in[i], 16)
                act.activation(wh[:, i * KC // WP:(i + 1) * KC // WP, :], wr[i][:, :, :], ACT.Copy).then_inc(w_high, 1)
            high_m(1)
            for t, (r0, n) in enumerate(tiles):
                if t + 1 < NT and t:
                    high_m(t + 1)
                act.wait_ge(added, t + 1)
                act.activation(junk[0:n, :], xt[t % 2][0:n, :], ACT.Square,
                               accum_out=st[0:n, 0, t % 2:t % 2 + 1]).then_inc(stat_step, 1)
                act.wait_ge(stat_step, 2 * t + 1)
                act.activation(st[0:n, 1, t % 2:t % 2 + 1], st[0:n, 0, t % 2:t % 2 + 1], ACT.Sqrt,
                               bias=eps[0:n, 0:1], scale=1.0 / D).then_inc(stat_step, 1)
                act.wait_ge(inverted, t + 1)
                if t >= 2:
                    act.wait_ge(turned, t - 1)
                act.activation(xn[t % 2][0:n, :], xt[t % 2][0:n, :], ACT.Copy,
                               scale=st[0:n, 2, t % 2:t % 2 + 1]).then_inc(scaled, 1)

        @block.vector
        def _(dve):
            dve.memset(eps[:, :], EPS).then_inc(eps_set, 1)
            def low_m(t):
                n = tiles[t][1]
                dve.wait_ge(m_high, t + 1)
                dve.tensor_tensor(ml[t % 2][:, :, 0:n], m[t % 2][:, :, 0:n], mh[t % 2][:, :, 0:n].bitcast(F32),
                                  ALU.subtract).then_inc(m_low, 1)

            low_m(0)
            for i in range(WP):
                dve.wait_ge(w_high, i + 1)
                ks = slice(i * KC // WP, (i + 1) * KC // WP)
                dve.tensor_tensor(wl[:, ks, :], wr[i][:, :, :], wh[:, ks, :].bitcast(F32), ALU.subtract).then_inc(w_low, 1)
            low_m(1)
            dve.wait_ge(consts_in, 32)

            def copy_out(t):
                n = tiles[t][1]
                dve.wait_ge(turned, t + 1)
                if t >= 2:
                    dve.wait_ge(h_stored[t % 2], 16 * (t // 2))
                for k in range(KC):
                    c = dve.tensor_scalar(ht[t % 2][:, k, 0:n], tp[k // 4][:, k % 4, 0:n], g[:, k:k + 1], None, ALU.mult)
                c.then_inc(h_out, 1)

            for t, (r0, n) in enumerate(tiles):
                if t + 1 < NT and t:
                    low_m(t + 1)
                dve.wait_ge(producted, t + 1)
                dve.wait_ge(x_in[t % 2], 16 * (t // 2 + 1))
                for h in range(2):
                    xs = xt[t % 2][0:n, h * 512:(h + 1) * 512]
                    a = dve.tensor_tensor(xs, xs, acc[t % 2][h][0:n, :], ALU.add)
                a.then_inc(added, 1)
                dve.wait_ge(stat_step, 2 * t + 2)
                dve.reciprocal(st[0:n, 2, t % 2:t % 2 + 1], st[0:n, 1, t % 2:t % 2 + 1]).then_inc(inverted, 1)
                if t:
                    copy_out(t - 1)
            copy_out(NT - 1)


FFB = 32
SUP = 2
NSUP = FFB // SUP


def super_loop(eng, body):
    body(0)
    body(1)
    with eng.Fori(1, NSUP // 2 - 1) as i:
        body(i * 2, 0)
        body(i * 2 + 1, 1)
    body(NSUP - 2)
    body(NSUP - 1)


def mlp_half(nc, outer, tag, c0, groups, tiles, h2T, x2, w_up, w_dn, fg, y_out):
    W = sum(n for _, n in groups)
    ng, nt = len(groups), len(tiles)
    NU, ND = ng, (4 if 2 * nt % 4 == 0 else 3)
    with ExitStack() as ctx:
        s = Scope(nc, ctx, outer)
        n_ = lambda x: f"{tag}_{x}"
        hh = s.sb(n_("hh"), [P, KC, W], F32R)
        hl = s.sb(n_("hl"), [P, KC, W], F32R)
        y = s.sb(n_("y"), [P, nt, D])
        uh = s.sb(n_("uh"), [P, 2, SUP, W], F32R)
        ul = s.sb(n_("ul"), [P, 2, SUP, W], F32R)
        wur = s.sb(n_("wur"), [P, 2, KC, P])
        wuh = s.sb(n_("wuh"), [P, 2, KC, P], F32R)
        wul = s.sb(n_("wul"), [P, 2, KC, P], F32R)
        wdr = s.sb(n_("wdr"), [P, 2, D])
        wdh = s.sb(n_("wdh"), [P, 2, D], F32R)
        wdl = s.sb(n_("wdl"), [P, 2, D], F32R)
        r = s.sb(n_("r"), [P, 2, 512])
        sq = s.sb(n_("sq"), [P, 2, 512])
        fgb = s.sb(n_("fg"), [P, D])
        eps = s.sb(n_("eps"), [P, 1])
        st = s.sb(n_("stat"), [P, 3, nt])
        ub = [s.ps(n_(f"ub{i}"), [P, 512]) for i in range(NU)]
        db = [s.ps(n_(f"db{i}"), [P, 512]) for i in range(ND)]
        h_in = [s.sem(n_(f"h_in{i}")) for i in range(2)]
        y_in = s.sem(n_("y_in"))
        fg_in = s.sem(n_("fg_in"))
        eps_set = s.sem(n_("eps_set"))
        wu_in = [s.sem(n_(f"wu_in{i}")) for i in range(2)]
        wd_in = [s.sem(n_(f"wd_in{i}")) for i in range(2)]
        h_high = s.sem(n_("h_high"))
        h_low = s.sem(n_("h_low"))
        wu_high = s.sem(n_("wu_high"))
        wu_low = s.sem(n_("wu_low"))
        wd_high = s.sem(n_("wd_high"))
        wd_low = s.sem(n_("wd_low"))
        up_done = s.sem(n_("up_done"))
        relued = s.sem(n_("relued"))
        u_high = s.sem(n_("u_high"))
        u_sq = s.sem(n_("u_sq"))
        u_low = s.sem(n_("u_low"))
        down_done = s.sem(n_("down_done"))
        y_added = s.sem(n_("y_added"))
        stat_step = s.sem(n_("stat_step"))
        norm_step = s.sem(n_("norm_step"))
        out_st = s.sem(n_("out_st"))
        block = ctx.enter_context(nc.Block())
        raw = lambda k: y[:, :, :].rearrange("p a d -> p (a d)")[:, k * W:(k + 1) * W]

        @block.sync
        def _(sp):
            sp.dma_start(wur[:, 0], w_up[0]).then_inc(wu_in[0], 16)
            for k in range(KC):
                sp.dma_start(raw(k), h2T[k, :, c0:c0 + W]).then_inc(h_in[k // 4], 16)
            sp.dma_start(wur[:, 1], w_up[1]).then_inc(wu_in[1], 16)
            for j in range(2):
                sp.dma_start(wdr[:, j], w_dn[j]).then_inc(wd_in[j], 16)
            sp.wait_ge(h_low, KC)
            for a, (t0, n) in enumerate(tiles):
                sp.dma_start(y[0:n, a, :], x2[c0 + t0:c0 + t0 + n, :]).then_inc(y_in, 16)
            sp.dma_start(fgb[:, :], fg).then_inc(fg_in, 16)
            with sp.Fori(0, FFB // 2 - 1) as i:
                for j in range(2):
                    sp.wait_ge(wu_low, 2 * i + j + 1)
                    sp.dma_start(wur[:, j], w_up[2 * i + j + 2]).then_inc(wu_in[j], 16)
                for j in range(2):
                    sp.wait_ge(wd_low, 2 * i + j + 1)
                    sp.dma_start(wdr[:, j], w_dn[2 * i + j + 2]).then_inc(wd_in[j], 16)
            for a, (t0, n) in enumerate(tiles):
                sp.wait_ge(norm_step, 2 * a + 2)
                sp.dma_start(y_out[c0 + t0:c0 + t0 + n, :], y[0:n, a, :]).then_inc(out_st, 16)
            sp.wait_ge(out_st, 16 * nt)

        def passes(pe, out, wh, wl, mh, ml, first, last):
            pe.matmul(out, wh, mh, start=first, stop=False)
            pe.matmul(out, wh, ml, start=False, stop=False)
            return pe.matmul(out, wl, mh, start=False, stop=last)

        @block.tensor
        def _(pe):
            def up(sup, par, first):
                for j in range(SUP):
                    pe.wait_ge(wu_low, sup * SUP + j + 1)
                    for g, (g0, n) in enumerate(groups):
                        if not (first and j == 0):
                            pe.wait_ge(relued, (sup * SUP + j - 1) * ng + g + 1)
                        for k in range(KC):
                            if first and j == 0 and g == 0:
                                pe.wait_ge(h_low, k + 1)
                            mm = passes(pe, ub[g][:, 0:n], wuh[:, j, k, :], wul[:, j, k, :],
                                        hh[:, k, g0:g0 + n], hl[:, k, g0:g0 + n], k == 0, k == KC - 1)
                        mm.then_inc(up_done, 1)

            def down(sup, par, first):
                pe.wait_ge(u_low, (sup + 1) * SUP * ng)
                pe.wait_ge(wd_low, (sup + 1) * SUP)
                for a, (t0, n) in enumerate(tiles):
                    for h in range(2):
                        b = 2 * a + h
                        if not (first and b < ND):
                            pe.wait_ge(y_added, sup * 2 * nt + b - ND + 1)
                        for j in range(SUP):
                            mm = passes(pe, db[b % ND][0:n, :], uh[:, par, j, t0:t0 + n], ul[:, par, j, t0:t0 + n],
                                        wdh[:, j, h * 512:(h + 1) * 512], wdl[:, j, h * 512:(h + 1) * 512],
                                        j == 0, j == SUP - 1)
                        mm.then_inc(down_done, 1)

            def body(sup, par=None):
                first = par is None and sup == 0
                par = sup % 2 if par is None else par
                up(sup, par, first)
                if not first:
                    down(sup - 1, 1 - par, isinstance(sup, int) and sup == 1)

            super_loop(pe, body)
            down(NSUP - 1, (NSUP - 1) % 2, False)

        @block.scalar
        def _(act):
            def high_h(k):
                act.wait_ge(h_in[k // 4], 64)
                act.activation(hh[:, k, :], raw(k), ACT.Copy).then_inc(h_high, 1)

            def high_up(pair, j, n_before, first=False):
                act.wait_ge(wu_in[j], (pair + 1) * 16)
                if not first:
                    act.wait_ge(up_done, n_before)
                act.activation(wuh[:, j], wur[:, j], ACT.Copy).then_inc(wu_high, 1)

            def high_u(sup, j, par, first):
                for g, (g0, n) in enumerate(groups):
                    q = (j * ng + g) % 2
                    done = (sup * SUP + j) * ng + g
                    act.wait_ge(up_done, done + 1)
                    if not (first and j * ng + g < 2):
                        act.wait_ge(u_sq, done - 1)
                    act.activation(r[:, q, 0:n], ub[g][:, 0:n], ACT.Relu).then_inc(relued, 1)
                    act.wait_ge(relued, done + 1)
                    act.activation(uh[:, par, j, g0:g0 + n], r[:, q, 0:n], ACT.Square).then_inc(u_high, 1)

            def body(sup, par=None):
                first = par is None and sup == 0
                last = par is None and sup == NSUP - 1
                par = sup % 2 if par is None else par
                high_up(sup, 1, sup * SUP * ng, first)
                if not (isinstance(sup, int) and sup < 2):
                    act.wait_ge(down_done, (sup - 1) * 2 * nt)
                high_u(sup, 0, par, first)
                if not last:
                    high_up(sup + 1, 0, (sup * SUP + 1) * ng)
                high_u(sup, 1, par, False)
                if not first:
                    act.wait_ge(down_done, sup * 2 * nt)
                for j in range(SUP):
                    act.wait_ge(wd_in[j], (sup + 1) * 16)
                    act.activation(wdh[:, j], wdr[:, j], ACT.Copy).then_inc(wd_high, 1)

            high_up(0, 0, 0, True)
            for k in range(KC):
                high_h(k)
            super_loop(act, body)
            act.wait_ge(eps_set, 1)
            for a, (t0, n) in enumerate(tiles):
                act.wait_ge(y_added, (NSUP - 1) * 2 * nt + 2 * a + 2)
                if a:
                    act.wait_ge(stat_step, 2 * a)
                for_junk = uh[0:n, 0, :, :].rearrange("p a b -> p (a b)")[:, 0:D]
                act.activation(for_junk, y[0:n, a, :], ACT.Square, accum_out=st[0:n, 0, a:a + 1]).then_inc(stat_step, 1)
                act.wait_ge(stat_step, 2 * a + 1)
                act.activation(st[0:n, 1, a:a + 1], st[0:n, 0, a:a + 1], ACT.Sqrt,
                               bias=eps[0:n, 0:1], scale=1.0 / D).then_inc(stat_step, 1)

        @block.vector
        def _(dve):
            dve.memset(eps[:, :], EPS).then_inc(eps_set, 1)
            def low_h(k):
                dve.wait_ge(h_high, k + 1)
                dve.tensor_tensor(hl[:, k, :], raw(k), hh[:, k, :].bitcast(F32), ALU.subtract).then_inc(h_low, 1)

            def low_up(blk, j):
                dve.wait_ge(wu_high, blk + 1)
                dve.tensor_tensor(wul[:, j], wur[:, j], wuh[:, j].bitcast(F32), ALU.subtract).then_inc(wu_low, 1)

            def low_u(sup, j, par, first):
                for g, (g0, n) in enumerate(groups):
                    q = (j * ng + g) % 2
                    done = (sup * SUP + j) * ng + g
                    dve.wait_ge(relued, done + 1)
                    if not (first and j * ng + g < 2):
                        dve.wait_ge(u_low, done - 1)
                    dve.tensor_tensor(sq[:, q, 0:n], r[:, q, 0:n], r[:, q, 0:n], ALU.mult).then_inc(u_sq, 1)
                    dve.wait_ge(u_sq, done + 1)
                    dve.wait_ge(u_high, done + 1)
                    dve.tensor_tensor(ul[:, par, j, g0:g0 + n], sq[:, q, 0:n], uh[:, par, j, g0:g0 + n].bitcast(F32),
                                      ALU.subtract).then_inc(u_low, 1)

            def normalise(a):
                n = tiles[a][1]
                dve.wait_ge(stat_step, 2 * a + 2)
                dve.reciprocal(st[0:n, 2, a:a + 1], st[0:n, 1, a:a + 1]).then_inc(norm_step, 1)
                dve.wait_ge(norm_step, 2 * a + 1)
                ys = y[0:n, a, :]
                dve.scalar_tensor_tensor(out=ys, in0=ys, scalar=st[0:n, 2, a:a + 1], in1=fgb[0:n, :],
                                         op0=ALU.mult, op1=ALU.mult).then_inc(norm_step, 1)

            def add_down(sup, first, last=False):
                if first:
                    dve.wait_ge(y_in, 16 * nt)
                for a, (t0, n) in enumerate(tiles):
                    for h in range(2):
                        b = 2 * a + h
                        dve.wait_ge(down_done, sup * 2 * nt + b + 1)
                        ys = y[0:n, a, h * 512:(h + 1) * 512]
                        if not first:
                            dve.wait_ge(y_added, (sup - 1) * 2 * nt + b + 1)
                        dve.tensor_tensor(ys, ys, db[b % ND][0:n, :], ALU.add).then_inc(y_added, 1)
                    if last and a >= 2:
                        normalise(a - 2)

            def body(sup, par=None):
                first = par is None and sup == 0
                last = par is None and sup == NSUP - 1
                par = sup % 2 if par is None else par
                low_up(sup * SUP + 1, 1)
                low_u(sup, 0, par, first)
                if not last:
                    low_up(sup * SUP + 2, 0)
                low_u(sup, 1, par, False)
                if not first:
                    add_down(sup - 1, isinstance(sup, int) and sup == 1)
                for j in range(SUP):
                    dve.wait_ge(wd_high, sup * SUP + j + 1)
                    dve.tensor_tensor(wdl[:, j], wdr[:, j], wdh[:, j].bitcast(F32), ALU.subtract).then_inc(wd_low, 1)

            low_up(0, 0)
            for k in range(KC):
                low_h(k)
            dve.wait_ge(fg_in, 16)
            super_loop(dve, body)
            add_down(NSUP - 1, False, last=True)
            normalise(nt - 2)
            normalise(nt - 1)


def decoder_trunk(nc, A):
    with ExitStack() as outer:
        mixT = nc.dram_tensor("mixT", (KC, P, T), F32).ap()
        x2 = nc.dram_tensor("x2", (T, D), F32).ap()
        h2T = nc.dram_tensor("h2T", (KC, P, T), F32).ap()
        cst = {k[4:]: v for k, v in A.items() if k.startswith("cst_")}
        wts = {"w2": A["lora"], "g2": A["c_g2"]}
        project(nc, outer, A["xT"], A["g1"], A["cst_ones"], A["w_fm"], A["w_v"], A["projT"], A["vtok"])
        prompt_attention(nc, outer, A["projT"], A["vtok"], A["cst_strip_a"], A["cst_strip_b"], A["sinks"],
                         A["cst_ident"], mixT)
        sample_attention(nc, outer, A["projT"], A["vtok"], A["kbT"], A["vb"], A["kaT"], A["va"], A["cst_mask_b"],
                         A["cst_mask_a"], A["sink_a"], A["cst_ident"], mixT)
        zc, mixC = A["projT"][ZC0:FMB], mixT[PAIRS:KC]
        rwkv(nc, outer, "cp", False, zc, None, None, cst, wts, mixC, 0, A["state_p"])
        rwkv(nc, outer, "cs", True, zc, A["shift0"], A["state0"], cst, wts, mixC, SEQ, A["state_s"])
        out_project(nc, outer, mixT, A["x"], A["w_o"], A["g2"], A["cst_ident"], x2, h2T)
        tiles = [(P * i, P) for i in range(8)]
        mlp_half(nc, outer, "ma", 0, [(0, 512), (512, 512)], tiles, h2T, x2, A["w_up"], A["w_dn"], A["fg"], A["y"])
        mlp_half(nc, outer, "mb", SEQ // 2, [(0, 352), (352, 352), (704, 352)], tiles + [(SEQ // 2, NS)], h2T, x2,
                 A["w_up"], A["w_dn"], A["fg"], A["y"])


def kernel(**inputs):
    import concourse.bacc as bacc
    from concourse.bass_utils import run_bass_kernel_spmd as run

    I = {k: np.asarray(v) for k, v in inputs.items()}
    nc = bacc.Bacc("TRN2", target_bir_lowering=False, num_devices=1)
    arrays, A = {}, {}

    def give(name, a):
        a = np.ascontiguousarray(a)
        arrays[name] = a
        A[name] = nc.dram_tensor(name, a.shape, mybir.dt.from_np(a.dtype), kind="ExternalInput").ap()

    cols = lambda a, n: a.reshape(n, P).T
    x = np.concatenate([I["x_prompt"][0], I["x_sample"].reshape(NS, D)], 0)
    give("x", x)
    give("xT", x.T.reshape(KC, P, T).transpose(1, 0, 2))
    give("g1", cols(I["norm1_g"][0], KC))
    give("g2", cols(I["norm2_g"][0], KC))
    give("fg", np.broadcast_to(I["final_norm_g"][None], (P, D)))
    w_in = I["w_in"][0].reshape(KC, P, 24, P)
    v_blocks = [3, 10, 11, 12]
    give("w_fm", w_in[:, :, [b for b in range(24) if b not in v_blocks]].transpose(2, 1, 0, 3))
    give("w_v", w_in[:, :, v_blocks].transpose(1, 0, 2, 3).reshape(P, KC, NV))
    give("w_o", I["w_out"][0].reshape(KC, P, D).transpose(1, 0, 2))
    give("w_up", I["mlp_up"][0].reshape(KC, P, FFB, P).transpose(2, 1, 0, 3))
    give("w_dn", I["mlp_down"][0].reshape(FFB, P, D))
    give("sinks", np.broadcast_to(I["a_sink"], (P, 4)))
    give("sink_a", np.broadcast_to(np.repeat(I["a_sink"][0], NQ)[:, None, None], (4 * NQ, NB, 1)))
    give("lora", np.concatenate([I["c_w2"][0], I["c_a2"][0]], 0))
    give("c_g2", I["c_g2"][0])
    give("cst_par", np.concatenate([cols(I["c_mu"][0], NZ)] + [cols(I[k][0].reshape(-1), NP3) for k in
                                   ("c_w0", "c_a0", "c_k_k", "c_k_a", "c_ln_w", "c_ln_b", "c_r_k")], 1))
    order = sample_order()
    kb = I["cache_b_k"][0][:, order[:NKC]].reshape(NB, NKC, B_PAIRS, P)
    give("kbT", kb.transpose(0, 3, 2, 1))
    give("vb", I["cache_b_v"][0][:, order[:NKC]].reshape(NB, NTB, P, 384).transpose(0, 2, 1, 3))
    give("kaT", I["cache_a_k"][0].reshape(NB, A_WIN, P).transpose(2, 0, 1))
    give("va", I["cache_a_v"][0].reshape(NB, A_WIN, P).transpose(1, 0, 2))
    give("shift0", I["state_c_shift"][0].reshape(NB, NZ, P).transpose(2, 1, 0)[..., None])
    give("state0", I["state_c_wkv"][0].reshape(NB, NP3, 2, HD, HD).transpose(2, 4, 1, 0, 3).reshape(P, NP3, NB, HD))
    strip_a, strip_b = strips()
    mask_b, mask_a = sample_masks()
    for name, a in dict(rwkv_constants(), ones=np.ones((P, P), np.float32), ident=np.eye(P, dtype=np.float32),
                        strip_a=strip_a, strip_b=strip_b, mask_b=mask_b, mask_a=mask_a).items():
        give("cst_" + name, a)
    for name, shape in (("y", (T, D)), ("projT", (FMB, P, T)), ("vtok", (T, NV)), ("state_p", (P, NP3, 1, HD)),
                        ("state_s", (P, NP3, NB, HD))):
        A[name] = nc.dram_tensor("out_" + name, shape, F32, kind="ExternalOutput").ap()
    decoder_trunk(nc, A)
    r = run(nc, [arrays], core_ids=[0]).results[0]
    y, projT, vtok = r["out_y"], r["out_projT"], r["out_vtok"]

    def rows(blocks, lo, hi, *shape):
        return np.ascontiguousarray(projT[blocks][:, :, lo:hi].transpose(2, 0, 1)).reshape(*shape)

    def values(c0, c1, lo, hi, *shape):
        return np.ascontiguousarray(vtok[lo:hi, c0:c1]).reshape(*shape)

    def state(a, n):
        return np.ascontiguousarray(a.reshape(2, HD, NP3, n, HD).transpose(3, 2, 0, 4, 1)).reshape(1, n, 6, HD, HD)

    ka, kb, zc = slice(2, 3), slice(6, 9), slice(ZC0, FMB)
    return (y[:SEQ].reshape(1, SEQ, D), y[SEQ:].reshape(NB, NQ, D),
            rows(ka, SEQ - P, SEQ, 1, 1, P, 2, HD), values(0, P, SEQ - P, SEQ, 1, 1, P, 2, HD),
            rows(kb, 0, SEQ, 1, 1, SEQ, 6, HD), values(P, NV, 0, SEQ, 1, 1, SEQ, 6, HD),
            state(r["out_state_p"], 1), rows(zc, SEQ - 1, SEQ, 1, 1, NZ * P),
            rows(ka, SEQ, T, 1, NB, NQ, 2, HD), values(0, P, SEQ, T, 1, NB, NQ, 2, HD),
            rows(kb, SEQ, T, 1, NB, NQ, 6, HD), values(P, NV, SEQ, T, 1, NB, NQ, 6, HD),
            state(r["out_state_s"], NB),
            np.ascontiguousarray(rows(zc, SEQ, T, NB, NQ, NZ * P)[:, NQ - 1]).reshape(1, NB, NZ * P))
```
